# Optimizing a Trainium2 kernel written in Bass

```python
import math
import numpy as np
import jax
import jax.numpy as jnp
from jax import lax

D_MODEL = 1024
BATCH = 1
SEQ = 512
DEPTH = 2

NORM_EPS = 1e-6
D_FF = 2816
FFN_RES_SCALE = 0.5

REL_BUCKETS = 32
REL_MAX_DIST = 128

GDN_HEADS = 4
GDN_DK = 128
GDN_DV = 128
GDN_CONV = 4
GDN_CHUNK = 64

NSA_HEADS = 8
NSA_GROUPS = 2
NSA_DK = 96
NSA_DV = 64
CMP_LEN = 32
CMP_STRIDE = 16
CMP_HIDDEN = 256
SEL_LEN = 64
SEL_TOPK = 16
WINDOW = 512
Q_BLOCK = 128

GLA_HEADS = 4
GLA_DK = 64
GLA_DV = 128
GLA_RANK = 16
GLA_TAU = 16
GLA_CHUNK = 16

N_BRANCH = 3
MASK_VALUE = -1e30

IN_COLUMNS = (
    ('gdn_q', GDN_HEADS * GDN_DK),
    ('gdn_k', GDN_HEADS * GDN_DK),
    ('gdn_v', GDN_HEADS * GDN_DV),
    ('gdn_z', GDN_HEADS * GDN_DV),
    ('gdn_b', GDN_HEADS),
    ('gdn_a', GDN_HEADS),
    ('nsa_q', NSA_HEADS * NSA_DK),
    ('nsa_kv_cmp', NSA_GROUPS * (NSA_DK + NSA_DV)),
    ('nsa_kv_sel', NSA_GROUPS * (NSA_DK + NSA_DV)),
    ('nsa_kv_win', NSA_GROUPS * (NSA_DK + NSA_DV)),
    ('nsa_gate', 3 * NSA_HEADS),
    ('gla_q', GLA_HEADS * GLA_DK),
    ('gla_k', GLA_HEADS * GLA_DK),
    ('gla_v', GLA_HEADS * GLA_DV),
    ('gla_r', GLA_HEADS * GLA_DV),
    ('gla_a', GLA_RANK),
    ('merge_gate', N_BRANCH * D_MODEL),
)
D_IN = sum(width for _, width in IN_COLUMNS)

kernel_name = "hybrid_gdn_nsa_gla_macaron"

def rms_norm(x, w, eps=NORM_EPS):
    xf = x.astype(jnp.float32)
    y = xf * lax.rsqrt(jnp.mean(xf * xf, axis=-1, keepdims=True) + eps)
    return (y * w.astype(jnp.float32)).astype(x.dtype)

def l2_normalize(t, eps=1e-6):
    t = t.astype(jnp.float32)
    return t * lax.rsqrt(jnp.sum(t * t, axis=-1, keepdims=True) + eps)

def swiglu(h, w_gate_up, w_down):
    g, u = jnp.split(h @ w_gate_up, 2, axis=-1)
    return (jax.nn.silu(g) * u) @ w_down

def macaron_ffn(x, norm_pre, w_gate_up, w_down, norm_post):
    y = swiglu(rms_norm(x, norm_pre), w_gate_up, w_down)
    return x + FFN_RES_SCALE * rms_norm(y, norm_post)

def split_columns(p):
    out = {}
    off = 0
    for name, width in IN_COLUMNS:
        out[name] = p[..., off:off + width]
        off += width
    return out

def rel_bucket(dist):
    n = jnp.maximum(dist, 0)
    max_exact = REL_BUCKETS // 2
    nf = jnp.maximum(n, 1).astype(jnp.float32)
    large = max_exact + (jnp.log(nf / max_exact) / math.log(REL_MAX_DIST / max_exact)
                         * (REL_BUCKETS - max_exact)).astype(jnp.int32)
    large = jnp.minimum(large, REL_BUCKETS - 1)
    return jnp.where(n < max_exact, n, large)

def causal_depthwise_conv(x, w):
    k_width, ch = w.shape
    return lax.conv_general_dilated(
        x, w[:, None, :].astype(x.dtype), window_strides=(1,),
        padding=[(k_width - 1, 0)], dimension_numbers=('NWC', 'WIO', 'NWC'),
        feature_group_count=ch)

def gated_deltanet(q, k, v, z, b, a, conv_w, a_log, dt_bias, norm_w):
    B, S, _ = q.shape
    H, dk, dv, C = GDN_HEADS, GDN_DK, GDN_DV, GDN_CHUNK
    N = S // C
    f32 = jnp.float32
    qkv = jax.nn.silu(causal_depthwise_conv(jnp.concatenate([q, k, v], axis=-1), conv_w))
    q, k, v = jnp.split(qkv, [H * dk, 2 * H * dk], axis=-1)
    q = l2_normalize(q.reshape(B, S, H, dk)) * dk ** -0.5
    k = l2_normalize(k.reshape(B, S, H, dk))
    v = v.reshape(B, S, H, dv)
    beta = jax.nn.sigmoid(b.astype(f32))
    g = -jnp.exp(a_log.astype(f32)) * jax.nn.softplus(a.astype(f32) + dt_bias.astype(f32))

    def chunk(t):
        return t.reshape(B, N, C, H, -1).transpose(0, 3, 1, 2, 4).astype(f32)

    qc, kc, vc = chunk(q), chunk(k), chunk(v)
    gc = jnp.cumsum(chunk(g[..., None])[..., 0], axis=-1)
    bc = chunk(beta[..., None])[..., 0]
    lower = jnp.tril(jnp.ones((C, C), bool))
    decay = jnp.exp(jnp.where(lower, gc[..., :, None] - gc[..., None, :], -jnp.inf))
    eye = jnp.eye(C, dtype=f32)
    kb = kc * bc[..., None]
    lmat = jnp.einsum('bhnid,bhnjd->bhnij', kb, kc) * decay * (1.0 - eye)
    rhs = jnp.concatenate([vc * bc[..., None], kb * jnp.exp(gc)[..., None]], axis=-1)
    sol = lax.linalg.triangular_solve(lmat + eye, rhs, left_side=True, lower=True)
    u, w = sol[..., :dv], sol[..., dv:]
    attn = jnp.einsum('bhnid,bhnjd->bhnij', qc, kc) * decay
    q_dec = qc * jnp.exp(gc)[..., None]
    k_dec = kc * jnp.exp(gc[..., -1:] - gc)[..., None]
    c_dec = jnp.exp(gc[..., -1])

    def step(state, xs):
        attn_n, u_n, w_n, q_n, k_n, d_n = xs
        v_new = u_n - jnp.einsum('bhcd,bhde->bhce', w_n, state)
        o = jnp.einsum('bhcd,bhde->bhce', q_n, state) + jnp.einsum('bhij,bhje->bhie', attn_n, v_new)
        state = state * d_n[..., None, None] + jnp.einsum('bhcd,bhce->bhde', k_n, v_new)
        return state, o

    xs = tuple(jnp.moveaxis(t, 2, 0) for t in (attn, u, w, q_dec, k_dec, c_dec))
    _, o = lax.scan(step, jnp.zeros((B, H, dk, dv), f32), xs)
    o = jnp.moveaxis(o, 0, 2).transpose(0, 2, 3, 1, 4).reshape(B, S, H, dv)
    o = rms_norm(o, norm_w) * jax.nn.silu(z.reshape(B, S, H, dv).astype(f32))
    return o.reshape(B, S, H * dv)

def compress_blocks(t, pe, w1, w2):
    B, S, G, d = t.shape
    n_seg = S // CMP_STRIDE
    r = CMP_LEN // CMP_STRIDE
    n_cmp = n_seg - r + 1
    seg = t.reshape(B, n_seg, CMP_STRIDE, G, d)
    blocks = jnp.concatenate([seg[:, j:j + n_cmp] for j in range(r)], axis=2)
    blocks = blocks + pe[None, None, :, None, :]
    flat = blocks.transpose(0, 1, 3, 2, 4).reshape(B, n_cmp, G, CMP_LEN * d)
    return jax.nn.gelu(flat @ w1) @ w2

def native_sparse_attention(q, kv_cmp, kv_sel, kv_win, gate_logits, rel_bias,
                            pe_k, w1_k, w2_k, pe_v, w1_v, w2_v):
    B, S, _ = q.shape
    G, HPG = NSA_GROUPS, NSA_HEADS // NSA_GROUPS
    dk, dv = NSA_DK, NSA_DV
    f32 = jnp.float32
    n_q = S // Q_BLOCK
    n_cmp = (S - CMP_LEN) // CMP_STRIDE + 1
    n_sel = S // SEL_LEN
    k_top = min(SEL_TOPK, n_sel)
    scale = dk ** -0.5

    def split_kv(kv):
        kv = kv.reshape(B, S, G, dk + dv)
        return kv[..., :dk], kv[..., dk:]

    k_c, v_c = split_kv(kv_cmp)
    k_s, v_s = split_kv(kv_sel)
    k_w, v_w = split_kv(kv_win)
    k_cmp = compress_blocks(k_c, pe_k, w1_k, w2_k)
    v_cmp = compress_blocks(v_c, pe_v, w1_v, w2_v)
    k_blk = k_s.reshape(B, n_sel, SEL_LEN, G, dk).transpose(0, 3, 1, 2, 4)
    v_blk = v_s.reshape(B, n_sel, SEL_LEN, G, dv).transpose(0, 3, 1, 2, 4)
    pad = ((0, 0), (WINDOW, 0), (0, 0), (0, 0))
    k_wp, v_wp = jnp.pad(k_w, pad), jnp.pad(v_w, pad)

    cmp_end = jnp.arange(n_cmp) * CMP_STRIDE + CMP_LEN - 1
    c_start = np.arange(n_cmp) * CMP_STRIDE
    s_start = np.arange(n_sel) * SEL_LEN
    overlap = jnp.asarray(((c_start[:, None] < s_start[None, :] + SEL_LEN)
                           & (c_start[:, None] + CMP_LEN > s_start[None, :])).astype(np.float32))
    tbl = rel_bias.astype(f32)
    tbl_g = tbl.reshape(REL_BUCKETS, G, HPG).transpose(1, 0, 2)
    bi = jnp.arange(B)[:, None, None, None]
    gi = jnp.arange(G)[None, None, :, None]
    sel_ids = jnp.arange(n_sel)
    kw_off = jnp.arange(WINDOW + Q_BLOCK) - WINDOW

    def head_bias(dist):
        bias = tbl[rel_bucket(dist)]
        return bias.reshape(dist.shape[0], dist.shape[1], G, HPG).transpose(2, 3, 0, 1)

    def block(args):
        i, qb, gb = args
        q0 = i * Q_BLOCK
        t = q0 + jnp.arange(Q_BLOCK)
        dist_c = t[:, None] - cmp_end[None, :]
        valid_c = dist_c >= 0
        s_c = jnp.einsum('bghqd,bngd->bghqn', qb, k_cmp).astype(f32) * scale + head_bias(dist_c)
        p_c = jax.nn.softmax(jnp.where(valid_c, s_c, MASK_VALUE), axis=-1)
        p_c = p_c * jnp.any(valid_c, axis=-1)[:, None]
        o_c = jnp.einsum('bghqn,bngd->bqghd', p_c.astype(v_cmp.dtype), v_cmp)
        imp = jnp.einsum('bghqn,ns->bqgs', p_c, overlap)
        blk_t = (t // SEL_LEN)[:, None]
        forced = (sel_ids == 0) | (sel_ids == blk_t) | (sel_ids == blk_t - 1)
        future = sel_ids > blk_t
        imp = jnp.where(forced[:, None, :], jnp.inf, jnp.where(future[:, None, :], -jnp.inf, imp))
        _, sel = lax.top_k(imp, k_top)
        k_g = k_blk[bi, gi, sel].reshape(B, Q_BLOCK, G, k_top * SEL_LEN, dk)
        v_g = v_blk[bi, gi, sel].reshape(B, Q_BLOCK, G, k_top * SEL_LEN, dv)
        pos = (sel[..., None] * SEL_LEN + jnp.arange(SEL_LEN)).reshape(B, Q_BLOCK, G, k_top * SEL_LEN)
        dist_s = t[None, :, None, None] - pos
        bias_s = tbl_g[gi, rel_bucket(dist_s)].transpose(0, 2, 4, 1, 3)
        s_s = jnp.einsum('bghqd,bqgsd->bghqs', qb, k_g).astype(f32) * scale + bias_s
        valid_s = (dist_s >= 0).transpose(0, 2, 1, 3)[:, :, None]
        p_s = jax.nn.softmax(jnp.where(valid_s, s_s, MASK_VALUE), axis=-1)
        o_s = jnp.einsum('bghqs,bqgsd->bqghd', p_s.astype(v_g.dtype), v_g)
        k_wb = lax.dynamic_slice_in_dim(k_wp, q0, WINDOW + Q_BLOCK, axis=1)
        v_wb = lax.dynamic_slice_in_dim(v_wp, q0, WINDOW + Q_BLOCK, axis=1)
        kpos = q0 + kw_off
        dist_w = t[:, None] - kpos[None, :]
        valid_w = (dist_w >= 0) & (dist_w < WINDOW) & (kpos[None, :] >= 0)
        s_w = jnp.einsum('bghqd,bkgd->bghqk', qb, k_wb).astype(f32) * scale + head_bias(dist_w)
        p_w = jax.nn.softmax(jnp.where(valid_w, s_w, MASK_VALUE), axis=-1)
        o_w = jnp.einsum('bghqk,bkgd->bqghd', p_w.astype(v_wb.dtype), v_wb)
        gb = gb.reshape(B, Q_BLOCK, G, HPG, 3)
        o = gb[..., 0:1] * o_c + gb[..., 1:2] * o_s + gb[..., 2:3] * o_w
        return o.reshape(B, Q_BLOCK, NSA_HEADS * dv)

    qb = q.reshape(B, n_q, Q_BLOCK, G, HPG, dk).transpose(1, 0, 3, 4, 2, 5)
    gates = jax.nn.sigmoid(gate_logits.astype(f32)).reshape(B, S, NSA_HEADS, 3)
    gb = gates.reshape(B, n_q, Q_BLOCK, NSA_HEADS, 3).transpose(1, 0, 2, 3, 4)
    out = lax.map(block, (jnp.arange(n_q), qb, gb))
    return out.transpose(1, 0, 2, 3).reshape(B, S, NSA_HEADS * dv)

def gated_linear_attention(q, k, v, r, a_low, gate_w, gate_b, norm_w):
    B, S, _ = q.shape
    H, dk, dv, C = GLA_HEADS, GLA_DK, GLA_DV, GLA_CHUNK
    N = S // C
    f32 = jnp.float32
    log_a = jax.nn.log_sigmoid((a_low @ gate_w + gate_b).astype(f32)) / GLA_TAU

    def chunk(t, d):
        return t.reshape(B, N, C, H, d).transpose(0, 3, 1, 2, 4).astype(f32)

    qc = chunk(q, dk) * dk ** -0.5
    kc = chunk(k, dk)
    vc = chunk(v, dv)
    bc = jnp.cumsum(chunk(log_a, dk), axis=-2)
    lower = jnp.tril(jnp.ones((C, C), bool))[..., None]
    dec = jnp.exp(jnp.where(lower, bc[..., :, None, :] - bc[..., None, :, :], -jnp.inf))
    attn = jnp.einsum('bhnid,bhnjd,bhnijd->bhnij', qc, kc, dec)
    o_intra = jnp.einsum('bhnij,bhnje->bhnie', attn, vc)
    q_dec = qc * jnp.exp(bc)
    k_dec = kc * jnp.exp(bc[..., -1:, :] - bc)
    c_dec = jnp.exp(bc[..., -1, :])

    def step(state, xs):
        q_n, k_n, v_n, d_n = xs
        o = jnp.einsum('bhcd,bhde->bhce', q_n, state)
        state = state * d_n[..., None] + jnp.einsum('bhcd,bhce->bhde', k_n, v_n)
        return state, o

    xs = tuple(jnp.moveaxis(t, 2, 0) for t in (q_dec, k_dec, vc, c_dec))
    _, o_inter = lax.scan(step, jnp.zeros((B, H, dk, dv), f32), xs)
    o = jnp.moveaxis(o_inter, 0, 2) + o_intra
    o = o.transpose(0, 2, 3, 1, 4).reshape(B, S, H, dv)
    o = rms_norm(o, norm_w) * jax.nn.silu(r.reshape(B, S, H, dv).astype(f32))
    return o.reshape(B, S, H * dv)

def token_mixing(h, rel_bias, w_in, gdn_conv_w, gdn_a_log, gdn_dt_bias, gdn_norm_w,
                 nsa_pe_k, nsa_cmp_k_w1, nsa_cmp_k_w2, nsa_pe_v, nsa_cmp_v_w1, nsa_cmp_v_w2,
                 gla_gate_w, gla_gate_b, gla_norm_w,
                 w_branch_gdn, w_branch_nsa, w_branch_gla, w_out):
    B, S, D = h.shape
    p = split_columns(h @ w_in)
    o_a = gated_deltanet(p['gdn_q'], p['gdn_k'], p['gdn_v'], p['gdn_z'], p['gdn_b'], p['gdn_a'],
                         gdn_conv_w, gdn_a_log, gdn_dt_bias, gdn_norm_w).astype(h.dtype)
    o_b = native_sparse_attention(p['nsa_q'], p['nsa_kv_cmp'], p['nsa_kv_sel'], p['nsa_kv_win'],
                                  p['nsa_gate'], rel_bias, nsa_pe_k, nsa_cmp_k_w1, nsa_cmp_k_w2,
                                  nsa_pe_v, nsa_cmp_v_w1, nsa_cmp_v_w2).astype(h.dtype)
    o_c = gated_linear_attention(p['gla_q'], p['gla_k'], p['gla_v'], p['gla_r'], p['gla_a'],
                                 gla_gate_w, gla_gate_b, gla_norm_w).astype(h.dtype)
    gates = jax.nn.sigmoid(p['merge_gate'].astype(jnp.float32)).astype(h.dtype).reshape(B, S, N_BRANCH, D)
    merged = (gates[:, :, 0] * (o_a @ w_branch_gdn)
              + gates[:, :, 1] * (o_b @ w_branch_nsa)
              + gates[:, :, 2] * (o_c @ w_branch_gla))
    return merged @ w_out

def setup_inputs(seed: int = 0) -> dict:
    key = jax.random.key(seed)
    keys = iter(jax.random.split(key, 40))
    f32 = jnp.float32
    L = DEPTH

    def dense(shape, fan_in):
        return jax.random.normal(next(keys), shape, f32) * fan_in ** -0.5

    def gain(shape):
        return 1.0 + 0.05 * jax.random.normal(next(keys), shape, f32)

    x = jax.random.normal(next(keys), (BATCH, SEQ, D_MODEL), f32)
    rel_bias = 0.2 * jax.random.normal(next(keys), (REL_BUCKETS, NSA_HEADS), f32)
    gdn_a_log = jnp.log(jax.random.uniform(next(keys), (L, GDN_HEADS), f32, minval=1.0, maxval=16.0))
    dt = jnp.exp(jax.random.uniform(next(keys), (L, GDN_HEADS), f32,
                                    minval=math.log(1e-3), maxval=math.log(1e-1)))
    gdn_dt_bias = dt + jnp.log(-jnp.expm1(-dt))
    return {
        "x": x,
        "rel_bias": rel_bias,
        "ffn1_norm_pre": gain((L, D_MODEL)),
        "ffn1_w_gate_up": dense((L, D_MODEL, 2 * D_FF), D_MODEL),
        "ffn1_w_down": dense((L, D_FF, D_MODEL), D_FF),
        "ffn1_norm_post": gain((L, D_MODEL)),
        "mix_norm_pre": gain((L, D_MODEL)),
        "w_in": dense((L, D_MODEL, D_IN), D_MODEL),
        "gdn_conv_w": dense((L, GDN_CONV, GDN_HEADS * (2 * GDN_DK + GDN_DV)), GDN_CONV),
        "gdn_a_log": gdn_a_log,
        "gdn_dt_bias": gdn_dt_bias,
        "gdn_norm_w": gain((L, GDN_DV)),
        "nsa_pe_k": dense((L, CMP_LEN, NSA_DK), NSA_DK),
        "nsa_cmp_k_w1": dense((L, CMP_LEN * NSA_DK, CMP_HIDDEN), CMP_LEN * NSA_DK),
        "nsa_cmp_k_w2": dense((L, CMP_HIDDEN, NSA_DK), CMP_HIDDEN),
        "nsa_pe_v": dense((L, CMP_LEN, NSA_DV), NSA_DV),
        "nsa_cmp_v_w1": dense((L, CMP_LEN * NSA_DV, CMP_HIDDEN), CMP_LEN * NSA_DV),
        "nsa_cmp_v_w2": dense((L, CMP_HIDDEN, NSA_DV), CMP_HIDDEN),
        "gla_gate_w": dense((L, GLA_RANK, GLA_HEADS * GLA_DK), GLA_RANK),
        "gla_gate_b": 0.1 * jax.random.normal(next(keys), (L, GLA_HEADS * GLA_DK), f32),
        "gla_norm_w": gain((L, GLA_DV)),
        "w_branch_gdn": dense((L, GDN_HEADS * GDN_DV, D_MODEL), GDN_HEADS * GDN_DV),
        "w_branch_nsa": dense((L, NSA_HEADS * NSA_DV, D_MODEL), NSA_HEADS * NSA_DV),
        "w_branch_gla": dense((L, GLA_HEADS * GLA_DV, D_MODEL), GLA_HEADS * GLA_DV),
        "w_out": dense((L, D_MODEL, D_MODEL), D_MODEL),
        "mix_norm_post": gain((L, D_MODEL)),
        "ffn2_norm_pre": gain((L, D_MODEL)),
        "ffn2_w_gate_up": dense((L, D_MODEL, 2 * D_FF), D_MODEL),
        "ffn2_w_down": dense((L, D_FF, D_MODEL), D_FF),
        "ffn2_norm_post": gain((L, D_MODEL)),
    }

def reference(x, rel_bias,
              ffn1_norm_pre, ffn1_w_gate_up, ffn1_w_down, ffn1_norm_post,
              mix_norm_pre, w_in, gdn_conv_w, gdn_a_log, gdn_dt_bias, gdn_norm_w,
              nsa_pe_k, nsa_cmp_k_w1, nsa_cmp_k_w2, nsa_pe_v, nsa_cmp_v_w1, nsa_cmp_v_w2,
              gla_gate_w, gla_gate_b, gla_norm_w,
              w_branch_gdn, w_branch_nsa, w_branch_gla, w_out, mix_norm_post,
              ffn2_norm_pre, ffn2_w_gate_up, ffn2_w_down, ffn2_norm_post):
    for l in range(DEPTH):
        x = macaron_ffn(x, ffn1_norm_pre[l], ffn1_w_gate_up[l], ffn1_w_down[l], ffn1_norm_post[l])
        y = token_mixing(rms_norm(x, mix_norm_pre[l]), rel_bias, w_in[l],
                         gdn_conv_w[l], gdn_a_log[l], gdn_dt_bias[l], gdn_norm_w[l],
                         nsa_pe_k[l], nsa_cmp_k_w1[l], nsa_cmp_k_w2[l],
                         nsa_pe_v[l], nsa_cmp_v_w1[l], nsa_cmp_v_w2[l],
                         gla_gate_w[l], gla_gate_b[l], gla_norm_w[l],
                         w_branch_gdn[l], w_branch_nsa[l], w_branch_gla[l], w_out[l])
        x = x + rms_norm(y, mix_norm_post[l])
        x = macaron_ffn(x, ffn2_norm_pre[l], ffn2_w_gate_up[l], ffn2_w_down[l], ffn2_norm_post[l])
    return x


_drawn_inputs = setup_inputs


def setup_inputs(seed=0):
    import zlib

    import numpy as np

    out = dict(_drawn_inputs(seed))
    spreads = {}
    factors = {'nsa_pe_k': 8.0}
    for name, (base, spread) in spreads.items():
        noise = np.random.default_rng([zlib.crc32(name.encode()), seed]).standard_normal(out[name].shape)
        drawn = base * np.exp(spread * noise) if base else spread * noise
        out[name] = jnp.asarray(drawn.astype(out[name].dtype))
    for name, factor in factors.items():
        out[name] = (out[name] * factor).astype(out[name].dtype)
    return out
```

```python
from contextlib import ExitStack

import concourse.bass as bass
from concourse import mybir

F32 = mybir.dt.float32
F32R = mybir.dt.float32r
ALU = mybir.AluOpType
ACT = mybir.ActivationFunctionType
AX = mybir.AxisListType.X

P = 128
D = 1024
S = 512
DEPTH = 2
FF = 2816
NT = S // P
KD = D // P
KF = FF // P
EPS = 1e-6
MASKED = -1e30

GDN_H = 4
GDN_C = 64
NSA_H = 8
NSA_G = 2
HPG = NSA_H // NSA_G
NDK = 96
NDV = 64
NCMP = 31
CMP_LEN = 32
CMP_STRIDE = 16
CMP_HID = 256
GLA_H = 4
GLA_C = 16
GLA_TAU = 16.0
GLA_GUARD = 40.0
BUCKETS = 32
NSA_LATE = NSA_H + 2 * NSA_G
NSA_CHUNKS = NSA_H + 6 * NSA_G
GLA_CHUNKS = 12
RLEN = 1024
WLEN = RLEN - P

PARAM_COLS = {}
_at = 0
for _name, _n in (("ffn1_pre", KD), ("mix_pre", KD), ("ffn2_pre", KD), ("conv", 48), ("gdn_norm", 1),
                  ("gla_norm", 1), ("gla_b", 2), ("pe_k", CMP_LEN), ("pe_v", CMP_LEN), ("gla_w", 256),
                  ("a_log", 4), ("dt_bias", 4), ("w2k", 2 * NDK), ("w2v", 2 * NDV)):
    PARAM_COLS[_name] = (_at, _at + _n)
    _at += _n
PARAM_N = _at

CONST_COLS = {}
_at = 0
for _name, _n in (("ident", P), ("ones", P), ("anti", P), ("tri64", P), ("blk64", P), ("lvl", 6 * P),
                  ("tri16", P), ("parity", 2), ("cmp_valid", 1), ("eps", 1), ("gdn_eps", 1), ("one", 1),
                  ("lnq", 1)):
    CONST_COLS[_name] = (_at, _at + _n)
    _at += _n
CONST_N = _at


def sbuf(nc, name, shape, dtype):
    return nc.sbuf_tensor(f"{name}_{nc.next_id()}", shape, dtype)


def phase(nc, names):
    return {n: nc.alloc_semaphore(name=f"{n}_{nc.next_id()}") for n in names}


def retire(nc, sems):
    nums = sorted(s.num for s in sems.values())
    first = nums[0]
    for a, b in zip(nums, nums[1:] + [None]):
        if b != a + 1:
            nc.sync.sem_clear(range(first, a + 1))
            first = b
    nc.all_engine_barrier()
    for s in sems.values():
        nc.release_semaphore(s)


def load(nc, out, in_):
    s = phase(nc, ["load"])
    with nc.Block() as block:
        @block.sync
        def _(e):
            e.dma_start(out, in_).then_inc(s["load"], 16)
            e.wait_ge(s["load"], 16)
    retire(nc, s)


def zero(nc, ap):
    with nc.Block() as block:
        @block.vector
        def _(e):
            e.memset(ap, 0.0)


def mm3(e, out, w_hi, w_lo, m_hi, m_lo, start, stop):
    e.matmul(out, w_hi, m_hi, start=start, stop=False, skip_group_check=True)
    e.matmul(out, w_lo, m_hi, start=False, stop=False, skip_group_check=True)
    return e.matmul(out, w_hi, m_lo, start=False, stop=stop, skip_group_check=True)


HALF = 4


class Background:

    SEMS = ["b_raw0", "b_raw1", "b_hi", "b_lo", "b_acc", "b_out", "b_pr", "b_add", "b_st0", "b_st1"]

    def __init__(self, C, s, jobs, sums, bank):
        self.C, self.s, self.jobs, self.sums, self.bank = C, s, jobs, sums, bank
        self.raw, self.hi_, self.lo_, self.stage, self.sg, self.pr = C["bg"]
        self.merged = C["merged"]
        self.sum_of, n = [], 0
        for job in jobs:
            self.sum_of.append(n)
            n += job[6]
        self.branches = [n for n, x in enumerate(sums) if x[0] == "branch"]
        self.stores = [n for n, x in enumerate(sums) if x[0] == "store"]

    def load(self, e, j):
        src, w = self.jobs[j][:2]
        if j >= 2:
            e.wait_ge(self.s["b_lo"], j - 1)
        e.dma_start(self.raw[:, j % 2, 0:HALF * w], src).then_inc(self.s[f"b_raw{j % 2}"], 16)

    def loads(self, e):
        for j in range(len(self.jobs)):
            self.load(e, j)

    def hi(self, e, j):
        n = HALF * self.jobs[j][1]
        e.wait_ge(self.s[f"b_raw{j % 2}"], 16 * (j // 2 + 1))
        if j >= 2:
            e.wait_ge(self.s["b_acc"], j - 1)
        e.copy(self.hi_[:, j % 2, 0:n], self.raw[:, j % 2, 0:n]).then_inc(self.s["b_hi"], 1)

    def lo(self, e, j):
        n = HALF * self.jobs[j][1]
        e.wait_ge(self.s["b_hi"], j + 1)
        e.tensor_tensor(self.lo_[:, j % 2, 0:n], self.raw[:, j % 2, 0:n], self.hi_[:, j % 2, 0:n].bitcast(F32),
                        ALU.subtract).then_inc(self.s["b_lo"], 1)

    def mm(self, e, j):
        _, w, m_hi, m_lo, k0, first, last = self.jobs[j]
        e.wait_ge(self.s["b_lo"], j + 1)
        if first and self.sum_of[j]:
            self._read(e, self.sum_of[j] - 1)
        for k in range(HALF):
            ins = mm3(e, self.bank[0:w, :], self.hi_[:, j % 2, k * w:(k + 1) * w], self.lo_[:, j % 2, k * w:(k + 1) * w],
                      m_hi[:, k0 + k, :], m_lo[:, k0 + k, :], first and k == 0, last and k == HALF - 1)
        ins.then_inc(self.s["b_acc"], 1)

    def _read(self, e, n):
        if n in self.branches:
            e.wait_ge(self.s["b_pr"], self.branches.index(n) + 1)
        else:
            e.wait_ge(self.s["b_out"], 1 + len([m for m in range(n) if m not in self.branches]))

    def _sum_ready(self, e, n):
        e.wait_ge(self.s["b_acc"], max(j for j, m in enumerate(self.sum_of) if m == n) + 1)

    def out(self, e, n):
        kind, dst = self.sums[n]
        if kind == "branch":
            return
        self._sum_ready(e, n)
        if kind == "gate":
            done = [b for b in self.branches if b < n]
            if done:
                e.wait_ge(self.s["b_pr"], len(done))
            e.activation(self.sg[:, :], self.bank[:, :], ACT.Tanh, scale=0.5).then_inc(self.s["b_out"], 1)
        else:
            i = self.stores.index(n)
            if i >= 2:
                e.wait_ge(self.s[f"b_st{i % 2}"], 16 * (i // 2))
            w = dst.shape[0]
            e.copy(self.stage[0:w, i % 2, :], self.bank[0:w, :]).then_inc(self.s["b_out"], 1)
            self._read(e, n)
            e.dma_start(dst, self.stage[0:w, i % 2, :]).then_inc(self.s[f"b_st{i % 2}"], 16)

    def product(self, e, n):
        i = self.branches.index(n)
        first, chunk = self.sums[n][1]
        self._sum_ready(e, n)
        self._read(e, n - 1)
        if i:
            e.wait_ge(self.s["b_add"], i)
        e.scalar_tensor_tensor(out=self.pr[:, :], in0=self.sg[:, :], scalar=1.0, in1=self.bank[:, :],
                               op0=ALU.add, op1=ALU.mult).then_inc(self.s["b_pr"], 1)

    def add(self, e, n):
        i = self.branches.index(n)
        first, chunk = self.sums[n][1]
        e.wait_ge(self.s["b_pr"], i + 1)
        m = self.merged[:, bass.ds(chunk, 1), :].rearrange("p a n -> p (a n)")
        if first:
            e.tensor_copy(m, self.pr[:, :]).then_inc(self.s["b_add"], 1)
        else:
            e.tensor_tensor(m, m, self.pr[:, :], ALU.add).then_inc(self.s["b_add"], 1)

    def stored(self, e):
        for slot in range(2):
            if n := len(self.stores[slot::2]):
                e.wait_ge(self.s[f"b_st{slot}"], 16 * n)


def column_jobs(src, w, h_hi, h_lo):
    return [(src[:, i * HALF * w:(i + 1) * HALF * w], w, h_hi, h_lo, i * HALF, i == 0, i == 1) for i in range(2)]


def merge_jobs(w_gate, w_branch, h_hi, h_lo, o_hi, o_lo, chunk, first):
    jobs = column_jobs(w_gate, P, h_hi, h_lo) + [(w_branch, P, o_hi, o_lo, 0, True, True)]
    return jobs, [("gate", None), ("branch", (first, chunk))]


def norm_transpose(nc, C, w_pre, h_hi, h_lo):
    s = phase(nc, ["sq", "ln", "rstd", "xn", "tr", "hi"])
    x, ps = C["x"], C["ps"]
    with ExitStack() as ctx:
        xn = ctx.enter_context(sbuf(nc, "nt_xn", [P, NT, D], F32))
        junk = ctx.enter_context(sbuf(nc, "nt_junk", [P, D], F32))
        ssq = ctx.enter_context(sbuf(nc, "nt_ssq", [P, NT], F32))
        rstd = ctx.enter_context(sbuf(nc, "nt_rstd", [P, NT], F32))
        with nc.Block() as block:
            @block.scalar
            def _(e):
                for t in range(NT):
                    if t:
                        e.wait_ge(s["sq"], t)
                    e.activation(junk[:, :], x[:, t, :], ACT.Square, accum_out=ssq[:, t:t + 1]).then_inc(s["sq"], 1)
                e.wait_ge(s["sq"], NT)
                e.activation(rstd[:, :], ssq[:, :], ACT.Ln, bias=C["eps"], scale=1.0 / D).then_inc(s["ln"], 1)
                e.wait_ge(s["ln"], 1)
                e.activation(rstd[:, :], rstd[:, :], ACT.Exp, scale=-0.5).then_inc(s["rstd"], 1)
                for t in range(NT):
                    for half in range(2):
                        e.wait_ge(s["tr"], 2 * t + half + 1)
                        for b in range(4):
                            k = 4 * half + b
                            ins = e.mul(h_hi[:, k, t * P:(t + 1) * P], ps[2 * t + half][:, b * P:(b + 1) * P], w_pre[:, k:k + 1])
                        ins.then_inc(s["hi"], 1)

            @block.vector
            def _(e):
                e.wait_ge(s["rstd"], 1)
                for t in range(NT):
                    e.tensor_scalar(xn[:, t, :], x[:, t, :], rstd[:, t:t + 1], None, ALU.mult).then_inc(s["xn"], 1)
                for t in range(NT):
                    for half in range(2):
                        e.wait_ge(s["hi"], 2 * t + half + 1)
                        for b in range(4):
                            k = 4 * half + b
                            e.scalar_tensor_tensor(out=h_lo[:, k, t * P:(t + 1) * P], in0=ps[2 * t + half][:, b * P:(b + 1) * P],
                                                   scalar=w_pre[:, k:k + 1], in1=h_hi[:, k, t * P:(t + 1) * P].bitcast(F32),
                                                   op0=ALU.mult, op1=ALU.subtract)

            @block.tensor
            def _(e):
                for t in range(NT):
                    e.wait_ge(s["xn"], t + 1)
                    for half in range(2):
                        for b in range(4):
                            k = 4 * half + b
                            ins = e.transpose(ps[2 * t + half][:, b * P:(b + 1) * P], xn[:, t, k * P:(k + 1) * P], C["ident"])
                        ins.then_inc(s["tr"], 1)
    retire(nc, s)


def weight_buffers(nc, ctx):
    raw = ctx.enter_context(sbuf(nc, "w_raw", [P, 2, D], F32))
    hi = ctx.enter_context(sbuf(nc, "w_hi", [P, 2, D], F32R))
    lo = ctx.enter_context(sbuf(nc, "w_lo", [P, 2, D], F32R))
    return raw, hi, lo


def ffn_gate_up(nc, C, l, w_gu, h_hi, h_lo, a_hi, a_lo):
    s = phase(nc, ["raw0", "raw1", "hi0", "hi1", "lo0", "lo1", "acc0", "acc1", "silu", "act", "ahi", "alo"])
    ps = C["ps"]
    with ExitStack() as ctx:
        raw, hi, lo = weight_buffers(nc, ctx)
        sg = ctx.enter_context(sbuf(nc, "sg", [P, S], F32))
        a32 = ctx.enter_context(sbuf(nc, "a32", [P, S], F32))
        RAW, HI, LO, ACC = ([s[n + "0"], s[n + "1"]] for n in ("raw", "hi", "lo", "acc"))
        FREE = [s["silu"], s["act"]]
        with nc.Block() as block:
            @block.sync
            def _(e):
                with e.Fori(0, KF) as it:
                    for u in range(2):
                        e.wait_ge(LO[u], it + 1)
                        e.dma_start(raw[:, u, :], w_gu[l, it, u]).then_inc(RAW[u], 16)

            @block.tensor
            def _(e):
                for u in range(2):
                    e.sem_inc(ACC[u], 1)
                with e.Fori(0, KF) as it:
                    for u in range(2):
                        e.wait_ge(HI[u], it + 1)
                        e.wait_ge(LO[u], it + 2)
                        e.wait_ge(FREE[u], it + 1)
                        for k in range(KD):
                            ins = mm3(e, ps[u][:, :], hi[:, u, k * P:(k + 1) * P], lo[:, u, k * P:(k + 1) * P],
                                      h_hi[:, k, :], h_lo[:, k, :], k == 0, k == KD - 1)
                        ins.then_inc(ACC[u], 1)

            @block.scalar
            def _(e):
                def split_hi(it, u):
                    e.wait_ge(RAW[u], 16 * (it + 1))
                    e.wait_ge(ACC[u], it + 1)
                    e.copy(hi[:, u, :], raw[:, u, :]).then_inc(HI[u], 1)

                e.sem_inc(s["silu"], 1)

                def silu(it):
                    e.wait_ge(ACC[0], it + 2)
                    e.wait_ge(s["act"], it + 1)
                    e.activation(sg[:, :], ps[0][:, :], ACT.Silu).then_inc(s["silu"], 1)

                def a_hi_copy(it):
                    e.wait_ge(s["act"], it + 2)
                    e.copy(a_hi[:, it, :], a32[:, :]).then_inc(s["ahi"], 1)

                split_hi(0, 0)
                split_hi(0, 1)
                with e.Fori(0, KF - 1) as it:
                    split_hi(it + 1, 0)
                    silu(it)
                    split_hi(it + 1, 1)
                    a_hi_copy(it)
                silu(KF - 1)
                a_hi_copy(KF - 1)

            @block.vector
            def _(e):
                for n in ("lo0", "lo1", "act", "alo"):
                    e.sem_inc(s[n], 1)

                def split_lo(it, u):
                    e.wait_ge(HI[u], it + 1)
                    e.tensor_tensor(lo[:, u, :], raw[:, u, :], hi[:, u, :].bitcast(F32), ALU.subtract).then_inc(LO[u], 1)

                def act(it):
                    e.wait_ge(ACC[1], it + 2)
                    e.wait_ge(s["silu"], it + 2)
                    e.wait_ge(s["alo"], it + 1)
                    e.tensor_tensor(a32[:, :], sg[:, :], ps[1][:, :], ALU.mult).then_inc(s["act"], 1)

                def a_lo_sub(it):
                    e.wait_ge(s["ahi"], it + 1)
                    e.tensor_tensor(a_lo[:, it, :], a32[:, :], a_hi[:, it, :].bitcast(F32), ALU.subtract).then_inc(s["alo"], 1)

                split_lo(0, 0)
                split_lo(0, 1)
                with e.Fori(0, KF - 1) as it:
                    split_lo(it + 1, 0)
                    act(it)
                    split_lo(it + 1, 1)
                    a_lo_sub(it)
                act(KF - 1)
                a_lo_sub(KF - 1)
    retire(nc, s)


def contract(nc, C, l, w_rows, kc, m_hi, m_lo, yT):
    s = phase(nc, ["raw0", "raw1", "hi0", "hi1", "lo0", "lo1", "used0", "used1"])
    ps = C["ps"]
    pairs = kc // 2
    with ExitStack() as ctx:
        raw, hi, lo = weight_buffers(nc, ctx)
        RAW, HI, LO, USED = ([s[n + "0"], s[n + "1"]] for n in ("raw", "hi", "lo", "used"))
        with nc.Block() as block:
            @block.sync
            def _(e):
                with e.Fori(0, pairs) as it:
                    for u in range(2):
                        e.wait_ge(LO[u], it + 1)
                        e.dma_start(raw[:, u, :], w_rows[l, it, u]).then_inc(RAW[u], 16)

            @block.scalar
            def _(e):
                with e.Fori(0, pairs) as it:
                    for u in range(2):
                        e.wait_ge(RAW[u], 16 * (it + 1))
                        e.wait_ge(USED[u], it + 1)
                        e.copy(hi[:, u, :], raw[:, u, :]).then_inc(HI[u], 1)
                e.wait_ge(USED[0], pairs + 1)
                e.wait_ge(USED[1], pairs + 1)
                for c in range(0, KD, 2):
                    e.copy(yT[:, c, :], ps[c][:, :])

            @block.vector
            def _(e):
                e.sem_inc(LO[0], 1)
                e.sem_inc(LO[1], 1)
                with e.Fori(0, pairs) as it:
                    for u in range(2):
                        e.wait_ge(HI[u], it + 1)
                        e.tensor_tensor(lo[:, u, :], raw[:, u, :], hi[:, u, :].bitcast(F32), ALU.subtract).then_inc(LO[u], 1)
                e.wait_ge(USED[0], pairs + 1)
                e.wait_ge(USED[1], pairs + 1)
                for c in range(1, KD, 2):
                    e.tensor_copy(yT[:, c, :], ps[c][:, :])

            @block.tensor
            def _(e):
                e.sem_inc(USED[0], 1)
                e.sem_inc(USED[1], 1)

                def pair(it, first, last):
                    for u in range(2):
                        e.wait_ge(HI[u], it + 1)
                        e.wait_ge(LO[u], it + 2)
                        for c in range(KD):
                            ins = mm3(e, ps[c][:, :], hi[:, u, c * P:(c + 1) * P], lo[:, u, c * P:(c + 1) * P],
                                      m_hi[:, 2 * it + u, :], m_lo[:, 2 * it + u, :], first and u == 0, last and u == 1)
                        ins.then_inc(USED[u], 1)

                pair(0, True, False)
                with e.Fori(1, pairs - 1) as it:
                    pair(it, False, False)
                pair(pairs - 1, False, True)
    retire(nc, s)


def residual(nc, C, l, yT, w_post, res):
    s = phase(nc, ["wp", "tr", "sq", "add", "ln", "rstd", "t", "x"])
    x, ps = C["x"], C["ps"]
    with ExitStack() as ctx:
        wp = ctx.enter_context(sbuf(nc, "rs_wp", [P, D], F32))
        junk = ctx.enter_context(sbuf(nc, "rs_junk", [P, 2, S], F32))
        tmp = ctx.enter_context(sbuf(nc, "rs_tmp", [P, 2, S], F32))
        ssq = ctx.enter_context(sbuf(nc, "rs_ssq", [P, NT, 2], F32))
        rstd = ctx.enter_context(sbuf(nc, "rs_rstd", [P, NT], F32))
        with nc.Block() as block:
            @block.sync
            def _(e):
                e.dma_start(wp[:, :], w_post[l].partition_broadcast(P)).then_inc(s["wp"], 16)

            @block.tensor
            def _(e):
                for t in range(NT):
                    for c in range(KD):
                        ins = e.transpose(ps[2 * t + c // 4][:, (c % 4) * P:(c % 4 + 1) * P], yT[:, c, t * P:(t + 1) * P], C["ident"])
                    ins.then_inc(s["tr"], 1)

            @block.scalar
            def _(e):
                for t in range(NT):
                    e.wait_ge(s["tr"], t + 1)
                    for half in range(2):
                        if t:
                            e.wait_ge(s["sq"], 2 * t + half - 1)
                        e.activation(junk[:, half, :], ps[2 * t + half][:, :], ACT.Square,
                                     accum_out=ssq[:, t, half:half + 1]).then_inc(s["sq"], 1)
                e.wait_ge(s["add"], 1)
                e.activation(rstd[:, :], rstd[:, :], ACT.Ln, bias=C["eps"], scale=1.0 / D).then_inc(s["ln"], 1)
                e.wait_ge(s["ln"], 1)
                e.activation(rstd[:, :], rstd[:, :], ACT.Exp, scale=-0.5).then_inc(s["rstd"], 1)

            @block.vector
            def _(e):
                e.wait_ge(s["sq"], 2 * NT)
                e.tensor_tensor(rstd[:, :], ssq[:, :, 0], ssq[:, :, 1], ALU.add).then_inc(s["add"], 1)
                e.wait_ge(s["rstd"], 1)
                e.wait_ge(s["wp"], 16)
                for n in range(2 * NT):
                    t, half = n // 2, n % 2
                    cols = slice(half * S, (half + 1) * S)
                    if n >= 2:
                        e.wait_ge(s["x"], n - 1)
                    e.scalar_tensor_tensor(out=tmp[:, half, :], in0=ps[n][:, :], scalar=rstd[:, t:t + 1], in1=wp[:, cols],
                                           op0=ALU.mult, op1=ALU.mult).then_inc(s["t"], 1)
                    e.wait_ge(s["t"], n + 1)
                    e.scalar_tensor_tensor(out=x[:, t, cols], in0=tmp[:, half, :], scalar=res, in1=x[:, t, cols],
                                           op0=ALU.mult, op1=ALU.add).then_inc(s["x"], 1)
    retire(nc, s)


def ffn(nc, C, l, w_pre, w_gu, w_down, w_post):
    with ExitStack() as outer:
        a_hi = outer.enter_context(sbuf(nc, "a_hi", [P, KF, S], F32R))
        a_lo = outer.enter_context(sbuf(nc, "a_lo", [P, KF, S], F32R))
        with ExitStack() as ctx:
            h_hi = ctx.enter_context(sbuf(nc, "h_hi", [P, KD, S], F32R))
            h_lo = ctx.enter_context(sbuf(nc, "h_lo", [P, KD, S], F32R))
            norm_transpose(nc, C, w_pre, h_hi, h_lo)
            ffn_gate_up(nc, C, l, w_gu, h_hi, h_lo, a_hi, a_lo)
        with ExitStack() as ctx:
            yT = ctx.enter_context(sbuf(nc, "yT", [P, KD, S], F32))
            contract(nc, C, l, w_down, KF, a_hi, a_lo, yT)
            residual(nc, C, l, yT, w_post, 0.5)


def project(nc, C, h_hi, h_lo, runs):
    s = phase(nc, ["raw0", "raw1", "hi0", "hi1", "lo0", "lo1", "acc0", "acc1", "free0", "free1"])
    ps = C["ps"]
    with ExitStack() as ctx:
        raw, hi, lo = weight_buffers(nc, ctx)
        RAW, HI, LO, ACC, FREE = ([s[n + "0"], s[n + "1"]] for n in ("raw", "hi", "lo", "acc", "free"))

        def over(e, n, body, first=0):
            if n - first == 1:
                body(first)
            elif n > first:
                with e.Fori(first, n) as it:
                    body(it)

        def starts():
            seen, out = [0, 0], []
            for iters, widths, _, _ in runs:
                out.append(tuple(seen))
                for u in range(len(widths)):
                    seen[u] += iters
            return out

        BASE = starts()
        with nc.Block() as block:
            @block.sync
            def _(e):
                for (iters, widths, src, _), base in zip(runs, BASE):
                    def body(it):
                        for u, w in enumerate(widths):
                            e.wait_ge(LO[u], it + (base[u] + 1))
                            e.dma_start(raw[:, u, 0:KD * w], src(it, u)).then_inc(RAW[u], 16)
                    over(e, iters, body)

            @block.tensor
            def _(e):
                for u in range(2):
                    e.sem_inc(ACC[u], 1)
                for (iters, widths, _, _), base in zip(runs, BASE):
                    def body(it):
                        for u, w in enumerate(widths):
                            e.wait_ge(HI[u], it + (base[u] + 1))
                            e.wait_ge(LO[u], it + (base[u] + 2))
                            e.wait_ge(FREE[u], it + (base[u] + 1))
                            for k in range(KD):
                                ins = mm3(e, ps[u][0:w, :], hi[:, u, k * w:(k + 1) * w], lo[:, u, k * w:(k + 1) * w],
                                          h_hi[:, k, :], h_lo[:, k, :], k == 0, k == KD - 1)
                            ins.then_inc(ACC[u], 1)
                    over(e, iters, body)

            @block.scalar
            def _(e):
                e.sem_inc(FREE[0], 1)
                for (iters, widths, _, dst), base in zip(runs, BASE):
                    def split_hi(it, u):
                        n = KD * widths[u]
                        e.wait_ge(RAW[u], 16 * it + 16 * (base[u] + 1))
                        e.wait_ge(ACC[u], it + (base[u] + 1))
                        e.copy(hi[:, u, 0:n], raw[:, u, 0:n]).then_inc(HI[u], 1)

                    def out0(it):
                        e.wait_ge(ACC[0], it + (base[0] + 2))
                        e.copy(dst(it, 0), ps[0][0:widths[0], :]).then_inc(FREE[0], 1)

                    for u in range(len(widths)):
                        split_hi(0, u)

                    def body(it):
                        split_hi(it + 1, 0)
                        out0(it)
                        if len(widths) > 1:
                            split_hi(it + 1, 1)
                    over(e, iters - 1, body)
                    out0(iters - 1)

            @block.vector
            def _(e):
                e.sem_inc(LO[0], 1)
                e.sem_inc(LO[1], 1)
                e.sem_inc(FREE[1], 1)
                for (iters, widths, _, dst), base in zip(runs, BASE):
                    def split_lo(it, u):
                        n = KD * widths[u]
                        e.wait_ge(HI[u], it + (base[u] + 1))
                        e.tensor_tensor(lo[:, u, 0:n], raw[:, u, 0:n], hi[:, u, 0:n].bitcast(F32), ALU.subtract).then_inc(LO[u], 1)

                    def out1(it):
                        e.wait_ge(ACC[1], it + (base[1] + 2))
                        e.tensor_copy(dst(it, 1), ps[1][0:widths[1], :]).then_inc(FREE[1], 1)

                    for u in range(len(widths)):
                        split_lo(0, u)

                    def body(it):
                        split_lo(it + 1, 0)
                        if len(widths) > 1:
                            out1(it)
                            split_lo(it + 1, 1)
                    over(e, iters - 1, body)
                    if len(widths) > 1:
                        out1(iters - 1)
    retire(nc, s)


def merge_branch(nc, C, l, w_gate, w_branch, h_hi, h_lo, o_hi, o_lo, merged, first):
    s = phase(nc, ["raw0", "raw1", "hi0", "hi1", "lo0", "lo1", "acc0", "acc1", "sig", "prod", "sum"])
    ps = C["ps"]
    KO = 4
    with ExitStack() as ctx:
        raw, hi, lo = weight_buffers(nc, ctx)
        sg = ctx.enter_context(sbuf(nc, "mb_sig", [P, S], F32))
        pr = ctx.enter_context(sbuf(nc, "mb_prod", [P, S], F32))
        RAW, HI, LO, ACC = ([s[n + "0"], s[n + "1"]] for n in ("raw", "hi", "lo", "acc"))
        N = [KD * P, KO * P]
        with nc.Block() as block:
            @block.sync
            def _(e):
                with e.Fori(0, KD) as it:
                    for u, w in enumerate((w_gate, w_branch)):
                        e.wait_ge(LO[u], it + 1)
                        e.dma_start(raw[:, u, 0:N[u]], w[l, it]).then_inc(RAW[u], 16)

            @block.tensor
            def _(e):
                for u in range(2):
                    e.sem_inc(ACC[u], 1)
                with e.Fori(0, KD) as it:
                    for u, (kc, m_hi, m_lo) in enumerate(((KD, h_hi, h_lo), (KO, o_hi, o_lo))):
                        e.wait_ge(HI[u], it + 1)
                        e.wait_ge(LO[u], it + 2)
                        e.wait_ge(s["prod"] if u else s["sig"], it + 1)
                        for k in range(kc):
                            ins = mm3(e, ps[u][:, :], hi[:, u, k * P:(k + 1) * P], lo[:, u, k * P:(k + 1) * P],
                                      m_hi[:, k, :], m_lo[:, k, :], k == 0, k == kc - 1)
                        ins.then_inc(ACC[u], 1)

            @block.scalar
            def _(e):
                e.sem_inc(s["sig"], 1)

                def split_hi(it, u):
                    e.wait_ge(RAW[u], 16 * it + 16)
                    e.wait_ge(ACC[u], it + 1)
                    e.copy(hi[:, u, 0:N[u]], raw[:, u, 0:N[u]]).then_inc(HI[u], 1)

                def sigmoid(it):
                    e.wait_ge(ACC[0], it + 2)
                    e.wait_ge(s["prod"], it + 1)
                    e.activation(sg[:, :], ps[0][:, :], ACT.Tanh, scale=0.5).then_inc(s["sig"], 1)

                split_hi(0, 0)
                split_hi(0, 1)
                with e.Fori(0, KD - 1) as it:
                    split_hi(it + 1, 0)
                    sigmoid(it)
                    split_hi(it + 1, 1)
                sigmoid(KD - 1)

            @block.vector
            def _(e):
                for n in ("lo0", "lo1", "prod", "sum"):
                    e.sem_inc(s[n], 1)

                def split_lo(it, u):
                    e.wait_ge(HI[u], it + 1)
                    e.tensor_tensor(lo[:, u, 0:N[u]], raw[:, u, 0:N[u]], hi[:, u, 0:N[u]].bitcast(F32),
                                    ALU.subtract).then_inc(LO[u], 1)

                def combine(it):
                    e.wait_ge(ACC[1], it + 2)
                    e.wait_ge(s["sig"], it + 2)
                    if first:
                        e.scalar_tensor_tensor(out=merged[:, it, :], in0=sg[:, :], scalar=1.0, in1=ps[1][:, :],
                                               op0=ALU.add, op1=ALU.mult).then_inc(s["prod"], 1)
                    else:
                        e.wait_ge(s["sum"], it + 1)
                        e.scalar_tensor_tensor(out=pr[:, :], in0=sg[:, :], scalar=1.0, in1=ps[1][:, :],
                                               op0=ALU.add, op1=ALU.mult).then_inc(s["prod"], 1)
                        e.wait_ge(s["prod"], it + 2)
                        e.tensor_tensor(merged[:, it, :], merged[:, it, :], pr[:, :], ALU.add).then_inc(s["sum"], 1)

                split_lo(0, 0)
                split_lo(0, 1)
                with e.Fori(0, KD - 1) as it:
                    split_lo(it + 1, 0)
                    combine(it)
                    split_lo(it + 1, 1)
                combine(KD - 1)
    retire(nc, s)


def gated_output(nc, C, o_raw, z, norm_w, o_hi, o_lo):
    s = phase(nc, ["sq", "ss", "ln", "rs", "silu", "a", "b", "hi"])
    ps = C["ps"]
    H = 4
    with ExitStack() as ctx:
        sq = ctx.enter_context(sbuf(nc, "go_sq", [P, H, S], F32))
        rs = ctx.enter_context(sbuf(nc, "go_rs", [P, H, S], F32))
        sz = ctx.enter_context(sbuf(nc, "go_sz", [P, H, S], F32))
        with nc.Block() as block:
            @block.scalar
            def _(e):
                e.activation(sz[:, :, :], z, ACT.Silu).then_inc(s["silu"], 1)
                for h in range(H):
                    e.activation(sq[:, h, :], o_raw[:, h, :], ACT.Square).then_inc(s["sq"], 1)
                for h in range(H):
                    e.wait_ge(s["ss"], h + 1)
                    e.activation(rs[:, h, :], ps[h][:, :], ACT.Ln, bias=C["eps"], scale=1.0 / P).then_inc(s["ln"], 1)
                for h in range(H):
                    e.wait_ge(s["ln"], h + 1)
                    e.activation(rs[:, h, :], rs[:, h, :], ACT.Exp, scale=-0.5).then_inc(s["rs"], 1)
                for h in range(H):
                    e.wait_ge(s["b"], h + 1)
                    e.copy(o_hi[:, h, :], sz[:, h, :]).then_inc(s["hi"], 1)

            @block.tensor
            def _(e):
                for h in range(H):
                    e.wait_ge(s["sq"], h + 1)
                    e.matmul(ps[h][:, :], C["ones"], sq[:, h, :], start=True, stop=True).then_inc(s["ss"], 1)

            @block.vector
            def _(e):
                e.wait_ge(s["silu"], 1)
                for h in range(H):
                    e.wait_ge(s["rs"], h + 1)
                    e.scalar_tensor_tensor(out=rs[:, h, :], in0=o_raw[:, h, :], scalar=norm_w, in1=rs[:, h, :],
                                           op0=ALU.mult, op1=ALU.mult).then_inc(s["a"], 1)
                    e.wait_ge(s["a"], h + 1)
                    e.tensor_tensor(sz[:, h, :], sz[:, h, :], rs[:, h, :], ALU.mult).then_inc(s["b"], 1)
                for h in range(H):
                    e.wait_ge(s["hi"], h + 1)
                    e.tensor_tensor(o_lo[:, h, :], sz[:, h, :], o_hi[:, h, :].bitcast(F32), ALU.subtract)
    retire(nc, s)


def gdn_prepare(nc, C, prm, pT, miscT, qkv, ba, beta, g):
    s = phase(nc, ["conv", "silu", "sq", "ss", "ln", "rs", "tr", "ba", "y", "ny", "my", "ex", "lg", "eb", "ea", "b1", "sp"])
    ps = C["ps"]
    QKV = 3 * GDN_H
    with ExitStack() as ctx:
        cv = ctx.enter_context(sbuf(nc, "cv", [P, 2, S], F32))
        sq = ctx.enter_context(sbuf(nc, "l2_sq", [P, 4, S], F32))
        rs = ctx.enter_context(sbuf(nc, "l2_rs", [P, 2 * GDN_H, S], F32))
        y = ctx.enter_context(sbuf(nc, "sp_y", [P, NT, 4], F32))
        ny = ctx.enter_context(sbuf(nc, "sp_ny", [P, NT, 4], F32))
        ea = ctx.enter_context(sbuf(nc, "exp_a_log", [P, 4], F32))
        eb = ctx.enter_context(sbuf(nc, "exp_b", [P, NT, 4], F32))
        w = prm["conv"]
        with nc.Block() as block:
            @block.vector
            def _(e):
                for c in range(QKV):
                    if c >= 2:
                        e.wait_ge(s["silu"], c - 1)
                    for n, j in enumerate(range(3, -1, -1)):
                        src = pT[:, c, 1 + j:1 + j + S]
                        wj = w[:, j * QKV + c:j * QKV + c + 1]
                        if n == 0:
                            e.tensor_scalar(cv[:, c % 2, :], src, wj, None, ALU.mult).then_inc(s["conv"], 1)
                        else:
                            e.wait_ge(s["conv"], 4 * c + n)
                            e.scalar_tensor_tensor(out=cv[:, c % 2, :], in0=src, scalar=wj, in1=cv[:, c % 2, :],
                                                   op0=ALU.mult, op1=ALU.add).then_inc(s["conv"], 1)
                e.wait_ge(s["tr"], 1)
                e.tensor_copy(ba[:, :, :], ps[7][:, :].rearrange("p (t c) -> p t c", t=NT)[:, :, 0:80]).then_inc(s["ba"], 1)
                e.wait_ge(s["ba"], 1)
                e.tensor_tensor(y[:, :, :], ba[:, :, 4:8], prm["dt_bias"].unsqueeze(1).to_broadcast([P, NT, 4]), ALU.add).then_inc(s["y"], 1)
                e.wait_ge(s["y"], 1)
                e.tensor_scalar(ny[:, :, :], y[:, :, :], -1.0, None, ALU.mult).then_inc(s["ny"], 1)
                e.wait_ge(s["ny"], 1)
                e.tensor_tensor(ny[:, :, :], ny[:, :, :], y[:, :, :], ALU.min).then_inc(s["my"], 1)
                e.wait_ge(s["eb"], 1)
                e.tensor_scalar(eb[:, :, :], eb[:, :, :], 1.0, None, ALU.add).then_inc(s["b1"], 1)
                e.wait_ge(s["b1"], 1)
                e.reciprocal(beta[:, :, :], eb[:, :, :])
                e.wait_ge(s["lg"], 1)
                e.scalar_tensor_tensor(out=y[:, :, :], in0=y[:, :, :], scalar=0.0, in1=ny[:, :, :], op0=ALU.max, op1=ALU.add).then_inc(s["sp"], 1)
                e.wait_ge(s["sp"], 1)
                e.wait_ge(s["ea"], 1)
                e.scalar_tensor_tensor(out=g[:, :, :], in0=y[:, :, :], scalar=-1.0, in1=ea[:, :].unsqueeze(1).to_broadcast([P, NT, 4]),
                                       op0=ALU.mult, op1=ALU.mult)
                for c in range(2 * GDN_H):
                    e.wait_ge(s["rs"], c + 1)
                    e.scalar_tensor_tensor(out=qkv[:, c, :], in0=qkv[:, c, :], scalar=(P ** -0.5 if c < GDN_H else 1.0),
                                           in1=rs[:, c, :], op0=ALU.mult, op1=ALU.mult).then_inc(s["sp"], 1)

            @block.scalar
            def _(e):
                for c in range(QKV):
                    e.wait_ge(s["conv"], 4 * (c + 1))
                    e.activation(qkv[:, c, :], cv[:, c % 2, :], ACT.Silu).then_inc(s["silu"], 1)
                e.activation(ea[:, :], prm["a_log"], ACT.Exp).then_inc(s["ea"], 1)
                e.wait_ge(s["ba"], 1)
                e.activation(eb[:, :, :], ba[:, :, 0:4], ACT.Exp, scale=-1.0).then_inc(s["eb"], 1)
                e.wait_ge(s["my"], 1)
                e.activation(ny[:, :, :], ny[:, :, :], ACT.Exp).then_inc(s["ex"], 1)
                e.wait_ge(s["ex"], 1)
                e.activation(ny[:, :, :], ny[:, :, :], ACT.Ln, bias=C["one"]).then_inc(s["lg"], 1)
                for c in range(2 * GDN_H):
                    e.wait_ge(s["ss"], c + 1)
                    e.activation(rs[:, c, :], ps[c % 4][:, :], ACT.Ln, bias=C["eps"]).then_inc(s["ln"], 1)
                for c in range(2 * GDN_H):
                    e.wait_ge(s["ln"], c + 1)
                    e.activation(rs[:, c, :], rs[:, c, :], ACT.Exp, scale=-0.5).then_inc(s["rs"], 1)

            @block.gpsimd
            def _(e):
                for c in range(2 * GDN_H):
                    e.wait_ge(s["silu"], c + 1)
                    if c >= 4:
                        e.wait_ge(s["ss"], c - 3)
                    e.tensor_tensor(sq[:, c % 4, :], qkv[:, c, :], qkv[:, c, :], ALU.mult).then_inc(s["sq"], 1)

            @block.tensor
            def _(e):
                for t in range(NT):
                    ins = e.transpose(ps[7][:, t * P:t * P + 80], miscT[:, t * P:(t + 1) * P], C["ident"][0:80, 0:80])
                ins.then_inc(s["tr"], 1)
                for c in range(2 * GDN_H):
                    e.wait_ge(s["sq"], c + 1)
                    if c >= 4:
                        e.wait_ge(s["ln"], c - 3)
                    e.matmul(ps[c % 4][:, :], C["ones"], sq[:, c % 4, :], start=True, stop=True).then_inc(s["ss"], 1)
    retire(nc, s)


def gdn_tile(nc, C, W, t, jobs, sums):
    s = phase(nc, ["qt", "kt", "vt", "gb", "gcb", "gc", "gcs", "dt0", "dt1", "dn0", "dn1", "eg", "egc", "ekd", "kd0", "qd",
                   "kk", "kq", "dtm", "at", "L0", "bbeta", "trk", "trv", "kde", "ken", "vb", "lv", "b1t", "T", "U", "q", "qs",
                   "uq", "wu", "u", "wt", "vs", "vn", "o", "st", "S", "os"] + Background.SEMS)
    ps = C["ps"]
    bg = Background(C, s, jobs, sums, ps[6])
    H = GDN_H
    HB = lambda ap: ap.rearrange("p (h c) -> p h c", h=H)
    cols = bass.ts(t, P)
    (qt, kt, vt, gb, DT, DN, EG, L, AT, B, Tm, U, Q, u, wT, kd, vb, kbe, qd, vn, St, sm) = (
        W[n] for n in ("qt", "kt", "vt", "gb", "DT", "DN", "EG", "L", "AT", "B", "Tm", "U", "Q", "u", "wT", "kd", "vb",
                       "kbe", "qd", "vn", "St", "sm"))
    qkv, beta, g, o_raw = W["qkv"], W["beta"], W["g"], W["o_raw"]
    gc, ekd, egc, beg, bt, gt = (sm[:, i, :] for i in range(6))
    lvl = lambda n: C["lvl"][:, n * P:(n + 1) * P].unsqueeze(1).to_broadcast([P, H, P])
    bc = lambda ap: ap.unsqueeze(1).to_broadcast([P, H, P])
    NL = 6
    with nc.Block() as block:
        @block.sync
        def _(e):
            bg.loads(e)

        @block.gpsimd
        def _(e):
            bg.lo(e, 0)
            bg.lo(e, 1)
            e.wait_ge(s["L0"], H)
            for n in range(NL):
                e.tensor_tensor(B[:, n, :, :], L[:, :, :], lvl(n), ALU.mult).then_inc(s["lv"], 1)
                if n:
                    bg.lo(e, n + 1)
            for j in range(NL + 1, len(jobs)):
                bg.lo(e, j)

        @block.vector
        def _(e):
            e.tensor_copy(gt, g[:, bass.ds(t, 1), :].rearrange("p a h -> p (a h)")).then_inc(s["gc"], 1)
            e.tensor_copy(bt, beta[:, bass.ds(t, 1), :].rearrange("p a h -> p (a h)")).then_inc(s["bbeta"], 1)
            e.wait_ge(s["gc"], 1)
            e.tensor_tensor(gb[:, :, :], bc(C["ones"]), gt.unsqueeze(2).to_broadcast([P, H, P]), ALU.mult).then_inc(s["gb"], 1)
            e.wait_ge(s["gcb"], 1)
            e.tensor_copy(gc, ps[0][:, 0:H]).then_inc(s["gcs"], 1)
            e.wait_ge(s["gcs"], 1)
            e.tensor_tensor(ekd, ps[0][:, H:2 * H], gc, ALU.subtract).then_inc(s["ekd"], 1)
            gcB = HB(ps[1][:, :])
            e.wait_ge(s["eg"], 1)
            for h in range(H):
                e.tensor_scalar(DT[:, h, :], gcB[:, h, :], gc[:, h:h + 1], 0.0, ALU.subtract, ALU.min).then_inc(s["dt0"], 1)
                e.tensor_scalar(DN[:, h, :], gcB[:, h, :], gc[:, h:h + 1], 0.0, ALU.subtract, ALU.max).then_inc(s["dn0"], 1)
            e.wait_ge(s["dt1"], 1)
            e.tensor_tensor(DT[:, :, :], DT[:, :, :], bc(C["tri64"]), ALU.mult).then_inc(s["dtm"], 1)
            e.wait_ge(s["kk"], 1)
            e.wait_ge(s["dn1"], 1)
            e.wait_ge(s["bbeta"], 1)
            for h in range(H):
                e.scalar_tensor_tensor(out=L[:, h, :], in0=HB(ps[2][:, :])[:, h, :], scalar=bt[:, h:h + 1], in1=DN[:, h, :],
                                       op0=ALU.mult, op1=ALU.mult).then_inc(s["L0"], 1)
            e.wait_ge(s["kq"], 1)
            e.wait_ge(s["dtm"], 1)
            e.tensor_tensor(AT[:, :, :], HB(ps[3][:, :]), DT[:, :, :], ALU.mult).then_inc(s["at"], 1)
            e.wait_ge(s["eg"], 1)
            e.wait_ge(s["qt"], 1)
            e.tensor_tensor(qd[:, :, :], qt[:, :, :], EG[:, :, :], ALU.mult).then_inc(s["qd"], 1)
            e.wait_ge(s["egc"], 2)
            e.tensor_tensor(beg, egc, bt, ALU.mult).then_inc(s["ken"], 1)
            e.wait_ge(s["ken"], 1)
            e.wait_ge(s["trk"], 1)
            for h in range(H):
                kn = HB(ps[4][:, :])[:, h, :]
                e.tensor_scalar(kd[:, h, :], kn, ekd[:, h:h + 1], None, ALU.mult).then_inc(s["kde"], 1)
                e.tensor_scalar(kbe[:, h, :], kn, beg[:, h:h + 1], None, ALU.mult).then_inc(s["kde"], 1)
            e.wait_ge(s["trv"], 1)
            for h in range(H):
                e.tensor_scalar(vb[:, h, :], HB(ps[5][:, :])[:, h, :], bt[:, h:h + 1], None, ALU.mult).then_inc(s["vb"], 1)
            e.wait_ge(s["lv"], 1)
            e.tensor_tensor(Tm[:, :, :], bc(C["ident"]), B[:, 0, :, :], ALU.subtract).then_inc(s["T"], 1)
            e.wait_ge(s["b1t"], 1)
            e.tensor_tensor(U[:, :, :], bc(C["ident"]), HB(ps[0][:, :]), ALU.subtract).then_inc(s["U"], 1)
            for n in range(1, NL):
                e.wait_ge(s["q"], n)
                e.tensor_copy(Q[:, :, :], HB(ps[1][:, :])).then_inc(s["qs"], 1)
                e.wait_ge(s["uq"], n)
                e.tensor_tensor(U[:, :, :], U[:, :, :], HB(ps[2][:, :]), ALU.subtract).then_inc(s["U"], 1)
                if n < NL - 1:
                    e.tensor_tensor(Tm[:, :, :], Tm[:, :, :], HB(ps[3][:, :]), ALU.subtract).then_inc(s["T"], 1)
            e.wait_ge(s["wu"], 1)
            e.tensor_copy(u[:, :, :], HB(ps[4][:, :])).then_inc(s["u"], 1)
            e.wait_ge(s["u"], 1)
            for c in range(2):
                rows = slice(c * GDN_C, (c + 1) * GDN_C)
                e.wait_ge(s["vs"], c + 1)
                e.tensor_tensor(vn[rows, :, :], u[rows, :, :], HB(ps[2][rows, :]), ALU.subtract).then_inc(s["vn"], 1)
                e.wait_ge(s["st"], c + 1)
                for h in range(H):
                    last = (c + 1) * GDN_C - 1
                    e.scalar_tensor_tensor(out=St[:, h, :], in0=St[:, h, :], scalar=EG[:, h, last:last + 1],
                                           in1=HB(ps[0][:, :])[:, h, :], op0=ALU.mult, op1=ALU.add).then_inc(s["S"], 1)

        @block.scalar
        def _(e):
            e.copy(kt[:, :, :], qkv[:, H:2 * H, cols]).then_inc(s["kt"], 1)
            e.copy(qt[:, :, :], qkv[:, 0:H, cols]).then_inc(s["qt"], 1)
            e.wait_ge(s["gcb"], 1)
            e.activation(EG[:, :, :], HB(ps[1][:, :]), ACT.Exp).then_inc(s["eg"], 1)
            e.copy(vt[:, :, :], qkv[:, 2 * H:3 * H, cols]).then_inc(s["vt"], 1)
            bg.hi(e, 0)
            bg.hi(e, 1)
            e.wait_ge(s["ekd"], 1)
            e.activation(ekd, ekd, ACT.Exp).then_inc(s["egc"], 1)
            e.activation(egc, gc, ACT.Exp).then_inc(s["egc"], 1)
            e.wait_ge(s["dt0"], H)
            e.activation(DT[:, :, :], DT[:, :, :], ACT.Exp).then_inc(s["dt1"], 1)
            e.wait_ge(s["dn0"], H)
            e.activation(DN[:, :, :], DN[:, :, :], ACT.Exp, scale=-1.0).then_inc(s["dn1"], 1)
            for n in range(len(sums) - 1):
                bg.hi(e, 2 * n + 2)
                bg.out(e, n)
                bg.hi(e, 2 * n + 3)
            e.wait_ge(s["wu"], 2)
            e.copy(wT[:, :, :], HB(ps[5][:, :])).then_inc(s["wt"], 1)
            bg.out(e, len(sums) - 1)
            e.wait_ge(s["o"], 2)
            e.copy(o_raw[:, :, cols], HB(ps[3][:, :])).then_inc(s["os"], 1)
            bg.stored(e)

        @block.tensor
        def _(e):
            e.wait_ge(s["gc"], 1)
            e.matmul(ps[0][:, 0:H], C["tri64"], gt, start=True, stop=True)
            e.matmul(ps[0][:, H:2 * H], C["blk64"], gt, start=True, stop=True)
            e.wait_ge(s["gb"], 1)
            for h in range(H):
                ins = e.matmul(HB(ps[1][:, :])[:, h, :], gb[:, h, :], C["tri64"], start=True, stop=True)
            ins.then_inc(s["gcb"], 1)
            e.wait_ge(s["kt"], 1)
            for h in range(H):
                ins = e.matmul(HB(ps[2][:, :])[:, h, :], kt[:, h, :], kt[:, h, :], start=True, stop=True)
            ins.then_inc(s["kk"], 1)
            e.wait_ge(s["qt"], 1)
            for h in range(H):
                ins = e.matmul(HB(ps[3][:, :])[:, h, :], kt[:, h, :], qt[:, h, :], start=True, stop=True)
            ins.then_inc(s["kq"], 1)
            for h in range(H):
                ins = e.transpose(HB(ps[4][:, :])[:, h, :], kt[:, h, :], C["ident"])
            ins.then_inc(s["trk"], 1)
            e.wait_ge(s["vt"], 1)
            for h in range(H):
                ins = e.transpose(HB(ps[5][:, :])[:, h, :], vt[:, h, :], C["ident"])
            ins.then_inc(s["trv"], 1)
            bg.mm(e, 0)
            bg.mm(e, 1)
            e.wait_ge(s["lv"], 1)
            e.wait_ge(s["ekd"], 1)
            for h in range(H):
                ins = e.transpose(HB(ps[0][:, :])[:, h, :], B[:, 0, h, :], C["ident"])
            ins.then_inc(s["b1t"], 1)
            for n in range(1, NL):
                e.wait_ge(s["lv"], n + 1)
                e.wait_ge(s["U"], n)
                e.wait_ge(s["dn0"], H)
                for h in range(H):
                    ins = e.matmul(HB(ps[1][:, :])[:, h, :], B[:, n, h, :], U[:, h, :], start=True, stop=True)
                ins.then_inc(s["q"], 1)
                bg.mm(e, n + 1)
                e.wait_ge(s["qs"], n)
                e.wait_ge(s["T"], n)
                e.wait_ge(s["L0"], H)
                for h in range(H):
                    ins = e.matmul(HB(ps[2][:, :])[:, h, :], Tm[:, h, :], Q[:, h, :], start=True, stop=True)
                if n < NL - 1:
                    e.wait_ge(s["at"], 1)
                    for h in range(H):
                        ins = e.matmul(HB(ps[3][:, :])[:, h, :], Q[:, h, :], Tm[:, h, :], start=True, stop=True)
                ins.then_inc(s["uq"], 1)
            bg.mm(e, NL + 1)
            e.wait_ge(s["U"], NL)
            e.wait_ge(s["vb"], H)
            e.wait_ge(s["kde"], 2 * H)
            for h in range(H):
                ins = e.matmul(HB(ps[4][:, :])[:, h, :], U[:, h, :], vb[:, h, :], start=True, stop=True)
            ins.then_inc(s["wu"], 1)
            for h in range(H):
                ins = e.matmul(HB(ps[5][:, :])[:, h, :], kbe[:, h, :], U[:, h, :], start=True, stop=True)
            ins.then_inc(s["wu"], 1)
            e.wait_ge(s["wt"], 1)
            e.wait_ge(s["at"], 1)
            e.wait_ge(s["qd"], 1)
            for c in range(2):
                rows = slice(c * GDN_C, (c + 1) * GDN_C)
                if c:
                    e.wait_ge(s["S"], H)
                for h in range(H):
                    ins = e.matmul(HB(ps[2][:, :])[:, h, :], wT[:, h, :], St[:, h, :], start=True, stop=True)
                ins.then_inc(s["vs"], 1)
                bg.mm(e, NL + 2 + c)
                e.wait_ge(s["vn"], c + 1)
                for h in range(H):
                    out = HB(ps[3][:, :])[:, h, rows]
                    e.matmul(out, St[:, h, :], qd[:, h, rows], start=True, stop=False)
                    ins = e.matmul(out, vn[rows, h, :], AT[rows, h, rows], start=False, stop=True)
                ins.then_inc(s["o"], 1)
                for h in range(H):
                    ins = e.matmul(HB(ps[0][:, :])[:, h, :], kd[rows, h, :], vn[rows, h, :], start=True, stop=True)
                ins.then_inc(s["st"], 1)
    retire(nc, s)


def gdn(nc, C, prm, l, wd, h_hi, h_lo, miscT, ba, o_hi, o_lo, nsa_rows):
    H = GDN_H
    with ExitStack() as ctx:
        sb = lambda n, shape: ctx.enter_context(sbuf(nc, n, shape, F32))
        z = sb("gdn_z", [P, H, S])
        qkv = sb("gdn_qkv", [P, 3 * H, S])
        beta = sb("gdn_beta", [P, NT, 4])
        g = sb("gdn_g", [P, NT, 4])
        o_raw = sb("gdn_o", [P, H, S])
        with ExitStack() as c2:
            pT = c2.enter_context(sbuf(nc, "gdn_pT", [P, 3 * H, 4 + S], F32))
            zero(nc, pT[:, :, 0:4])
            w_gdn = wd["w_gdn"]
            project(nc, C, h_hi, h_lo, [
                (6, (P, P), lambda it, u: w_gdn[l, 2 * it + u], lambda it, u: pT[:, 2 * it + u, 4:4 + S]),
                (2, (P, P), lambda it, u: w_gdn[l, 2 * it + (12 + u)], lambda it, u: z[:, 2 * it + u, :]),
                (1, (80,), lambda it, u: wd["w_misc"][l], lambda it, u: miscT[:, :])])
            gdn_prepare(nc, C, prm, pT, miscT, qkv, ba, beta, g)
        with ExitStack() as c2:
            W = {"qkv": qkv, "beta": beta, "g": g, "o_raw": o_raw}
            for k, n in enumerate(("qt", "kt", "vt", "gb", "DT", "DN", "EG", "L")):
                W[n] = C["merged"][:, k, :].rearrange("p (h c) -> p h c", h=H)
            for n in ("AT", "Tm", "U", "Q", "u", "wT", "kd", "vb", "kbe", "qd", "vn", "St"):
                W[n] = c2.enter_context(sbuf(nc, "gdn_" + n, [P, H, P], F32))
            W["B"] = c2.enter_context(sbuf(nc, "gdn_B", [P, 6, H, P], F32))
            W["sm"] = c2.enter_context(sbuf(nc, "gdn_sm", [P, 6, 4], F32))
            zero(nc, W["St"][:, :, :])
            with nc.Fori(0, NT) as t:
                jobs, sums = [], []
                for c in range(NSA_CHUNKS // NT):
                    n = (NSA_CHUNKS // NT) * t + c
                    jobs += column_jobs(wd["w_nsa"][l, n], NDK, h_hi, h_lo)
                    sums.append(("store", nsa_rows[bass.ds(n, 1)].rearrange("a p n -> (a p) n")))
                gdn_tile(nc, C, W, t, jobs, sums)
        gated_output(nc, C, o_raw, z[:, :, :], prm["gdn_norm"], o_hi, o_lo)


def nsa_compress(nc, C, prm, l, wd, nsa_rows, early, miscT, gates, vnat, kcT, vc, jobs, sums):
    kT, vT = early[:, 0:NSA_G, :], early[0:NDV, NSA_G:4 * NSA_G, :]
    s = phase(nc, Background.SEMS + ["early", "g0", "g1", "trg", "gate", "gate2", "tr0", "tr1", "v0", "v1", "xk", "xv", "wk0", "wk1", "wv0", "wv1", "usedk0",
                   "usedk1", "usedv0", "usedv1", "hk", "hv", "hid", "kc", "vc", "kcs"])
    ps = C["ps"]
    bg = Background(C, s, jobs, sums, ps[6])
    LB = 8
    NB = CMP_LEN // LB
    with ExitStack() as ctx:
        sb = lambda n, shape: ctx.enter_context(sbuf(nc, n, shape, F32))
        xk = sb("cmp_xk", [NDK, CMP_LEN, NSA_G, NCMP])
        xv = sb("cmp_xv", [NDV, CMP_LEN, NSA_G, NCMP])
        wk = sb("cmp_wk", [NDK, 2, LB, CMP_HID])
        wv = sb("cmp_wv", [NDV, 2, LB, CMP_HID])
        hk = sb("cmp_hk", [P, 2, NSA_G * NCMP])
        hv = sb("cmp_hv", [P, 2, NSA_G * NCMP])
        with nc.Block() as block:
            @block.sync
            def _(e):
                e.dma_start(early[:, :, :], nsa_rows[NSA_LATE:NSA_CHUNKS].rearrange("c p n -> p c n")).then_inc(s["early"], 16)
                bg.load(e, 0)
                bg.load(e, 1)
                for b in range(NB):
                    if b >= 2:
                        for j in range(5 * b - 8, 5 * b - 3):
                            bg.load(e, j)
                        e.wait_ge(s[f"usedk{b % 2}"], b // 2)
                    e.dma_start(wk[:, b % 2, :, :], wd["w_ck"][l, :, b * LB:(b + 1) * LB, :]).then_inc(s[f"wk{b % 2}"], 16)
                    if b >= 2:
                        e.wait_ge(s[f"usedv{b % 2}"], b // 2)
                    e.dma_start(wv[:, b % 2, :, :], wd["w_cv"][l, :, b * LB:(b + 1) * LB, :]).then_inc(s[f"wv{b % 2}"], 16)

            @block.gpsimd
            def _(e):
                for j in range(len(jobs)):
                    bg.lo(e, j)
                    if bg.sums[bg.sum_of[j]][0] == "branch":
                        bg.add(e, bg.sum_of[j])

            @block.tensor
            def _(e):
                for t in range(NT):
                    ins = e.transpose(ps[7][:, t * P:t * P + 80], miscT[:, t * P:(t + 1) * P], C["ident"][0:80, 0:80])
                ins.then_inc(s["trg"], 1)
                e.wait_ge(s["early"], 16)
                for b in range(2):
                    for g in range(NSA_G):
                        for t in range(NT):
                            n = g * NT + t
                            ins = e.transpose(ps[4 + b][:, n * NDV:(n + 1) * NDV], vT[:, 2 * (b + 1) + g, t * P:(t + 1) * P],
                                              C["ident"][0:NDV, 0:NDV])
                    ins.then_inc(s[f"tr{b}"], 1)
                bg.mm(e, 0)
                e.wait_ge(s["xk"], NSA_G)
                e.wait_ge(s["xv"], NSA_G)
                for b in range(NB):
                    e.wait_ge(s[f"wk{b % 2}"], 16 * (b // 2 + 1))
                    for j in range(LB):
                        p = b * LB + j
                        for c in range(2):
                            ins = e.matmul(ps[c][:, 0:NSA_G * NCMP], wk[:, b % 2, j, c * P:(c + 1) * P],
                                           xk[:, p, :, :].rearrange("p g n -> p (g n)"), start=(p == 0), stop=(p == CMP_LEN - 1))
                    ins.then_inc(s[f"usedk{b % 2}"], 1)
                    bg.mm(e, 3 * b + 1)
                    e.wait_ge(s[f"wv{b % 2}"], 16 * (b // 2 + 1))
                    for j in range(LB):
                        p = b * LB + j
                        for c in range(2):
                            ins = e.matmul(ps[2 + c][:, 0:NSA_G * NCMP], wv[:, b % 2, j, c * P:(c + 1) * P],
                                           xv[:, p, :, :].rearrange("p g n -> p (g n)"), start=(p == 0), stop=(p == CMP_LEN - 1))
                    ins.then_inc(s[f"usedv{b % 2}"], 1)
                    bg.mm(e, 3 * b + 2)
                    if b + 1 < NB:
                        bg.mm(e, 3 * b + 3)
                e.wait_ge(s["hid"], 4)
                e.wait_ge(s["kcs"], 2)
                for c in range(2):
                    ins = e.matmul(ps[4][0:NDK, 0:NSA_G * NCMP], prm["w2k"][:, c * NDK:(c + 1) * NDK], hk[:, c, :],
                                   start=(c == 0), stop=(c == 1))
                ins.then_inc(s["kc"], 1)
                for g in range(NSA_G):
                    for c in range(2):
                        ins = e.matmul(ps[5][0:NCMP, g * NDV:(g + 1) * NDV], hv[:, c, g * NCMP:(g + 1) * NCMP],
                                       prm["w2v"][:, c * NDV:(c + 1) * NDV], start=(c == 0), stop=(c == 1))
                ins.then_inc(s["vc"], 1)

            @block.scalar
            def _(e):
                e.wait_ge(s["trg"], 1)
                e.activation(gates[:, :, :], ps[7][:, :].rearrange("p (t c) -> p t c", t=NT)[:, :, 32:56], ACT.Tanh,
                             scale=0.5).then_inc(s["gate"], 1)
                bg.hi(e, 0)
                bg.hi(e, 1)
                for b in range(2):
                    e.wait_ge(s[f"tr{b}"], 1)
                    e.copy(vnat[:, b, :, :, :], ps[4 + b][:, :].rearrange("p (g t d) -> p g t d", g=NSA_G, t=NT)).then_inc(s["kcs"], 1)
                for j in range(2, len(jobs)):
                    bg.hi(e, j)
                    if jobs[j - 1][6]:
                        bg.out(e, bg.sum_of[j - 1])
                e.wait_ge(s["usedk1"], NB // 2)
                for c in range(2):
                    e.activation(hk[:, c, :], ps[c][:, 0:NSA_G * NCMP], ACT.Gelu_apprx_tanh).then_inc(s["hid"], 1)
                e.wait_ge(s["usedv1"], NB // 2)
                for c in range(2):
                    e.activation(hv[:, c, :], ps[2 + c][:, 0:NSA_G * NCMP], ACT.Gelu_apprx_tanh).then_inc(s["hid"], 1)
                e.wait_ge(s["kc"], 1)
                e.copy(kcT[:, :, :], ps[4][0:NDK, 0:NSA_G * NCMP].rearrange("p (g n) -> p g n", g=NSA_G))
                e.wait_ge(s["vc"], 1)
                e.copy(vc[:, :, :], ps[5][0:NCMP, 0:NSA_G * NDV].rearrange("p (g d) -> p g d", g=NSA_G))

            @block.vector
            def _(e):
                def blocks(x, pe, out, sem):
                    for g in range(NSA_G):
                        for half in range(2):
                            pos = slice(half * CMP_STRIDE, (half + 1) * CMP_STRIDE)
                            src = x[:, g, half * CMP_STRIDE:half * CMP_STRIDE + NCMP * CMP_STRIDE]
                            ins = e.tensor_tensor(out[:, pos, g, :], src.rearrange("p (n j) -> p j n", j=CMP_STRIDE),
                                                  pe[:, pos].unsqueeze(2).to_broadcast([x.shape[0], CMP_STRIDE, NCMP]), ALU.add)
                        ins.then_inc(s[sem], 1)

                e.wait_ge(s["early"], 16)
                blocks(kT, prm["pe_k"][0:NDK, :], xk, "xk")
                blocks(vT, prm["pe_v"][0:NDV, :], xv, "xv")
                e.wait_ge(s["gate"], 1)
                e.tensor_scalar(gates[:, :, :], gates[:, :, :], 0.5, 0.5, ALU.mult, ALU.add).then_inc(s["gate2"], 1)
                e.wait_ge(s["gate2"], 1)
                cg = gates[:, 0, :].rearrange("p (h b) -> p h b", b=3)[:, :, 0]
                e.tensor_scalar(cg, cg, C["cmp_valid"], None, ALU.mult)
                for n in bg.branches:
                    bg.product(e, n)
    retire(nc, s)


def nsa_heads(nc, C, W, grp, pr, jobs, sums):
    s = phase(nc, Background.SEMS + ["q", "v", "vcs", "bias", "gst", "sc", "scw", "scc", "lg", "lgw", "mx", "ex", "rc", "rg", "pn", "tr",
                   "pts", "ptc", "ptw", "o", "ohi", "olo"])
    ps = C["ps"]
    bg = Background(C, s, jobs, sums, ps[2])
    late, kcT, vnat, vc, gates = (W[n] for n in ("late", "kcT", "vnat", "vc", "gates"))
    qs, vs, vcs, bs, bcs, gs, lg, st, pt = (W[n] for n in ("qs", "vs", "vcs", "bs", "bcs", "gs", "lg", "st", "pt"))
    o_hi, o_lo = W["o_hi"], W["o_lo"]
    head = 4 * grp + 2 * pr
    chunk = 2 * grp + pr
    scale = NDK ** -0.5
    items = [(hh, t) for hh in range(2) for t in range(NT)]
    one = lambda ap, pat, **k: ap.rearrange(pat, **k)
    BR = 3
    with nc.Block() as block:
        @block.gpsimd
        def _(e):
            e.tensor_copy(vs[:, :, :, :], vnat[:, :, bass.ds(grp, 1), :, :].rearrange("p b a t d -> p b (a t) d")).then_inc(s["v"], 1)
            e.tensor_copy(vcs[:, :], vc[:, bass.ds(grp, 1), :].rearrange("p a d -> p (a d)")).then_inc(s["vcs"], 1)
            for j in range(len(jobs)):
                bg.lo(e, j)
            for n in bg.branches:
                bg.add(e, n)

        @block.sync
        def _(e):
            e.dma_start(bs[:, :, :], W["bias"][bass.ds(chunk, 1)].rearrange("a p h n -> (a p) h n")).then_inc(s["bias"], 16)
            e.dma_start(bcs[:, :, :], W["biasc"][bass.ds(chunk, 1)].rearrange("a p h n -> (a p) h n")).then_inc(s["bias"], 16)
            bg.loads(e)

        @block.tensor
        def _(e):
            def scores(i):
                hh, t = items[i]
                w = (t + 1) * P
                if i == 0:
                    e.wait_ge(s["q"], 1)
                lhs = qs[:, hh, t * P:(t + 1) * P]
                if i:
                    e.wait_ge(s["lg"], BR * (i - 1) + 1)
                if i >= 2:
                    e.wait_ge(s["ptc"], i - 1)
                e.matmul(ps[5][:, P:P + NCMP], lhs, kcT[:, bass.ds(grp, 1), :].rearrange("p a n -> p (a n)"),
                         start=True, stop=True).then_inc(s["sc"], 1)
                for b in range(2):
                    if i:
                        e.wait_ge(s["lg"], BR * (i - 1) + b + 2)
                    k = late[:, bass.ds(grp + (NSA_H + NSA_G * b), 1), 0:w].rearrange("p a n -> p (a n)")
                    e.matmul(ps[b][:, 0:w], lhs, k, start=True, stop=True).then_inc(s["sc"], 1)
            def values(i):
                hh, t = items[i]
                w = (t + 1) * P
                for b in (1, 2, 0):
                    e.wait_ge(s["pn"], BR * i + b + 1)
                    if i:
                        e.wait_ge(s[("ptc", "pts", "ptw")[b]], i)
                    if b:
                        for j in range(t + 1):
                            ins = e.transpose(ps[2 + b][:, j * P:(j + 1) * P], lg[:, i % 2, b, j * P:(j + 1) * P], C["ident"])
                    else:
                        if i + 1 < len(items):
                            e.wait_ge(s["lg"], BR * (i + 1) + 1)
                        ins = e.transpose(ps[5][0:NCMP, 0:P], lg[:, i % 2, b, 0:NCMP], C["ident"])
                    ins.then_inc(s["tr"], 1)
                if i == 0:
                    e.wait_ge(s["v"], 1)
                    e.wait_ge(s["vcs"], 1)
                if i >= 2:
                    e.wait_ge(s["olo"], i - 1)
                out = ps[6 + i % 2][hh * NDV:(hh + 1) * NDV, 0:P]
                e.wait_ge(s["pts"], i + 1)
                for j in range(t + 1):
                    e.matmul(out, vs[:, 0, j, :], pt[:, 0, j * P:(j + 1) * P], start=(j == 0), stop=False)
                e.wait_ge(s["ptw"], i + 1)
                for j in range(t + 1):
                    e.matmul(out, vs[:, 1, j, :], pt[:, 1, j * P:(j + 1) * P], start=False, stop=False)
                e.wait_ge(s["ptc"], i + 1)
                e.matmul(out, vcs[:, :], pt[0:NCMP, 2, 0:P], start=False, stop=True).then_inc(s["o"], 1)

            scores(0)
            for i in range(len(items)):
                if i + 1 < len(items):
                    scores(i + 1)
                bg.mm(e, i)
                values(i)
            for j in range(len(items), len(jobs)):
                bg.mm(e, j)

        @block.vector
        def _(e):
            e.tensor_copy(gs[:, :, :], gates[:, :, bass.ds(3 * head, 6)]).then_inc(s["gst"], 1)
            e.wait_ge(s["bias"], 32)
            e.wait_ge(s["gst"], 1)

            def logits(i):
                hh, t = items[i]
                w = (t + 1) * P
                if i >= 2:
                    e.wait_ge(s["tr"], BR * (i - 1))
                for b in range(BR):
                    e.wait_ge(s["sc"], BR * i + b + 1)
                    n = w if b else NCMP
                    bb = bs[:, hh, S - w:S] if b else bcs[:, hh, (NT - 1 - t) * NCMP:(NT - t) * NCMP]
                    sc = ps[b - 1][:, 0:n] if b else ps[5][:, P:P + n]
                    e.scalar_tensor_tensor(out=lg[:, i % 2, b, 0:n], in0=sc, scalar=scale, in1=bb,
                                           op0=ALU.mult, op1=ALU.add).then_inc(s["lg"], 1)
                for b in range(BR):
                    n = w if b else NCMP
                    e.wait_ge(s["lg"], BR * i + b + 1)
                    e.tensor_reduce(st[:, i % 2, b:b + 1], lg[:, i % 2, b, 0:n], AX, ALU.max, negate=True).then_inc(s["mx"], 1)

            def normalise(i):
                hh, t = items[i]
                w = (t + 1) * P
                e.wait_ge(s["ex"], BR * (i + 1))
                e.reciprocal(st[:, i % 2, 8:11], st[:, i % 2, 4:7]).then_inc(s["rc"], 1)
                e.wait_ge(s["rc"], i + 1)
                e.tensor_tensor(st[:, i % 2, 12:15], st[:, i % 2, 8:11], gs[:, t, 3 * hh:3 * hh + 3], ALU.mult).then_inc(s["rg"], 1)
                e.wait_ge(s["rg"], i + 1)
                for b in range(BR):
                    n = w if b else NCMP
                    e.tensor_scalar(lg[:, i % 2, b, 0:n], lg[:, i % 2, b, 0:n], st[:, i % 2, 12 + b:13 + b], None, ALU.mult).then_inc(s["pn"], 1)

            def window_probs(i):
                hh, t = items[i]
                w = (t + 1) * P
                e.wait_ge(s["tr"], BR * i + 2)
                if i:
                    e.wait_ge(s["o"], i)
                e.tensor_copy(pt[:, 1, 0:w], ps[4][:, 0:w]).then_inc(s["ptw"], 1)

            def out_lo(i):
                hh, t = items[i]
                rows = slice(hh * NDV, (hh + 1) * NDV)
                e.wait_ge(s["ohi"], i + 1)
                dst = bass.ds(chunk, 1)
                e.tensor_tensor(o_lo[rows, dst, t * P:(t + 1) * P].rearrange("p a n -> p (a n)"), ps[6 + i % 2][rows, 0:P],
                                o_hi[rows, dst, t * P:(t + 1) * P].rearrange("p a n -> p (a n)").bitcast(F32), ALU.subtract).then_inc(s["olo"], 1)

            logits(0)
            for i in range(len(items)):
                normalise(i)
                if i + 1 < len(items):
                    logits(i + 1)
                window_probs(i)
                if i:
                    out_lo(i - 1)
            out_lo(len(items) - 1)
            for n in bg.branches:
                bg.product(e, n)

        @block.scalar
        def _(e):
            e.copy(qs[:, :, :], late[:, bass.ds(head, 2), :]).then_inc(s["q"], 1)
            bg.hi(e, 0)
            bg.hi(e, 1)

            def exps(i):
                hh, t = items[i]
                w = (t + 1) * P
                for b in range(BR):
                    n = w if b else NCMP
                    e.wait_ge(s["mx"], BR * i + b + 1)
                    e.activation(lg[:, i % 2, b, 0:n], lg[:, i % 2, b, 0:n], ACT.Exp, bias=st[:, i % 2, b:b + 1],
                                 accum_out=st[:, i % 2, 4 + b:5 + b]).then_inc(s["ex"], 1)

            def probs(i):
                hh, t = items[i]
                w = (t + 1) * P
                e.wait_ge(s["tr"], BR * i + 1)
                if i:
                    e.wait_ge(s["o"], i)
                e.copy(pt[:, 0, 0:w], ps[3][:, 0:w]).then_inc(s["pts"], 1)
                e.wait_ge(s["tr"], BR * i + 3)
                e.copy(pt[0:NCMP, 2, 0:P], ps[5][0:NCMP, 0:P]).then_inc(s["ptc"], 1)

            def out_hi(i):
                hh, t = items[i]
                rows = slice(hh * NDV, (hh + 1) * NDV)
                e.wait_ge(s["o"], i + 1)
                dst = bass.ds(chunk, 1)
                e.copy(o_hi[rows, dst, t * P:(t + 1) * P].rearrange("p a n -> p (a n)"), ps[6 + i % 2][rows, 0:P]).then_inc(s["ohi"], 1)

            exps(0)
            for i in range(len(items)):
                if i + 1 < len(items):
                    exps(i + 1)
                if i + 2 < len(jobs):
                    bg.hi(e, i + 2)
                if jobs[i][6]:
                    bg.out(e, bg.sum_of[i])
                probs(i)
                out_hi(i)
            bg.stored(e)
    retire(nc, s)


def nsa(nc, C, prm, l, wd, h_hi, h_lo, miscT, nsa_rows, gla_rows, bias, biasc, d_hi, d_lo, o_hi, o_lo):

    def merge(chunk):
        return merge_jobs(wd["w_gate0"][l, chunk], wd["w_branch0"][l, chunk], h_hi, h_lo, d_hi, d_lo, chunk, True)

    with ExitStack() as ctx:
        sb = lambda n, shape: ctx.enter_context(sbuf(nc, n, shape, F32))
        W = {"o_hi": o_hi, "o_lo": o_lo, "bias": bias, "biasc": biasc}
        vnat = W["vnat"] = sb("nsa_vnat", [P, 2, NSA_G, NT, NDV])
        kcT = W["kcT"] = sb("nsa_kcT", [NDK, NSA_G, NCMP])
        vc = W["vc"] = sb("nsa_vc", [NCMP, NSA_G, NDV])
        gates = W["gates"] = sb("nsa_gates", [P, NT, 3 * NSA_H])
        with ExitStack() as c2:
            early = c2.enter_context(sbuf(nc, "nsa_early", [NDK, NSA_CHUNKS - NSA_LATE, S], F32))
            jobs, sums = [], []
            for c in range(4):
                j, m = merge(4 + c)
                jobs, sums = jobs + j, sums + m
            nsa_compress(nc, C, prm, l, wd, nsa_rows, early, miscT, gates, vnat, kcT, vc, jobs, sums)
        with ExitStack() as c2:
            late = W["late"] = c2.enter_context(sbuf(nc, "nsa_late", [NDK, NSA_LATE, S], F32))
            load(nc, late[:, :, :], nsa_rows[0:NSA_LATE].rearrange("c p n -> p c n"))
            for n, shape in (("qs", [NDK, 2, S]), ("vs", [P, 2, NT, NDV]), ("vcs", [NCMP, NDV]), ("bs", [P, 2, S]),
                             ("bcs", [P, 2, NT * NCMP]), ("gs", [P, NT, 6]), ("lg", [P, 2, 3, S]), ("st", [P, 2, 16]),
                             ("pt", [P, 3, S])):
                W[n] = c2.enter_context(sbuf(nc, "nsa_" + n, shape, F32))
            with nc.Fori(0, NSA_G) as grp:
                with nc.Fori(0, 2) as pr:
                    jobs, sums = [], []
                    for c in range(3):
                        n = 6 * grp + 3 * pr + c
                        jobs += column_jobs(wd["w_gla"][l, n], P, h_hi, h_lo)
                        sums.append(("store", gla_rows[bass.ds(n, 1)].rearrange("a p n -> (a p) n")))
                    j, m = merge(2 * grp + pr)
                    nsa_heads(nc, C, W, grp, pr, jobs + j, sums + m)


def gla_prepare(nc, C, prm, miscT, pT, q1, k1, qd, kd, ebc):
    s = phase(nc, ["lg", "x", "nx", "m", "ex", "ln", "ls", "cs", "d", "e", "q"])
    ps = C["ps"]
    NC_ = S // GLA_C
    with ExitStack() as ctx:
        sb = lambda n: ctx.enter_context(sbuf(nc, n, [P, 2, S], F32))
        x, y = sb("gla_x"), sb("gla_y")
        V = lambda ap: ap.rearrange("p a (n c) -> p (a n) c", c=GLA_C)
        at = lambda ap, i: V(ap)[:, :, i:i + 1].to_broadcast([P, 2 * NC_, GLA_C])
        with nc.Block() as block:
            @block.tensor
            def _(e):
                for c in range(2):
                    ins = e.matmul(ps[c][:, :], prm["gla_w"][64:80, c * P:(c + 1) * P], miscT[64:80, :], start=True, stop=True)
                ins.then_inc(s["lg"], 1)

            @block.vector
            def _(e):
                e.wait_ge(s["lg"], 1)
                for c in range(2):
                    e.tensor_scalar(x[:, c, :], ps[c][:, :], prm["gla_b"][:, c:c + 1], None, ALU.add).then_inc(s["x"], 1)
                e.wait_ge(s["x"], 2)
                e.tensor_scalar(y[:, :, :], x[:, :, :], -1.0, None, ALU.mult).then_inc(s["nx"], 1)
                e.wait_ge(s["nx"], 1)
                e.tensor_tensor(y[:, :, :], y[:, :, :], x[:, :, :], ALU.min).then_inc(s["m"], 1)
                e.wait_ge(s["ln"], 1)
                e.scalar_tensor_tensor(out=x[:, :, :], in0=x[:, :, :], scalar=0.0, in1=y[:, :, :], op0=ALU.min, op1=ALU.subtract).then_inc(s["ls"], 1)
                e.wait_ge(s["ls"], 1)
                e.tensor_scalar(x[:, :, :], x[:, :, :], 1.0 / GLA_TAU, None, ALU.mult).then_inc(s["cs"], 1)
                a, b, n = x, y, 1
                for sh in (1, 2, 4, 8):
                    e.wait_ge(s["cs"], n)
                    e.tensor_tensor(V(b[:, :, :])[:, :, sh:], V(a[:, :, :])[:, :, sh:], V(a[:, :, :])[:, :, :GLA_C - sh], ALU.add).then_inc(s["cs"], 1)
                    e.tensor_copy(V(b[:, :, :])[:, :, :sh], V(a[:, :, :])[:, :, :sh]).then_inc(s["cs"], 1)
                    a, b, n = b, a, n + 2
                e.wait_ge(s["cs"], n)
                bc = x
                e.tensor_tensor(V(q1[:, :, :]), V(bc[:, :, :]), at(bc[:, :, :], 7), ALU.subtract).then_inc(s["d"], 1)
                e.tensor_tensor(V(k1[:, :, :]), at(bc[:, :, :], 7), V(bc[:, :, :]), ALU.subtract).then_inc(s["d"], 1)
                e.tensor_tensor(V(kd[:, :, :]), at(bc[:, :, :], 15), V(bc[:, :, :]), ALU.subtract).then_inc(s["d"], 1)
                e.wait_ge(s["d"], 2)
                e.tensor_scalar(q1[:, :, :], q1[:, :, :], GLA_GUARD, None, ALU.min).then_inc(s["d"], 1)
                e.tensor_scalar(k1[:, :, :], k1[:, :, :], GLA_GUARD, None, ALU.min).then_inc(s["d"], 1)
                sc = (P // 2) ** -0.5
                e.wait_ge(s["e"], 4)
                e.scalar_tensor_tensor(out=q1[:, :, :], in0=pT[:, 0:2, :], scalar=sc, in1=q1[:, :, :], op0=ALU.mult, op1=ALU.mult)
                e.tensor_tensor(k1[:, :, :], pT[:, 2:4, :], k1[:, :, :], ALU.mult)
                e.tensor_tensor(kd[:, :, :], pT[:, 2:4, :], kd[:, :, :], ALU.mult)
                e.scalar_tensor_tensor(out=qd[:, :, :], in0=pT[:, 0:2, :], scalar=sc, in1=ebc[:, :, :], op0=ALU.mult, op1=ALU.mult)

            @block.scalar
            def _(e):
                e.wait_ge(s["m"], 1)
                e.activation(y[:, :, :], y[:, :, :], ACT.Exp).then_inc(s["ex"], 1)
                e.wait_ge(s["ex"], 1)
                e.activation(y[:, :, :], y[:, :, :], ACT.Ln, bias=C["one"]).then_inc(s["ln"], 1)
                e.wait_ge(s["cs"], 9)
                e.activation(ebc[:, :, :], x[:, :, :], ACT.Exp).then_inc(s["e"], 1)
                e.wait_ge(s["d"], 5)
                e.activation(kd[:, :, :], kd[:, :, :], ACT.Exp).then_inc(s["e"], 1)
                e.activation(q1[:, :, :], q1[:, :, :], ACT.Exp).then_inc(s["e"], 1)
                e.activation(k1[:, :, :], k1[:, :, :], ACT.Exp).then_inc(s["e"], 1)
    retire(nc, s)


def gla_tile(nc, C, W, t, jobs, sums):
    s = phase(nc, Background.SEMS + ["k1", "kd", "vt", "qd", "eb", "trk", "trv", "kn", "vn", "at", "ats", "kv", "S", "o", "carry", "os", "q1"])
    ps = C["ps"]
    H = GLA_H
    cols = bass.ts(t, P)
    HB = lambda ap: ap.rearrange("p (h c) -> p h c", c=P)
    k1t, q1t, kdt, qdt, vt, ebt, kn, vn, at, SS = (W[n] for n in ("k1t", "q1t", "kdt", "qdt", "vt", "ebt", "kn", "vn", "at", "SS"))
    bg = Background(C, s, jobs, sums, ps[7])
    kv_bank = [ps[4], ps[5], ps[6], ps[0]]
    NCH = P // GLA_C
    half = lambda h: slice((h % 2) * 64, (h % 2) * 64 + 64)
    with nc.Block() as block:
        @block.sync
        def _(e):
            bg.loads(e)

        @block.gpsimd
        def _(e):
            for j in range(len(jobs)):
                bg.lo(e, j)
                if bg.sums[bg.sum_of[j]][0] == "branch":
                    bg.add(e, bg.sum_of[j])

        @block.vector
        def _(e):
            e.tensor_copy(q1t[:, :, :], W["q1"][:, :, cols]).then_inc(s["q1"], 1)
            e.tensor_copy(qdt[:, :, :], W["qd"][:, :, cols]).then_inc(s["qd"], 1)
            e.tensor_copy(ebt[:, :, :], W["ebc"][:, :, cols]).then_inc(s["eb"], 1)
            e.wait_ge(s["trk"], 1)
            for par in range(2):
                e.tensor_scalar(kn[:, par, :], ps[0][:, 0:2 * P], C["parity"][:, par:par + 1], None, ALU.mult).then_inc(s["kn"], 1)
            e.wait_ge(s["at"], 1)
            for par in range(2):
                e.tensor_tensor(at[:, par, :, :], HB(ps[2 + par][:, 0:2 * P]), C["tri16"].unsqueeze(1).to_broadcast([P, 2, P]),
                                ALU.mult).then_inc(s["ats"], 1)
            e.wait_ge(s["eb"], 1)
            for c in range(NCH):
                if c == 4:
                    bg.product(e, bg.branches[0])
                e.wait_ge(s["kv"], 2 * (c // 2) + 2)
                if c:
                    e.wait_ge(s["S"], 2 * c)
                for p in range(2):
                    last = (c + 1) * GLA_C - 1
                    e.scalar_tensor_tensor(out=SS[:, c + 1, p, :], in0=SS[:, c, p, :], scalar=ebt[:, p, last:last + 1],
                                           in1=kv_bank[c // 2][:, (2 * (c % 2) + p) * P:(2 * (c % 2) + p + 1) * P],
                                           op0=ALU.mult, op1=ALU.add).then_inc(s["S"], 1)
            e.wait_ge(s["S"], 2 * NCH)
            e.wait_ge(s["o"], 1)
            e.tensor_copy(SS[:, 0, :, :], SS[:, NCH, :, :]).then_inc(s["carry"], 1)
            bg.product(e, bg.branches[1])

        @block.scalar
        def _(e):
            e.copy(kdt[:, :, :], W["kd"][:, :, cols]).then_inc(s["kd"], 1)
            e.copy(vt[:, :, :], W["pT"][:, 4:8, cols]).then_inc(s["vt"], 1)
            e.copy(k1t[:, :, :], W["k1"][:, :, cols]).then_inc(s["k1"], 1)
            bg.hi(e, 0)
            bg.hi(e, 1)
            e.wait_ge(s["trv"], 1)
            e.copy(vn[:, :, :], HB(ps[1][:, :])).then_inc(s["vn"], 1)
            for j in range(2, len(jobs)):
                bg.hi(e, j)
                if jobs[j - 1][6]:
                    bg.out(e, bg.sum_of[j - 1])
            e.wait_ge(s["o"], 1)
            for par in range(2):
                e.copy(W["o_raw"][:, :, cols].rearrange("p (a b) n -> p b a n", b=2)[:, par, :, :], HB(ps[2 + par][:, 0:2 * P])).then_inc(s["os"], 1)

        @block.tensor
        def _(e):
            e.wait_ge(s["kd"], 1)
            for p in range(2):
                ins = e.transpose(ps[0][:, p * P:(p + 1) * P], kdt[:, p, :], C["ident"])
            ins.then_inc(s["trk"], 1)
            e.wait_ge(s["vt"], 1)
            for h in range(H):
                ins = e.transpose(HB(ps[1][:, :])[:, h, :], vt[:, h, :], C["ident"])
            ins.then_inc(s["trv"], 1)
            e.wait_ge(s["k1"], 1)
            e.wait_ge(s["q1"], 1)
            for h in range(H):
                ins = e.matmul(HB(ps[2 + h % 2][:, :])[:, h // 2, :], k1t[half(h), h // 2, :], q1t[half(h), h // 2, :], start=True, stop=True)
            ins.then_inc(s["at"], 1)
            bg.mm(e, 0)
            e.wait_ge(s["kn"], 2)
            e.wait_ge(s["vn"], 1)
            for c in range(NCH):
                rows = slice(32 * (c // 2), 32 * (c // 2) + 32)
                for h in range(H):
                    col = (2 * (c % 2) + h // 2) * P
                    ins = e.matmul(kv_bank[c // 2][half(h), col:col + P], kn[rows, c % 2, h * 64:(h + 1) * 64], vn[rows, h, :],
                                   start=True, stop=True)
                ins.then_inc(s["kv"], 1)
            for j in range(1, 5):
                bg.mm(e, j)
            e.wait_ge(s["ats"], 2)
            e.wait_ge(s["qd"], 1)
            e.wait_ge(s["S"], 2 * NCH - 2)
            for h in range(H):
                out = HB(ps[2 + h % 2][:, :])[:, h // 2, :]
                for c in range(NCH):
                    cc = slice(c * GLA_C, (c + 1) * GLA_C)
                    e.matmul(out[:, cc], SS[half(h), c, h // 2, :], qdt[half(h), h // 2, cc], start=(c == 0), stop=False,
                             skip_group_check=True)
                ins = e.matmul(out, vn[:, h, :], at[:, h % 2, h // 2, :], start=False, stop=True, skip_group_check=True)
            ins.then_inc(s["o"], 1)
            bg.mm(e, 5)
    retire(nc, s)


def gla(nc, C, prm, l, wd, h_hi, h_lo, miscT, gla_rows, n_hi, n_lo, o_hi, o_lo):
    with ExitStack() as ctx:
        sb = lambda n, shape: ctx.enter_context(sbuf(nc, n, shape, F32))
        W = {}
        pT = W["pT"] = sb("gla_pT", [P, 12, S])
        o_raw = W["o_raw"] = sb("gla_o", [P, GLA_H, S])
        load(nc, pT[:, :, :], gla_rows.rearrange("c p n -> p c n"))
        with ExitStack() as c2:
            for n, shape in (("q1", [P, 2, S]), ("k1", [P, 2, S]), ("qd", [P, 2, S]), ("kd", [P, 2, S]), ("ebc", [P, 2, S])):
                W[n] = c2.enter_context(sbuf(nc, "gla_" + n, shape, F32))
            gla_prepare(nc, C, prm, miscT, pT, W["q1"], W["k1"], W["qd"], W["kd"], W["ebc"])
            for n, shape in (("k1t", [P, 2, P]), ("q1t", [P, 2, P]), ("kdt", [P, 2, P]), ("qdt", [P, 2, P]), ("vt", [P, 4, P]),
                             ("ebt", [P, 2, P]), ("kn", [P, 2, 2 * P]), ("vn", [P, 4, P]), ("at", [P, 2, 2, P]), ("SS", [P, 9, 2, P])):
                W[n] = c2.enter_context(sbuf(nc, "gla_" + n, shape, F32))
            zero(nc, W["SS"][:, 0, :, :])
            with nc.Fori(0, NT) as t:
                jobs, sums = [], []
                for c in range(2):
                    chunk = 2 * t + c
                    j, m = merge_jobs(wd["w_gate1"][l, chunk], wd["w_branch1"][l, chunk], h_hi, h_lo, n_hi, n_lo, chunk, False)
                    jobs, sums = jobs + j, sums + m
                gla_tile(nc, C, W, t, jobs, sums)
        gated_output(nc, C, o_raw, pT[:, 8:12, :], prm["gla_norm"], o_hi, o_lo)


def position_bias(nc, C, rel_bias, one_hot, scratch, bias_dram, biasc_dram):
    s = phase(nc, ["tb", "mask", "oh", "row", "rows", "st", "ld", "flip", "out"])
    ps = C["ps"]
    with ExitStack() as ctx:
        sb = lambda n, shape: ctx.enter_context(sbuf(nc, n, shape, F32))
        tbl = sb("pb_tbl", [BUCKETS + 1, NSA_H])
        oh = sb("pb_oh", [BUCKETS + 1, RLEN])
        row = sb("pb_row", [NSA_H, RLEN])
        wt = sb("pb_wt", [P, NSA_H, WLEN])
        bias = sb("pb_bias", [P, NSA_H, S])
        biasc = sb("pb_biasc", [P, NSA_H, NT * NCMP])
        with nc.Block() as block:
            @block.sync
            def _(e):
                e.dma_start(tbl[0:BUCKETS, :], rel_bias).then_inc(s["tb"], 16)
                e.dma_start(oh[:, :], one_hot).then_inc(s["oh"], 16)
                e.wait_ge(s["rows"], 2)
                e.dma_start(scratch, row[:, :]).then_inc(s["st"], 16)
                e.wait_ge(s["st"], 16)
                src = bass.AP(scratch.tensor, 0, [[1, P], [RLEN, NSA_H], [1, WLEN]])
                e.dma_start(wt[:, :, :], src).then_inc(s["ld"], 16)
                e.wait_ge(s["out"], 2 * NSA_H)
                e.dma_start(bias_dram.rearrange("c p h n -> p c h n"), bias[:, :, :].rearrange("p (c h) n -> p c h n", h=2)).then_inc(s["st"], 16)
                e.dma_start(biasc_dram.rearrange("c p h n -> p c h n"), biasc[:, :, :].rearrange("p (c h) n -> p c h n", h=2)).then_inc(s["st"], 16)
                e.wait_ge(s["st"], 48)

            @block.vector
            def _(e):
                e.memset(tbl[BUCKETS:BUCKETS + 1, :], MASKED).then_inc(s["mask"], 1)
                e.wait_ge(s["row"], 2)
                for c in range(2):
                    e.tensor_copy(row[:, c * S:(c + 1) * S], ps[c][0:NSA_H, :]).then_inc(s["rows"], 1)
                for h in range(NSA_H):
                    e.wait_ge(s["flip"], h + 1)
                    e.tensor_copy(bias[:, h, :], ps[2 + 2 * (h % 2)][:, :]).then_inc(s["out"], 1)
                    e.tensor_copy(biasc[:, h, :], ps[3 + 2 * (h % 2)][:, 0:NT * NCMP]).then_inc(s["out"], 1)

            @block.tensor
            def _(e):
                e.wait_ge(s["tb"], 16)
                e.wait_ge(s["mask"], 1)
                e.wait_ge(s["oh"], 16)
                for c in range(2):
                    e.matmul(ps[c][0:NSA_H, :], tbl[:, :], oh[:, c * S:(c + 1) * S], start=True, stop=True).then_inc(s["row"], 1)
                e.wait_ge(s["ld"], 16)
                for h in range(NSA_H):
                    if h >= 2:
                        e.wait_ge(s["out"], 2 * (h - 1))
                    e.matmul(ps[2 + 2 * (h % 2)][:, :], C["anti"], wt[:, h, 0:S], start=True, stop=True)
                    src = wt[:, h, CMP_LEN - 1:CMP_LEN - 1 + NT * P]
                    for q in range(NT):
                        a = CMP_LEN - 1 + q * P
                        ins = e.matmul(ps[3 + 2 * (h % 2)][:, q * NCMP:(q + 1) * NCMP], C["anti"],
                                       wt[:, h, a:a + (NCMP - 1) * CMP_STRIDE + 1:CMP_STRIDE], start=True, stop=True)
                    ins.then_inc(s["flip"], 1)
    retire(nc, s)


def trunk(nc, x_in, rel_bias, consts, one_hot, params, wd, out, scratch):
    with ExitStack() as ctx:
        sb = lambda n, shape: ctx.enter_context(sbuf(nc, n, shape, F32))
        x = sb("x", [P, NT, D])
        cst = sb("consts", [P, CONST_N])
        prm_t = sb("params", [P, PARAM_N])
        bias = nc.dram_tensor("bias", (NSA_H // 2, P, 2, S), F32, kind="Internal").ap()
        biasc = nc.dram_tensor("biasc", (NSA_H // 2, P, 2, NT * NCMP), F32, kind="Internal").ap()
        nsa_rows = nc.dram_tensor("nsa_rows", (NSA_CHUNKS, NDK, S), F32, kind="Internal").ap()
        gla_rows = nc.dram_tensor("gla_rows", (GLA_CHUNKS, P, S), F32, kind="Internal").ap()
        ps = [ctx.enter_context(nc.psum_tensor(f"ps{i}", [P, S], F32)) for i in range(8)]
        C = {n: cst[:, a:b] for n, (a, b) in CONST_COLS.items()}
        C["x"], C["ps"] = x, ps
        s = phase(nc, ["x", "c"])
        with nc.Block() as block:
            @block.sync
            def _(e):
                e.dma_start(x[:, :, :], x_in.rearrange("b (t p) d -> p (b t) d", p=P)).then_inc(s["x"], 16)
                e.dma_start(cst[:, :], consts).then_inc(s["c"], 16)
                e.wait_ge(s["x"], 16)
                e.wait_ge(s["c"], 16)
        retire(nc, s)
        position_bias(nc, C, rel_bias, one_hot, scratch, bias, biasc)

        with nc.Fori(0, DEPTH) as l:
            s = phase(nc, ["p"])
            with nc.Block() as block:
                @block.sync
                def _(e):
                    e.dma_start(prm_t[:, :], params[l]).then_inc(s["p"], 16)
                    e.wait_ge(s["p"], 16)
            retire(nc, s)
            prm = {n: prm_t[:, a:b] for n, (a, b) in PARAM_COLS.items()}
            ffn(nc, C, l, prm["ffn1_pre"], wd["w_gu1"], wd["w_down1"], wd["post1"], )
            with ExitStack() as cm:
                merged = cm.enter_context(sbuf(nc, "merged", [P, KD, S], F32))
                with ExitStack() as ch:
                    h_hi = ch.enter_context(sbuf(nc, "m_h_hi", [P, KD, S], F32R))
                    h_lo = ch.enter_context(sbuf(nc, "m_h_lo", [P, KD, S], F32R))
                    miscT = ch.enter_context(sbuf(nc, "miscT", [80, S], F32))
                    ba = ch.enter_context(sbuf(nc, "misc", [P, NT, 80], F32))
                    o_hi = ch.enter_context(sbuf(nc, "o_hi", [P, 4, S], F32R))
                    o_lo = ch.enter_context(sbuf(nc, "o_lo", [P, 4, S], F32R))
                    C["merged"] = merged
                    C["bg"] = tuple(ch.enter_context(sbuf(nc, n, [P, 2, S], dt)) for n, dt in
                                    (("bg_raw", F32), ("bg_hi", F32R), ("bg_lo", F32R), ("bg_stage", F32))) + tuple(
                        ch.enter_context(sbuf(nc, n, [P, S], F32)) for n in ("bg_sg", "bg_pr"))
                    norm_transpose(nc, C, prm["mix_pre"], h_hi, h_lo)
                    gdn(nc, C, prm, l, wd, h_hi, h_lo, miscT, ba, o_hi, o_lo, nsa_rows)
                    with ExitStack() as cb:
                        n_hi = cb.enter_context(sbuf(nc, "n_hi", [P, 4, S], F32R))
                        n_lo = cb.enter_context(sbuf(nc, "n_lo", [P, 4, S], F32R))
                        nsa(nc, C, prm, l, wd, h_hi, h_lo, miscT, nsa_rows, gla_rows, bias, biasc, o_hi, o_lo, n_hi, n_lo)
                        gla(nc, C, prm, l, wd, h_hi, h_lo, miscT, gla_rows, n_hi, n_lo, o_hi, o_lo)
                    merge_branch(nc, C, l, wd["w_gate2"], wd["w_branch2"], h_hi, h_lo, o_hi, o_lo, merged, False)
                with ExitStack() as ch:
                    g_hi = ch.enter_context(sbuf(nc, "g_hi", [P, KD, S], F32R))
                    g_lo = ch.enter_context(sbuf(nc, "g_lo", [P, KD, S], F32R))
                    yT = ch.enter_context(sbuf(nc, "m_yT", [P, KD, S], F32))
                    split_rows(nc, merged, g_hi, g_lo)
                    contract(nc, C, l, wd["w_out"], KD, g_hi, g_lo, yT)
                    residual(nc, C, l, yT, wd["mix_post"], 1.0)
            ffn(nc, C, l, prm["ffn2_pre"], wd["w_gu2"], wd["w_down2"], wd["post2"])

        s = phase(nc, ["out"])
        with nc.Block() as block:
            @block.sync
            def _(e):
                e.dma_start(out.rearrange("b (t p) d -> p (b t) d", p=P), x[:, :, :]).then_inc(s["out"], 16)
                e.wait_ge(s["out"], 16)


def split_rows(nc, src, hi, lo):
    s = phase(nc, ["hi"])
    with nc.Block() as block:
        @block.scalar
        def _(e):
            for k in range(KD):
                e.mul(hi[:, k, :], src[:, k, :], 0.5).then_inc(s["hi"], 1)

        @block.vector
        def _(e):
            for k in range(KD):
                e.wait_ge(s["hi"], k + 1)
                e.scalar_tensor_tensor(out=lo[:, k, :], in0=src[:, k, :], scalar=0.5, in1=hi[:, k, :].bitcast(F32),
                                       op0=ALU.mult, op1=ALU.subtract)
    retire(nc, s)


def constants():
    import numpy as np
    c = np.zeros((P, CONST_N), np.float32)
    i, j = np.arange(P)[:, None], np.arange(P)[None, :]

    def put(name, v):
        a, b = CONST_COLS[name]
        c[:, a:b] = v

    put("ident", i == j)
    put("ones", 1.0)
    put("anti", i + j == P - 1)
    same64 = i // GDN_C == j // GDN_C
    put("tri64", (i <= j) & same64)
    put("blk64", same64)
    lv = [((i // (2 * b) == j // (2 * b)) & (i % (2 * b) >= b) & (j % (2 * b) < b)) for b in (1, 2, 4, 8, 16, 32)]
    put("lvl", np.concatenate(lv, 1))
    put("tri16", (i <= j) & (i // GLA_C == j // GLA_C))
    put("parity", np.concatenate([(i // GLA_C) % 2 == 0, (i // GLA_C) % 2 == 1], 1))
    put("cmp_valid", i >= CMP_LEN - 1)
    put("eps", EPS)
    put("gdn_eps", EPS)
    put("one", 1.0)
    put("lnq", 0.0)
    dist = S - 1 - np.arange(RLEN)
    n = np.maximum(dist, 0)
    exact = BUCKETS // 2
    large = exact + (np.log(np.maximum(n, 1).astype(np.float64) / exact) / np.log(128 / exact) * (BUCKETS - exact) + 1e-9).astype(np.int64)
    bucket = np.where(n < exact, n, np.minimum(large, BUCKETS - 1))
    oh = np.zeros((BUCKETS + 1, RLEN), np.float32)
    oh[bucket, np.arange(RLEN)] = dist >= 0
    oh[BUCKETS] = dist < 0
    return c, oh


def kernel(**inputs):
    import numpy as np
    import concourse.bacc as bacc
    from concourse import mybir as mb
    from concourse.bass_utils import run_bass_kernel_spmd as run

    a = {k: np.asarray(v) for k, v in inputs.items()}
    L = DEPTH
    c, oh = constants()

    def tiles(w, width):
        k, n = w.shape[1] // P, w.shape[2] // width
        return w.reshape(L, k, P, n, width).transpose(0, 3, 2, 1, 4).reshape(L, n, P, k * width)

    arrays = {"x": a["x"], "rel_bias": a["rel_bias"], "consts": c, "one_hot": oh}
    for f in ("1", "2"):
        gu = a[f"ffn{f}_w_gate_up"]
        g, u = tiles(gu[:, :, :FF], P), tiles(gu[:, :, FF:], P)
        arrays["w_gu" + f] = np.stack([g, u], 2)
        arrays["w_down" + f] = a[f"ffn{f}_w_down"].reshape(L, KF // 2, 2, P, D)
        arrays["post" + f] = a[f"ffn{f}_norm_post"].reshape(L, 1, D)
    arrays["w_out"] = a["w_out"].reshape(L, KD // 2, 2, P, D)
    arrays["mix_post"] = a["mix_norm_post"].reshape(L, 1, D)
    wi = a["w_in"]
    at = 0

    def take(n):
        nonlocal at
        at += n
        return wi[:, :, at - n:at]

    arrays["w_gdn"] = tiles(take(2048), P)
    w_ba = take(8)
    nq = take(NSA_H * NDK).reshape(L, D, NSA_H, NDK)
    kv = take(3 * NSA_G * (NDK + NDV)).reshape(L, D, 3 * NSA_G, NDK + NDV)
    nk, nv = kv[..., :NDK], np.zeros((L, D, 3 * NSA_G, NDK), np.float32)
    nv[..., :NDV] = kv[..., NDK:]
    arrays["w_nsa"] = tiles(np.concatenate([nq, nk[:, :, NSA_G:], nk[:, :, :NSA_G], nv], 2).reshape(L, D, -1), NDK)
    w_ng = take(3 * NSA_H)
    arrays["w_gla"] = tiles(take(1536), P)
    w_ga = take(16)
    misc = np.zeros((L, D, 80), np.float32)
    misc[:, :, 0:8], misc[:, :, 32:56], misc[:, :, 64:80] = w_ba, w_ng, w_ga
    arrays["w_misc"] = tiles(misc, 80)[:, 0]
    for b, name in enumerate(("gdn", "nsa", "gla")):
        arrays[f"w_gate{b}"] = tiles(take(D), P)
        arrays[f"w_branch{b}"] = tiles(a[f"w_branch_{name}"], P)
    arrays["w_ck"] = a["nsa_cmp_k_w1"].reshape(L, CMP_LEN, NDK, CMP_HID).transpose(0, 2, 1, 3)
    arrays["w_cv"] = a["nsa_cmp_v_w1"].reshape(L, CMP_LEN, NDV, CMP_HID).transpose(0, 2, 1, 3)

    prm = np.zeros((L, P, PARAM_N), np.float32)

    def put(name, v, rows=slice(0, P)):
        lo, hi = PARAM_COLS[name]
        prm[:, rows, lo:hi] = v

    for name, key in (("ffn1_pre", "ffn1_norm_pre"), ("mix_pre", "mix_norm_pre"), ("ffn2_pre", "ffn2_norm_pre")):
        put(name, a[key].reshape(L, KD, P).transpose(0, 2, 1))
    put("conv", a["gdn_conv_w"].reshape(L, 4, 12, P).transpose(0, 3, 1, 2).reshape(L, P, 48))
    put("gdn_norm", a["gdn_norm_w"].reshape(L, P, 1))
    put("gla_norm", a["gla_norm_w"].reshape(L, P, 1))
    put("gla_b", a["gla_gate_b"].reshape(L, 2, P).transpose(0, 2, 1))
    put("pe_k", a["nsa_pe_k"].transpose(0, 2, 1), slice(0, NDK))
    put("pe_v", a["nsa_pe_v"].transpose(0, 2, 1), slice(0, NDV))
    put("gla_w", a["gla_gate_w"], slice(64, 80))
    put("a_log", a["gdn_a_log"].reshape(L, 1, 4))
    put("dt_bias", a["gdn_dt_bias"].reshape(L, 1, 4))
    put("w2k", a["nsa_cmp_k_w2"].reshape(L, 2, P, NDK).transpose(0, 2, 1, 3).reshape(L, P, -1))
    put("w2v", a["nsa_cmp_v_w2"].reshape(L, 2, P, NDV).transpose(0, 2, 1, 3).reshape(L, P, -1))
    arrays["params"] = prm

    nc = bacc.Bacc("TRN2", target_bir_lowering=False, num_devices=1)
    arrays = {"in_" + k: np.ascontiguousarray(v) for k, v in arrays.items()}
    t = {k[3:]: nc.dram_tensor(k, v.shape, mb.dt.from_np(v.dtype), kind="ExternalInput").ap() for k, v in arrays.items()}
    out = nc.dram_tensor("out", (1, S, D), F32, kind="ExternalOutput").ap()
    scratch = nc.dram_tensor("bias_rows", (NSA_H, RLEN), F32, kind="Internal").ap()
    trunk(nc, t["x"], t["rel_bias"], t["consts"], t["one_hot"], t["params"], t, out, scratch)
    return run(nc, [arrays], core_ids=[0]).results[0]["out"]
```

```python
from contextlib import ExitStack

import concourse.bass as bass
from concourse import mybir

F32 = mybir.dt.float32
F32R = mybir.dt.float32r
ALU = mybir.AluOpType
ACT = mybir.ActivationFunctionType
AX = mybir.AxisListType.X

P = 128
D = 1024
S = 512
DEPTH = 2
FF = 2816
NT = S // P
KD = D // P
KF = FF // P
EPS = 1e-6
MASKED = -1e30

GDN_H = 4
GDN_C = 64
NSA_H = 8
NSA_G = 2
HPG = NSA_H // NSA_G
NDK = 96
NDV = 64
NCMP = 31
CMP_LEN = 32
CMP_STRIDE = 16
CMP_HID = 256
GLA_H = 4
GLA_C = 16
GLA_TAU = 16.0
GLA_GUARD = 40.0
BUCKETS = 32
NSA_LATE = NSA_H + 2 * NSA_G
NSA_CHUNKS = NSA_H + 6 * NSA_G
GLA_CHUNKS = 12
RLEN = 1024
WLEN = RLEN - P

PARAM_COLS = {}
_at = 0
for _name, _n in (("ffn1_pre", KD), ("mix_pre", KD), ("ffn2_pre", KD), ("conv", 48), ("gdn_norm", 1),
                  ("gla_norm", 1), ("gla_b", 2), ("pe_k", CMP_LEN), ("pe_v", CMP_LEN), ("gla_w", 256),
                  ("a_log", 4), ("dt_bias", 4), ("w2k", 2 * NDK), ("w2v", 2 * NDV)):
    PARAM_COLS[_name] = (_at, _at + _n)
    _at += _n
PARAM_N = _at

CONST_COLS = {}
_at = 0
for _name, _n in (("ident", P), ("ones", P), ("anti", P), ("tri64", P), ("blk64", P), ("lvl", 6 * P),
                  ("tri16", P), ("parity", 2), ("cmp_valid", 1), ("eps", 1), ("gdn_eps", 1), ("one", 1),
                  ("lnq", 1)):
    CONST_COLS[_name] = (_at, _at + _n)
    _at += _n
CONST_N = _at


def sbuf(nc, name, shape, dtype):
    return nc.sbuf_tensor(f"{name}_{nc.next_id()}", shape, dtype)


def phase(nc, names):
    return {n: nc.alloc_semaphore(name=f"{n}_{nc.next_id()}") for n in names}


def retire(nc, sems):
    nums = sorted(s.num for s in sems.values())
    first = nums[0]
    for a, b in zip(nums, nums[1:] + [None]):
        if b != a + 1:
            nc.sync.sem_clear(range(first, a + 1))
            first = b
    nc.all_engine_barrier()
    for s in sems.values():
        nc.release_semaphore(s)


def load(nc, out, in_):
    s = phase(nc, ["load"])
    with nc.Block() as block:
        @block.sync
        def _(e):
            e.dma_start(out, in_).then_inc(s["load"], 16)
            e.wait_ge(s["load"], 16)
    retire(nc, s)


def zero(nc, ap):
    with nc.Block() as block:
        @block.vector
        def _(e):
            e.memset(ap, 0.0)


def mm3(e, out, w_hi, w_lo, m_hi, m_lo, start, stop):
    e.matmul(out, w_hi, m_hi, start=start, stop=False, skip_group_check=True)
    e.matmul(out, w_lo, m_hi, start=False, stop=False, skip_group_check=True)
    return e.matmul(out, w_hi, m_lo, start=False, stop=stop, skip_group_check=True)


HALF = 4
NSA_FIRST = 4
STREAM = []
FIRST_JOB = {}


def _stream():
    column = lambda kind, n: [(kind, n, i) for i in range(2)]
    gate = lambda b, chunk: [("gate", (b, chunk), i) for i in range(2)]
    merge = lambda b, chunk: gate(b, chunk) + [("branch", (b, chunk), 0)]
    heads = [j for half in range(4) for j in
             [x for c in range(3) for x in column("gla", 3 * half + c)] + merge(0, half)]
    for name, jobs in (("gdn_prepare", [x for n in range(NSA_FIRST) for x in column("nsa", n)] +
                        [x for c in range(3) for x in gate(2, c)]),
                       ("gdn", [x for n in range(NSA_FIRST, NSA_CHUNKS) for x in column("nsa", n)]),
                       ("gdn_out", gate(2, 3)),
                       ("compress", [x for c in range(4, KD) for x in merge(0, c)]),
                       ("heads", heads),
                       ("gla_prepare", [x for c in range(4, KD) for x in gate(2, c)]),
                       ("gla", [x for c in range(KD) for x in merge(1, c)]),
                       ("last", [("branch", (2, c), 0) for c in range(KD)])):
        FIRST_JOB[name] = len(STREAM)
        STREAM.extend(jobs)


_stream()
STREAM_N = len(STREAM) + 2


class Background:

    SEMS = ["b_raw0", "b_raw1", "b_hi", "b_lo", "b_acc", "b_out", "b_pr", "b_add", "b_st0", "b_st1"]

    def __init__(self, C, s, w_stream, l, first_job, jobs, sums, banks, started=True):
        self.C, self.s, self.jobs, self.sums, self.banks = C, s, jobs, sums, banks
        self.src = lambda j: w_stream[l, first_job + j]
        self.n = len(jobs)
        assert self.n % 2 == 0
        self.loaded, self.split = (2, 1) if started else (0, 0)
        self.raw, self.hi_, self.lo_, self.stage, self.sg, self.pr = C["bg"]
        self.merged = C["merged"]
        self.sum_of, n = [], 0
        for job in jobs:
            self.sum_of.append(n)
            n += job[5]
        self.branches = [n for n, x in enumerate(sums) if x[0] == "branch"]
        self.stores = [n for n, x in enumerate(sums) if x[0] in ("store", "tanh")]

    def width(self, j):
        return HALF * (self.jobs[j][0] if j < self.n else P)

    def load(self, e, j):
        w = self.width(j)
        if j - 1 - self.split > 0:
            e.wait_ge(self.s["b_lo"], j - 1 - self.split)
        e.dma_start(self.raw[:, j % 2, 0:w], self.src(j)[:, 0:w]).then_inc(self.s[f"b_raw{j % 2}"], 16)

    def loads(self, e):
        for j in range(self.loaded, self.n + 2):
            self.load(e, j)
        self.loads_done(e)

    def loads_done(self, e):
        slot = (self.n + 1) % 2
        if n := (self.n + 1) // 2 + 1 - self.loaded // 2:
            e.wait_ge(self.s[f"b_raw{slot}"], 16 * n)

    def hi(self, e, j):
        n = self.width(j)
        if j >= self.loaded:
            e.wait_ge(self.s[f"b_raw{j % 2}"], 16 * (j // 2 + 1 - self.loaded // 2))
        if j >= 2:
            e.wait_ge(self.s["b_acc"], j - 1)
        e.copy(self.hi_[:, j % 2, 0:n], self.raw[:, j % 2, 0:n]).then_inc(self.s["b_hi"], 1)

    def lo(self, e, j):
        n = self.width(j)
        e.wait_ge(self.s["b_hi"], j + 1 - self.split)
        e.tensor_tensor(self.lo_[:, j % 2, 0:n], self.raw[:, j % 2, 0:n], self.hi_[:, j % 2, 0:n].bitcast(F32),
                        ALU.subtract).then_inc(self.s["b_lo"], 1)

    def bank(self, n):
        return self.banks[n % len(self.banks)]

    def mm(self, e, j):
        w, m_hi, m_lo, k0, first, last = self.jobs[j]
        if j >= self.split:
            e.wait_ge(self.s["b_lo"], j + 1 - self.split)
        m = self.sum_of[j]
        if first and m >= len(self.banks):
            self._read(e, m - len(self.banks))
        for k in range(HALF):
            ins = mm3(e, self.bank(m)[0:w, :], self.hi_[:, j % 2, k * w:(k + 1) * w], self.lo_[:, j % 2, k * w:(k + 1) * w],
                      m_hi[:, k0 + k, :], m_lo[:, k0 + k, :], first and k == 0, last and k == HALF - 1)
        ins.then_inc(self.s["b_acc"], 1)

    def _read(self, e, n):
        if n in self.branches:
            e.wait_ge(self.s["b_pr"], self.branches.index(n) + 1)
        else:
            e.wait_ge(self.s["b_out"], 1 + len([m for m in range(n) if m not in self.branches]))

    def _sum_ready(self, e, n):
        e.wait_ge(self.s["b_acc"], max(j for j, m in enumerate(self.sum_of) if m == n) + 1)

    def out(self, e, n):
        kind, dst = self.sums[n]
        if kind == "branch":
            return
        self._sum_ready(e, n)
        if kind == "gate":
            done = [b for b in self.branches if b < n]
            if done:
                e.wait_ge(self.s["b_pr"], len(done))
            e.activation(self.sg[:, :], self.bank(n)[:, :], ACT.Tanh, scale=0.5).then_inc(self.s["b_out"], 1)
        else:
            i = self.stores.index(n)
            if i >= 2:
                e.wait_ge(self.s[f"b_st{i % 2}"], 16 * (i // 2))
            w = dst.shape[0]
            if kind == "tanh":
                e.activation(self.stage[0:w, i % 2, :], self.bank(n)[0:w, :], ACT.Tanh, scale=0.5).then_inc(self.s["b_out"], 1)
            else:
                e.copy(self.stage[0:w, i % 2, :], self.bank(n)[0:w, :]).then_inc(self.s["b_out"], 1)
            self._read(e, n)
            e.dma_start(dst, self.stage[0:w, i % 2, :]).then_inc(self.s[f"b_st{i % 2}"], 16)

    def product(self, e, n):
        i = self.branches.index(n)
        self._sum_ready(e, n)
        self._read(e, n - 1)
        if i:
            e.wait_ge(self.s["b_add"], i)
        e.scalar_tensor_tensor(out=self.pr[:, :], in0=self.sg[:, :], scalar=1.0, in1=self.bank(n)[:, :],
                               op0=ALU.add, op1=ALU.mult).then_inc(self.s["b_pr"], 1)

    def add(self, e, n):
        i = self.branches.index(n)
        first, chunk = self.sums[n][1]
        e.wait_ge(self.s["b_pr"], i + 1)
        m = self.merged[:, bass.ds(chunk, 1), :].rearrange("p a n -> p (a n)")
        if first:
            e.tensor_copy(m, self.pr[:, :]).then_inc(self.s["b_add"], 1)
        else:
            e.tensor_tensor(m, m, self.pr[:, :], ALU.add).then_inc(self.s["b_add"], 1)

    def stored(self, e):
        for slot in range(2):
            if n := len(self.stores[slot::2]):
                e.wait_ge(self.s[f"b_st{slot}"], 16 * n)


def column_jobs(w, h_hi, h_lo):
    return [(w, h_hi, h_lo, i * HALF, i == 0, i == 1) for i in range(2)]


def merge_jobs(h_hi, h_lo, o_hi, o_lo, chunk, first):
    jobs = column_jobs(P, h_hi, h_lo) + [(P, o_hi, o_lo, 0, True, True)]
    return jobs, [("gate", None), ("branch", (first, chunk))]


def norm_transpose(nc, C, w_pre, h_hi, h_lo):
    s = phase(nc, ["sq", "ln", "rstd", "xn", "tr", "hi"])
    x, ps = C["x"], C["ps"]
    with ExitStack() as ctx:
        xn = ctx.enter_context(sbuf(nc, "nt_xn", [P, NT, D], F32))
        junk = ctx.enter_context(sbuf(nc, "nt_junk", [P, D], F32))
        ssq = ctx.enter_context(sbuf(nc, "nt_ssq", [P, NT], F32))
        rstd = ctx.enter_context(sbuf(nc, "nt_rstd", [P, NT], F32))
        with nc.Block() as block:
            @block.scalar
            def _(e):
                for t in range(NT):
                    if t:
                        e.wait_ge(s["sq"], t)
                    e.activation(junk[:, :], x[:, t, :], ACT.Square, accum_out=ssq[:, t:t + 1]).then_inc(s["sq"], 1)
                e.wait_ge(s["sq"], NT)
                e.activation(rstd[:, :], ssq[:, :], ACT.Ln, bias=C["eps"], scale=1.0 / D).then_inc(s["ln"], 1)
                e.wait_ge(s["ln"], 1)
                e.activation(rstd[:, :], rstd[:, :], ACT.Exp, scale=-0.5).then_inc(s["rstd"], 1)
                for t in range(NT):
                    for half in range(2):
                        e.wait_ge(s["tr"], 2 * t + half + 1)
                        for b in range(4):
                            k = 4 * half + b
                            ins = e.mul(h_hi[:, k, t * P:(t + 1) * P], ps[2 * t + half][:, b * P:(b + 1) * P], w_pre[:, k:k + 1])
                        ins.then_inc(s["hi"], 1)

            @block.vector
            def _(e):
                e.wait_ge(s["rstd"], 1)
                for t in range(NT):
                    e.tensor_scalar(xn[:, t, :], x[:, t, :], rstd[:, t:t + 1], None, ALU.mult).then_inc(s["xn"], 1)
                for t in range(NT):
                    for half in range(2):
                        e.wait_ge(s["hi"], 2 * t + half + 1)
                        for b in range(4):
                            k = 4 * half + b
                            e.scalar_tensor_tensor(out=h_lo[:, k, t * P:(t + 1) * P], in0=ps[2 * t + half][:, b * P:(b + 1) * P],
                                                   scalar=w_pre[:, k:k + 1], in1=h_hi[:, k, t * P:(t + 1) * P].bitcast(F32),
                                                   op0=ALU.mult, op1=ALU.subtract)

            @block.tensor
            def _(e):
                for t in range(NT):
                    e.wait_ge(s["xn"], t + 1)
                    for half in range(2):
                        for b in range(4):
                            k = 4 * half + b
                            ins = e.transpose(ps[2 * t + half][:, b * P:(b + 1) * P], xn[:, t, k * P:(k + 1) * P], C["ident"])
                        ins.then_inc(s["tr"], 1)
    retire(nc, s)


def weight_buffers(nc, ctx):
    raw = ctx.enter_context(sbuf(nc, "w_raw", [P, 2, D], F32))
    hi = ctx.enter_context(sbuf(nc, "w_hi", [P, 2, D], F32R))
    lo = ctx.enter_context(sbuf(nc, "w_lo", [P, 2, D], F32R))
    return raw, hi, lo


def ffn_gate_up(nc, C, l, w_gu, h_hi, h_lo, a_hi, a_lo):
    s = phase(nc, ["raw0", "raw1", "hi0", "hi1", "lo0", "lo1", "acc0", "acc1", "silu", "act", "ahi", "alo"])
    ps = C["ps"]
    with ExitStack() as ctx:
        raw, hi, lo = weight_buffers(nc, ctx)
        sg = ctx.enter_context(sbuf(nc, "sg", [P, S], F32))
        a32 = ctx.enter_context(sbuf(nc, "a32", [P, S], F32))
        RAW, HI, LO, ACC = ([s[n + "0"], s[n + "1"]] for n in ("raw", "hi", "lo", "acc"))
        FREE = [s["silu"], s["act"]]
        with nc.Block() as block:
            @block.sync
            def _(e):
                with e.Fori(0, KF) as it:
                    for u in range(2):
                        e.wait_ge(LO[u], it + 1)
                        e.dma_start(raw[:, u, :], w_gu[l, it, u]).then_inc(RAW[u], 16)

            @block.tensor
            def _(e):
                for u in range(2):
                    e.sem_inc(ACC[u], 1)
                with e.Fori(0, KF) as it:
                    for u in range(2):
                        e.wait_ge(HI[u], it + 1)
                        e.wait_ge(LO[u], it + 2)
                        e.wait_ge(FREE[u], it + 1)
                        for k in range(KD):
                            ins = mm3(e, ps[u][:, :], hi[:, u, k * P:(k + 1) * P], lo[:, u, k * P:(k + 1) * P],
                                      h_hi[:, k, :], h_lo[:, k, :], k == 0, k == KD - 1)
                        ins.then_inc(ACC[u], 1)

            @block.scalar
            def _(e):
                def split_hi(it, u):
                    e.wait_ge(RAW[u], 16 * (it + 1))
                    e.wait_ge(ACC[u], it + 1)
                    e.copy(hi[:, u, :], raw[:, u, :]).then_inc(HI[u], 1)

                e.sem_inc(s["silu"], 1)

                def silu(it):
                    e.wait_ge(ACC[0], it + 2)
                    e.wait_ge(s["act"], it + 1)
                    e.activation(sg[:, :], ps[0][:, :], ACT.Silu).then_inc(s["silu"], 1)

                def a_hi_copy(it):
                    e.wait_ge(s["act"], it + 2)
                    e.copy(a_hi[:, it, :], a32[:, :]).then_inc(s["ahi"], 1)

                split_hi(0, 0)
                split_hi(0, 1)
                with e.Fori(0, KF - 1) as it:
                    split_hi(it + 1, 0)
                    silu(it)
                    split_hi(it + 1, 1)
                    a_hi_copy(it)
                silu(KF - 1)
                a_hi_copy(KF - 1)

            @block.vector
            def _(e):
                for n in ("lo0", "lo1", "act", "alo"):
                    e.sem_inc(s[n], 1)

                def split_lo(it, u):
                    e.wait_ge(HI[u], it + 1)
                    e.tensor_tensor(lo[:, u, :], raw[:, u, :], hi[:, u, :].bitcast(F32), ALU.subtract).then_inc(LO[u], 1)

                def act(it):
                    e.wait_ge(ACC[1], it + 2)
                    e.wait_ge(s["silu"], it + 2)
                    e.wait_ge(s["alo"], it + 1)
                    e.tensor_tensor(a32[:, :], sg[:, :], ps[1][:, :], ALU.mult).then_inc(s["act"], 1)

                def a_lo_sub(it):
                    e.wait_ge(s["ahi"], it + 1)
                    e.tensor_tensor(a_lo[:, it, :], a32[:, :], a_hi[:, it, :].bitcast(F32), ALU.subtract).then_inc(s["alo"], 1)

                split_lo(0, 0)
                split_lo(0, 1)
                with e.Fori(0, KF - 1) as it:
                    split_lo(it + 1, 0)
                    act(it)
                    split_lo(it + 1, 1)
                    a_lo_sub(it)
                act(KF - 1)
                a_lo_sub(KF - 1)
    retire(nc, s)


def contract(nc, C, l, w_rows, kc, m_hi, m_lo, yT):
    s = phase(nc, ["raw0", "raw1", "hi0", "hi1", "lo0", "lo1", "used0", "used1"])
    ps = C["ps"]
    pairs = kc // 2
    with ExitStack() as ctx:
        raw, hi, lo = weight_buffers(nc, ctx)
        RAW, HI, LO, USED = ([s[n + "0"], s[n + "1"]] for n in ("raw", "hi", "lo", "used"))
        with nc.Block() as block:
            @block.sync
            def _(e):
                with e.Fori(0, pairs) as it:
                    for u in range(2):
                        e.wait_ge(LO[u], it + 1)
                        e.dma_start(raw[:, u, :], w_rows[l, it, u]).then_inc(RAW[u], 16)

            @block.scalar
            def _(e):
                with e.Fori(0, pairs) as it:
                    for u in range(2):
                        e.wait_ge(RAW[u], 16 * (it + 1))
                        e.wait_ge(USED[u], it + 1)
                        e.copy(hi[:, u, :], raw[:, u, :]).then_inc(HI[u], 1)
                e.wait_ge(USED[0], pairs + 1)
                e.wait_ge(USED[1], pairs + 1)
                for c in range(0, KD, 2):
                    e.copy(yT[:, c, :], ps[c][:, :])

            @block.vector
            def _(e):
                e.sem_inc(LO[0], 1)
                e.sem_inc(LO[1], 1)
                with e.Fori(0, pairs) as it:
                    for u in range(2):
                        e.wait_ge(HI[u], it + 1)
                        e.tensor_tensor(lo[:, u, :], raw[:, u, :], hi[:, u, :].bitcast(F32), ALU.subtract).then_inc(LO[u], 1)
                e.wait_ge(USED[0], pairs + 1)
                e.wait_ge(USED[1], pairs + 1)
                for c in range(1, KD, 2):
                    e.tensor_copy(yT[:, c, :], ps[c][:, :])

            @block.tensor
            def _(e):
                e.sem_inc(USED[0], 1)
                e.sem_inc(USED[1], 1)

                def pair(it, first, last):
                    for u in range(2):
                        e.wait_ge(HI[u], it + 1)
                        e.wait_ge(LO[u], it + 2)
                        for c in range(KD):
                            ins = mm3(e, ps[c][:, :], hi[:, u, c * P:(c + 1) * P], lo[:, u, c * P:(c + 1) * P],
                                      m_hi[:, 2 * it + u, :], m_lo[:, 2 * it + u, :], first and u == 0, last and u == 1)
                        ins.then_inc(USED[u], 1)

                pair(0, True, False)
                with e.Fori(1, pairs - 1) as it:
                    pair(it, False, False)
                pair(pairs - 1, False, True)
    retire(nc, s)


def residual(nc, C, l, yT, w_post, res):
    s = phase(nc, ["wp", "tr", "sq", "add", "ln", "rstd", "t", "x"])
    x, ps = C["x"], C["ps"]
    with ExitStack() as ctx:
        wp = ctx.enter_context(sbuf(nc, "rs_wp", [P, D], F32))
        junk = ctx.enter_context(sbuf(nc, "rs_junk", [P, 2, S], F32))
        tmp = ctx.enter_context(sbuf(nc, "rs_tmp", [P, 2, S], F32))
        ssq = ctx.enter_context(sbuf(nc, "rs_ssq", [P, NT, 2], F32))
        rstd = ctx.enter_context(sbuf(nc, "rs_rstd", [P, NT], F32))
        with nc.Block() as block:
            @block.sync
            def _(e):
                e.dma_start(wp[:, :], w_post[l].partition_broadcast(P)).then_inc(s["wp"], 16)

            @block.tensor
            def _(e):
                for t in range(NT):
                    for c in range(KD):
                        ins = e.transpose(ps[2 * t + c // 4][:, (c % 4) * P:(c % 4 + 1) * P], yT[:, c, t * P:(t + 1) * P], C["ident"])
                    ins.then_inc(s["tr"], 1)

            @block.scalar
            def _(e):
                for t in range(NT):
                    e.wait_ge(s["tr"], t + 1)
                    for half in range(2):
                        if t:
                            e.wait_ge(s["sq"], 2 * t + half - 1)
                        e.activation(junk[:, half, :], ps[2 * t + half][:, :], ACT.Square,
                                     accum_out=ssq[:, t, half:half + 1]).then_inc(s["sq"], 1)
                e.wait_ge(s["add"], 1)
                e.activation(rstd[:, :], rstd[:, :], ACT.Ln, bias=C["eps"], scale=1.0 / D).then_inc(s["ln"], 1)
                e.wait_ge(s["ln"], 1)
                e.activation(rstd[:, :], rstd[:, :], ACT.Exp, scale=-0.5).then_inc(s["rstd"], 1)

            @block.vector
            def _(e):
                e.wait_ge(s["sq"], 2 * NT)
                e.tensor_tensor(rstd[:, :], ssq[:, :, 0], ssq[:, :, 1], ALU.add).then_inc(s["add"], 1)
                e.wait_ge(s["rstd"], 1)
                e.wait_ge(s["wp"], 16)
                for n in range(2 * NT):
                    t, half = n // 2, n % 2
                    cols = slice(half * S, (half + 1) * S)
                    if n >= 2:
                        e.wait_ge(s["x"], n - 1)
                    e.scalar_tensor_tensor(out=tmp[:, half, :], in0=ps[n][:, :], scalar=rstd[:, t:t + 1], in1=wp[:, cols],
                                           op0=ALU.mult, op1=ALU.mult).then_inc(s["t"], 1)
                    e.wait_ge(s["t"], n + 1)
                    e.scalar_tensor_tensor(out=x[:, t, cols], in0=tmp[:, half, :], scalar=res, in1=x[:, t, cols],
                                           op0=ALU.mult, op1=ALU.add).then_inc(s["x"], 1)
    retire(nc, s)


def ffn(nc, C, l, w_pre, w_gu, w_down, w_post):
    with ExitStack() as outer:
        a_hi = outer.enter_context(sbuf(nc, "a_hi", [P, KF, S], F32R))
        a_lo = outer.enter_context(sbuf(nc, "a_lo", [P, KF, S], F32R))
        with ExitStack() as ctx:
            h_hi = ctx.enter_context(sbuf(nc, "h_hi", [P, KD, S], F32R))
            h_lo = ctx.enter_context(sbuf(nc, "h_lo", [P, KD, S], F32R))
            norm_transpose(nc, C, w_pre, h_hi, h_lo)
            ffn_gate_up(nc, C, l, w_gu, h_hi, h_lo, a_hi, a_lo)
        with ExitStack() as ctx:
            yT = ctx.enter_context(sbuf(nc, "yT", [P, KD, S], F32))
            contract(nc, C, l, w_down, KF, a_hi, a_lo, yT)
            residual(nc, C, l, yT, w_post, 0.5)


def project(nc, C, h_hi, h_lo, runs):
    s = phase(nc, ["raw0", "raw1", "hi0", "hi1", "lo0", "lo1", "acc0", "acc1", "free0", "free1"])
    ps = C["ps"]
    with ExitStack() as ctx:
        raw, hi, lo = weight_buffers(nc, ctx)
        RAW, HI, LO, ACC, FREE = ([s[n + "0"], s[n + "1"]] for n in ("raw", "hi", "lo", "acc", "free"))

        def over(e, n, body, first=0):
            if n - first == 1:
                body(first)
            elif n > first:
                with e.Fori(first, n) as it:
                    body(it)

        def starts():
            seen, out = [0, 0], []
            for iters, widths, _, _ in runs:
                out.append(tuple(seen))
                for u in range(len(widths)):
                    seen[u] += iters
            return out

        BASE = starts()
        with nc.Block() as block:
            @block.sync
            def _(e):
                for (iters, widths, src, _), base in zip(runs, BASE):
                    def body(it):
                        for u, w in enumerate(widths):
                            e.wait_ge(LO[u], it + (base[u] + 1))
                            e.dma_start(raw[:, u, 0:KD * w], src(it, u)).then_inc(RAW[u], 16)
                    over(e, iters, body)

            @block.tensor
            def _(e):
                for u in range(2):
                    e.sem_inc(ACC[u], 1)
                for (iters, widths, _, _), base in zip(runs, BASE):
                    def body(it):
                        for u, w in enumerate(widths):
                            e.wait_ge(HI[u], it + (base[u] + 1))
                            e.wait_ge(LO[u], it + (base[u] + 2))
                            e.wait_ge(FREE[u], it + (base[u] + 1))
                            for k in range(KD):
                                ins = mm3(e, ps[u][0:w, :], hi[:, u, k * w:(k + 1) * w], lo[:, u, k * w:(k + 1) * w],
                                          h_hi[:, k, :], h_lo[:, k, :], k == 0, k == KD - 1)
                            ins.then_inc(ACC[u], 1)
                    over(e, iters, body)

            @block.scalar
            def _(e):
                e.sem_inc(FREE[0], 1)
                for (iters, widths, _, dst), base in zip(runs, BASE):
                    def split_hi(it, u):
                        n = KD * widths[u]
                        e.wait_ge(RAW[u], 16 * it + 16 * (base[u] + 1))
                        e.wait_ge(ACC[u], it + (base[u] + 1))
                        e.copy(hi[:, u, 0:n], raw[:, u, 0:n]).then_inc(HI[u], 1)

                    def out0(it):
                        e.wait_ge(ACC[0], it + (base[0] + 2))
                        e.copy(dst(it, 0), ps[0][0:widths[0], :]).then_inc(FREE[0], 1)

                    for u in range(len(widths)):
                        split_hi(0, u)

                    def body(it):
                        split_hi(it + 1, 0)
                        out0(it)
                        if len(widths) > 1:
                            split_hi(it + 1, 1)
                    over(e, iters - 1, body)
                    out0(iters - 1)

            @block.vector
            def _(e):
                e.sem_inc(LO[0], 1)
                e.sem_inc(LO[1], 1)
                e.sem_inc(FREE[1], 1)
                for (iters, widths, _, dst), base in zip(runs, BASE):
                    def split_lo(it, u):
                        n = KD * widths[u]
                        e.wait_ge(HI[u], it + (base[u] + 1))
                        e.tensor_tensor(lo[:, u, 0:n], raw[:, u, 0:n], hi[:, u, 0:n].bitcast(F32), ALU.subtract).then_inc(LO[u], 1)

                    def out1(it):
                        e.wait_ge(ACC[1], it + (base[1] + 2))
                        e.tensor_copy(dst(it, 1), ps[1][0:widths[1], :]).then_inc(FREE[1], 1)

                    for u in range(len(widths)):
                        split_lo(0, u)

                    def body(it):
                        split_lo(it + 1, 0)
                        if len(widths) > 1:
                            out1(it)
                            split_lo(it + 1, 1)
                    over(e, iters - 1, body)
                    if len(widths) > 1:
                        out1(iters - 1)
    retire(nc, s)


def merge_last(nc, C, l, w_stream, gla_gates, o_hi, o_lo, g_hi, g_lo):
    s = phase(nc, Background.SEMS + ["tg0", "tg1", "ghi"])
    ps, merged = C["ps"], C["merged"]
    sums = [("branch", (False, c)) for c in range(KD)]
    bg = Background(C, s, w_stream, l, FIRST_JOB["last"], [(P, o_hi, o_lo, 0, True, True)] * KD, sums, [ps[0], ps[1]])
    with ExitStack() as ctx:
        tg = ctx.enter_context(sbuf(nc, "tanh_gate", [P, 2, KD // 2, S], F32))
        with nc.Block() as block:
            @block.sync
            def _(e):
                for half in range(2):
                    e.dma_start(tg[:, half, :, :], gla_gates[half * (KD // 2):(half + 1) * (KD // 2)].rearrange("c p n -> p c n")
                                ).then_inc(s[f"tg{half}"], 16)
                bg.loads(e)

            @block.gpsimd
            def _(e):
                bg.lo(e, 1)
                for c in range(KD):
                    if c + 2 <= bg.n:
                        bg.lo(e, c + 2)
                    bg.add(e, c)

            @block.tensor
            def _(e):
                for c in range(KD):
                    bg.mm(e, c)

            @block.vector
            def _(e):
                def split_lo(c):
                    e.wait_ge(s["ghi"], c + 1)
                    e.scalar_tensor_tensor(out=g_lo[:, c, :], in0=merged[:, c, :], scalar=0.5, in1=g_hi[:, c, :].bitcast(F32),
                                           op0=ALU.mult, op1=ALU.subtract)

                for c in range(KD):
                    if c % (KD // 2) == 0:
                        e.wait_ge(s[f"tg{c // (KD // 2)}"], 16)
                    e.wait_ge(s["b_acc"], c + 1)
                    if c:
                        e.wait_ge(s["b_add"], c)
                    e.scalar_tensor_tensor(out=bg.pr[:, :], in0=tg[:, c // (KD // 2), c % (KD // 2), :], scalar=1.0,
                                           in1=bg.bank(c)[:, :], op0=ALU.add, op1=ALU.mult).then_inc(s["b_pr"], 1)
                    if c >= 2:
                        split_lo(c - 2)
                split_lo(KD - 2)
                split_lo(KD - 1)

            @block.scalar
            def _(e):
                bg.hi(e, 1)
                for c in range(KD):
                    if c + 2 <= bg.n:
                        bg.hi(e, c + 2)
                    if c:
                        e.wait_ge(s["b_add"], c)
                        e.mul(g_hi[:, c - 1, :], merged[:, c - 1, :], 0.5).then_inc(s["ghi"], 1)
                e.wait_ge(s["b_add"], KD)
                e.mul(g_hi[:, KD - 1, :], merged[:, KD - 1, :], 0.5).then_inc(s["ghi"], 1)
    retire(nc, s)


def gated_output(nc, C, o_raw, z, norm_w, o_hi, o_lo, stream, jobs, sums):
    s = phase(nc, Background.SEMS + ["sq", "ss", "ln", "rs", "silu", "a", "b", "hi"])
    ps = C["ps"]
    H = 4
    bg = Background(C, s, *stream, jobs, sums, [ps[4]])
    with ExitStack() as ctx:
        sq = ctx.enter_context(sbuf(nc, "go_sq", [P, H, S], F32))
        rs = ctx.enter_context(sbuf(nc, "go_rs", [P, H, S], F32))
        sz = ctx.enter_context(sbuf(nc, "go_sz", [P, H, S], F32))
        with nc.Block() as block:
            @block.sync
            def _(e):
                bg.loads(e)

            @block.gpsimd
            def _(e):
                for j in range(1, bg.n + 1):
                    bg.lo(e, j)

            @block.scalar
            def _(e):
                if jobs:
                    bg.hi(e, 1)
                e.activation(sz[:, :, :], z, ACT.Silu).then_inc(s["silu"], 1)
                for h in range(H):
                    e.activation(sq[:, h, :], o_raw[:, h, :], ACT.Square).then_inc(s["sq"], 1)
                for h in range(H):
                    e.wait_ge(s["ss"], h + 1)
                    e.activation(rs[:, h, :], ps[h][:, :], ACT.Ln, bias=C["eps"], scale=1.0 / P).then_inc(s["ln"], 1)
                for h in range(H):
                    e.wait_ge(s["ln"], h + 1)
                    e.activation(rs[:, h, :], rs[:, h, :], ACT.Exp, scale=-0.5).then_inc(s["rs"], 1)
                if jobs:
                    bg.hi(e, 2)
                    bg.out(e, 0)
                for h in range(H):
                    e.wait_ge(s["b"], h + 1)
                    e.copy(o_hi[:, h, :], sz[:, h, :]).then_inc(s["hi"], 1)
                bg.stored(e)

            @block.tensor
            def _(e):
                if jobs:
                    bg.mm(e, 0)
                for h in range(H):
                    e.wait_ge(s["sq"], h + 1)
                    e.matmul(ps[h][:, :], C["ones"], sq[:, h, :], start=True, stop=True).then_inc(s["ss"], 1)
                if jobs:
                    bg.mm(e, 1)

            @block.vector
            def _(e):
                e.wait_ge(s["silu"], 1)
                for h in range(H):
                    e.wait_ge(s["rs"], h + 1)
                    e.scalar_tensor_tensor(out=rs[:, h, :], in0=o_raw[:, h, :], scalar=norm_w, in1=rs[:, h, :],
                                           op0=ALU.mult, op1=ALU.mult).then_inc(s["a"], 1)
                    e.wait_ge(s["a"], h + 1)
                    e.tensor_tensor(sz[:, h, :], sz[:, h, :], rs[:, h, :], ALU.mult).then_inc(s["b"], 1)
                for h in range(H):
                    e.wait_ge(s["hi"], h + 1)
                    e.tensor_tensor(o_lo[:, h, :], sz[:, h, :], o_hi[:, h, :].bitcast(F32), ALU.subtract)
    retire(nc, s)


def gdn_prepare(nc, C, prm, pT, miscT, qkv, ba, beta, g, stream, jobs, sums):
    s = phase(nc, Background.SEMS + ["conv", "silu", "sq", "ss", "ln", "rs", "tr", "ba", "y", "ny", "my", "ex", "lg", "eb", "ea", "b1", "sp"])
    ps = C["ps"]
    QKV = 3 * GDN_H
    bg = Background(C, s, *stream, jobs, sums, [ps[4], ps[5], ps[6]], started=False)
    with ExitStack() as ctx:
        cv = ctx.enter_context(sbuf(nc, "cv", [P, 2, S], F32))
        sq = ctx.enter_context(sbuf(nc, "l2_sq", [P, 4, S], F32))
        rs = ctx.enter_context(sbuf(nc, "l2_rs", [P, 2 * GDN_H, S], F32))
        y = ctx.enter_context(sbuf(nc, "sp_y", [P, NT, 4], F32))
        ny = ctx.enter_context(sbuf(nc, "sp_ny", [P, NT, 4], F32))
        ea = ctx.enter_context(sbuf(nc, "exp_a_log", [P, 4], F32))
        eb = ctx.enter_context(sbuf(nc, "exp_b", [P, NT, 4], F32))
        w = prm["conv"]
        with nc.Block() as block:
            @block.sync
            def _(e):
                bg.loads(e)

            @block.vector
            def _(e):
                for c in range(QKV):
                    if c >= 2:
                        e.wait_ge(s["silu"], c - 1)
                    for n, j in enumerate(range(3, -1, -1)):
                        src = pT[:, c, 1 + j:1 + j + S]
                        wj = w[:, j * QKV + c:j * QKV + c + 1]
                        if n == 0:
                            e.tensor_scalar(cv[:, c % 2, :], src, wj, None, ALU.mult).then_inc(s["conv"], 1)
                        else:
                            e.wait_ge(s["conv"], 4 * c + n)
                            e.scalar_tensor_tensor(out=cv[:, c % 2, :], in0=src, scalar=wj, in1=cv[:, c % 2, :],
                                                   op0=ALU.mult, op1=ALU.add).then_inc(s["conv"], 1)
                e.wait_ge(s["tr"], 1)
                e.tensor_copy(ba[:, :, :], ps[7][:, :].rearrange("p (t c) -> p t c", t=NT)[:, :, 0:80]).then_inc(s["ba"], 1)
                e.wait_ge(s["ba"], 1)
                e.tensor_tensor(y[:, :, :], ba[:, :, 4:8], prm["dt_bias"].unsqueeze(1).to_broadcast([P, NT, 4]), ALU.add).then_inc(s["y"], 1)
                e.wait_ge(s["y"], 1)
                e.tensor_scalar(ny[:, :, :], y[:, :, :], -1.0, None, ALU.mult).then_inc(s["ny"], 1)
                e.wait_ge(s["ny"], 1)
                e.tensor_tensor(ny[:, :, :], ny[:, :, :], y[:, :, :], ALU.min).then_inc(s["my"], 1)
                e.wait_ge(s["eb"], 1)
                e.tensor_scalar(eb[:, :, :], eb[:, :, :], 1.0, None, ALU.add).then_inc(s["b1"], 1)
                e.wait_ge(s["b1"], 1)
                e.reciprocal(beta[:, :, :], eb[:, :, :])
                e.wait_ge(s["lg"], 1)
                e.scalar_tensor_tensor(out=y[:, :, :], in0=y[:, :, :], scalar=0.0, in1=ny[:, :, :], op0=ALU.max, op1=ALU.add).then_inc(s["sp"], 1)
                e.wait_ge(s["sp"], 1)
                e.wait_ge(s["ea"], 1)
                e.scalar_tensor_tensor(out=g[:, :, :], in0=y[:, :, :], scalar=-1.0, in1=ea[:, :].unsqueeze(1).to_broadcast([P, NT, 4]),
                                       op0=ALU.mult, op1=ALU.mult)
                for c in range(2 * GDN_H):
                    e.wait_ge(s["rs"], c + 1)
                    e.scalar_tensor_tensor(out=qkv[:, c, :], in0=qkv[:, c, :], scalar=(P ** -0.5 if c < GDN_H else 1.0),
                                           in1=rs[:, c, :], op0=ALU.mult, op1=ALU.mult).then_inc(s["sp"], 1)

            @block.scalar
            def _(e):
                bg.hi(e, 0)
                bg.hi(e, 1)
                for c in range(QKV):
                    e.wait_ge(s["conv"], 4 * (c + 1))
                    e.activation(qkv[:, c, :], cv[:, c % 2, :], ACT.Silu).then_inc(s["silu"], 1)
                    if c >= 2 and c % 2 == 0 and c // 2 - 1 < NSA_FIRST:
                        bg.out(e, c // 2 - 1)
                    bg.hi(e, c + 2)
                bg.hi(e, QKV + 2)
                e.activation(ea[:, :], prm["a_log"], ACT.Exp).then_inc(s["ea"], 1)
                e.wait_ge(s["ba"], 1)
                e.activation(eb[:, :, :], ba[:, :, 0:4], ACT.Exp, scale=-1.0).then_inc(s["eb"], 1)
                e.wait_ge(s["my"], 1)
                e.activation(ny[:, :, :], ny[:, :, :], ACT.Exp).then_inc(s["ex"], 1)
                for n in range(NSA_FIRST, len(sums)):
                    bg.out(e, n)
                e.wait_ge(s["ex"], 1)
                e.activation(ny[:, :, :], ny[:, :, :], ACT.Ln, bias=C["one"]).then_inc(s["lg"], 1)
                for c in range(2 * GDN_H):
                    e.wait_ge(s["ss"], c + 1)
                    e.activation(rs[:, c, :], ps[c % 4][:, :], ACT.Ln, bias=C["eps"]).then_inc(s["ln"], 1)
                for c in range(2 * GDN_H):
                    e.wait_ge(s["ln"], c + 1)
                    e.activation(rs[:, c, :], rs[:, c, :], ACT.Exp, scale=-0.5).then_inc(s["rs"], 1)
                bg.stored(e)

            @block.gpsimd
            def _(e):
                bg.lo(e, 0)
                bg.lo(e, 1)
                for c in range(2 * GDN_H):
                    e.wait_ge(s["silu"], c + 1)
                    if c >= 4:
                        e.wait_ge(s["ss"], c - 3)
                    e.tensor_tensor(sq[:, c % 4, :], qkv[:, c, :], qkv[:, c, :], ALU.mult).then_inc(s["sq"], 1)
                    bg.lo(e, c + 2)
                for j in range(2 * GDN_H + 2, bg.n + 1):
                    bg.lo(e, j)

            @block.tensor
            def _(e):
                for t in range(NT):
                    ins = e.transpose(ps[7][:, t * P:t * P + 80], miscT[:, t * P:(t + 1) * P], C["ident"][0:80, 0:80])
                ins.then_inc(s["tr"], 1)

                def squares(c):
                    e.wait_ge(s["sq"], c + 1)
                    if c >= 4:
                        e.wait_ge(s["ln"], c - 3)
                    e.matmul(ps[c % 4][:, :], C["ones"], sq[:, c % 4, :], start=True, stop=True).then_inc(s["ss"], 1)

                bg.mm(e, 0)
                bg.mm(e, 1)
                for c in range(4):
                    squares(c)
                    bg.mm(e, c + 2)
                for j in range(6, bg.n):
                    bg.mm(e, j)
                for c in range(4, 2 * GDN_H):
                    squares(c)
    retire(nc, s)


def gdn_tile(nc, C, W, t, stream, jobs, sums):
    s = phase(nc, ["qt", "kt", "vt", "gb", "gcb", "gc", "gcs", "dt0", "dt1", "dn0", "dn1", "eg", "egc", "ekd", "kd0", "qd",
                   "kk", "kq", "dtm", "at", "L0", "bbeta", "trk", "trv", "kde", "ken", "vb", "lv", "b1t", "T", "U", "q", "qs",
                   "uq", "wu", "u", "wt", "vs", "vn", "o", "st", "S", "os"] + Background.SEMS)
    ps = C["ps"]
    bg = Background(C, s, *stream, jobs, sums, [ps[6], ps[7]])
    H = GDN_H
    HB = lambda ap: ap.rearrange("p (h c) -> p h c", h=H)
    cols = bass.ts(t, P)
    (qt, kt, vt, gb, DT, DN, EG, L, AT, B, Tm, U, Q, u, wT, kd, vb, kbe, qd, vn, St, sm) = (
        W[n] for n in ("qt", "kt", "vt", "gb", "DT", "DN", "EG", "L", "AT", "B", "Tm", "U", "Q", "u", "wT", "kd", "vb",
                       "kbe", "qd", "vn", "St", "sm"))
    qkv, beta, g, o_raw = W["qkv"], W["beta"], W["g"], W["o_raw"]
    gc, ekd, egc, beg, bt, gt = (sm[:, i, :] for i in range(6))
    lvl = lambda n: C["lvl"][:, n * P:(n + 1) * P].unsqueeze(1).to_broadcast([P, H, P])
    bc = lambda ap: ap.unsqueeze(1).to_broadcast([P, H, P])
    NL = 6
    with nc.Block() as block:
        @block.sync
        def _(e):
            bg.loads(e)

        @block.gpsimd
        def _(e):
            bg.lo(e, 1)
            e.wait_ge(s["L0"], H)
            for n in range(NL):
                e.tensor_tensor(B[:, n, :, :], L[:, :, :], lvl(n), ALU.mult).then_inc(s["lv"], 1)
                bg.lo(e, n + 2)
            for j in range(NL + 2, bg.n + 1):
                bg.lo(e, j)

        @block.vector
        def _(e):
            e.tensor_copy(gt, g[:, bass.ds(t, 1), :].rearrange("p a h -> p (a h)")).then_inc(s["gc"], 1)
            e.tensor_copy(bt, beta[:, bass.ds(t, 1), :].rearrange("p a h -> p (a h)")).then_inc(s["bbeta"], 1)
            e.wait_ge(s["gc"], 1)
            e.tensor_tensor(gb[:, :, :], bc(C["ones"]), gt.unsqueeze(2).to_broadcast([P, H, P]), ALU.mult).then_inc(s["gb"], 1)
            e.wait_ge(s["gcb"], 1)
            e.tensor_copy(gc, ps[0][:, 0:H]).then_inc(s["gcs"], 1)
            e.wait_ge(s["gcs"], 1)
            e.tensor_tensor(ekd, ps[0][:, H:2 * H], gc, ALU.subtract).then_inc(s["ekd"], 1)
            gcB = HB(ps[1][:, :])
            e.wait_ge(s["eg"], 1)
            for h in range(H):
                e.tensor_scalar(DT[:, h, :], gcB[:, h, :], gc[:, h:h + 1], 0.0, ALU.subtract, ALU.min).then_inc(s["dt0"], 1)
                e.tensor_scalar(DN[:, h, :], gcB[:, h, :], gc[:, h:h + 1], 0.0, ALU.subtract, ALU.max).then_inc(s["dn0"], 1)
            e.wait_ge(s["dt1"], 1)
            e.tensor_tensor(DT[:, :, :], DT[:, :, :], bc(C["tri64"]), ALU.mult).then_inc(s["dtm"], 1)
            e.wait_ge(s["kk"], 1)
            e.wait_ge(s["dn1"], 1)
            e.wait_ge(s["bbeta"], 1)
            for h in range(H):
                e.scalar_tensor_tensor(out=L[:, h, :], in0=HB(ps[2][:, :])[:, h, :], scalar=bt[:, h:h + 1], in1=DN[:, h, :],
                                       op0=ALU.mult, op1=ALU.mult).then_inc(s["L0"], 1)
            e.wait_ge(s["kq"], 1)
            e.wait_ge(s["dtm"], 1)
            e.tensor_tensor(AT[:, :, :], HB(ps[3][:, :]), DT[:, :, :], ALU.mult).then_inc(s["at"], 1)
            e.wait_ge(s["eg"], 1)
            e.wait_ge(s["qt"], 1)
            e.tensor_tensor(qd[:, :, :], qt[:, :, :], EG[:, :, :], ALU.mult).then_inc(s["qd"], 1)
            e.wait_ge(s["egc"], 2)
            e.tensor_tensor(beg, egc, bt, ALU.mult).then_inc(s["ken"], 1)
            e.wait_ge(s["ken"], 1)
            e.wait_ge(s["trk"], 1)
            for h in range(H):
                kn = HB(ps[4][:, :])[:, h, :]
                e.tensor_scalar(kd[:, h, :], kn, ekd[:, h:h + 1], None, ALU.mult).then_inc(s["kde"], 1)
                e.tensor_scalar(kbe[:, h, :], kn, beg[:, h:h + 1], None, ALU.mult).then_inc(s["kde"], 1)
            e.wait_ge(s["trv"], 1)
            for h in range(H):
                e.tensor_scalar(vb[:, h, :], HB(ps[5][:, :])[:, h, :], bt[:, h:h + 1], None, ALU.mult).then_inc(s["vb"], 1)
            e.wait_ge(s["lv"], 1)
            e.tensor_tensor(Tm[:, :, :], bc(C["ident"]), B[:, 0, :, :], ALU.subtract).then_inc(s["T"], 1)
            e.wait_ge(s["b1t"], 1)
            e.tensor_tensor(U[:, :, :], bc(C["ident"]), HB(ps[0][:, :]), ALU.subtract).then_inc(s["U"], 1)
            for n in range(1, NL):
                e.wait_ge(s["q"], n)
                e.tensor_copy(Q[:, :, :], HB(ps[1][:, :])).then_inc(s["qs"], 1)
                e.wait_ge(s["uq"], n)
                e.tensor_tensor(U[:, :, :], U[:, :, :], HB(ps[2][:, :]), ALU.subtract).then_inc(s["U"], 1)
                if n < NL - 1:
                    e.tensor_tensor(Tm[:, :, :], Tm[:, :, :], HB(ps[3][:, :]), ALU.subtract).then_inc(s["T"], 1)
            e.wait_ge(s["wu"], 1)
            e.tensor_copy(u[:, :, :], HB(ps[4][:, :])).then_inc(s["u"], 1)
            e.wait_ge(s["u"], 1)
            for c in range(2):
                rows = slice(c * GDN_C, (c + 1) * GDN_C)
                e.wait_ge(s["vs"], c + 1)
                e.tensor_tensor(vn[rows, :, :], u[rows, :, :], HB(ps[2][rows, :]), ALU.subtract).then_inc(s["vn"], 1)
                e.wait_ge(s["st"], c + 1)
                for h in range(H):
                    last = (c + 1) * GDN_C - 1
                    e.scalar_tensor_tensor(out=St[:, h, :], in0=St[:, h, :], scalar=EG[:, h, last:last + 1],
                                           in1=HB(ps[0][:, :])[:, h, :], op0=ALU.mult, op1=ALU.add).then_inc(s["S"], 1)

        @block.scalar
        def _(e):
            e.copy(kt[:, :, :], qkv[:, H:2 * H, cols]).then_inc(s["kt"], 1)
            bg.hi(e, 1)
            e.copy(qt[:, :, :], qkv[:, 0:H, cols]).then_inc(s["qt"], 1)
            e.wait_ge(s["gcb"], 1)
            e.activation(EG[:, :, :], HB(ps[1][:, :]), ACT.Exp).then_inc(s["eg"], 1)
            e.copy(vt[:, :, :], qkv[:, 2 * H:3 * H, cols]).then_inc(s["vt"], 1)
            e.wait_ge(s["ekd"], 1)
            e.activation(ekd, ekd, ACT.Exp).then_inc(s["egc"], 1)
            e.activation(egc, gc, ACT.Exp).then_inc(s["egc"], 1)
            e.wait_ge(s["dt0"], H)
            e.activation(DT[:, :, :], DT[:, :, :], ACT.Exp).then_inc(s["dt1"], 1)
            e.wait_ge(s["dn0"], H)
            e.activation(DN[:, :, :], DN[:, :, :], ACT.Exp, scale=-1.0).then_inc(s["dn1"], 1)
            bg.hi(e, 2)
            for n in range(len(sums) - 1):
                bg.hi(e, 2 * n + 3)
                bg.out(e, n)
                bg.hi(e, 2 * n + 4)
            e.wait_ge(s["wu"], 2)
            e.copy(wT[:, :, :], HB(ps[5][:, :])).then_inc(s["wt"], 1)
            bg.out(e, len(sums) - 1)
            e.wait_ge(s["o"], 2)
            e.copy(o_raw[:, :, cols], HB(ps[3][:, :])).then_inc(s["os"], 1)
            bg.stored(e)

        @block.tensor
        def _(e):
            e.wait_ge(s["gc"], 1)
            e.matmul(ps[0][:, 0:H], C["tri64"], gt, start=True, stop=True)
            e.matmul(ps[0][:, H:2 * H], C["blk64"], gt, start=True, stop=True)
            e.wait_ge(s["gb"], 1)
            for h in range(H):
                ins = e.matmul(HB(ps[1][:, :])[:, h, :], gb[:, h, :], C["tri64"], start=True, stop=True)
            ins.then_inc(s["gcb"], 1)
            bg.mm(e, 0)
            e.wait_ge(s["kt"], 1)
            for h in range(H):
                ins = e.matmul(HB(ps[2][:, :])[:, h, :], kt[:, h, :], kt[:, h, :], start=True, stop=True)
            ins.then_inc(s["kk"], 1)
            e.wait_ge(s["qt"], 1)
            for h in range(H):
                ins = e.matmul(HB(ps[3][:, :])[:, h, :], kt[:, h, :], qt[:, h, :], start=True, stop=True)
            ins.then_inc(s["kq"], 1)
            for h in range(H):
                ins = e.transpose(HB(ps[4][:, :])[:, h, :], kt[:, h, :], C["ident"])
            ins.then_inc(s["trk"], 1)
            e.wait_ge(s["vt"], 1)
            for h in range(H):
                ins = e.transpose(HB(ps[5][:, :])[:, h, :], vt[:, h, :], C["ident"])
            ins.then_inc(s["trv"], 1)
            bg.mm(e, 1)
            e.wait_ge(s["lv"], 1)
            e.wait_ge(s["ekd"], 1)
            for h in range(H):
                ins = e.transpose(HB(ps[0][:, :])[:, h, :], B[:, 0, h, :], C["ident"])
            ins.then_inc(s["b1t"], 1)
            bg.mm(e, 2)
            for n in range(1, NL):
                e.wait_ge(s["lv"], n + 1)
                e.wait_ge(s["U"], n)
                e.wait_ge(s["dn0"], H)
                for h in range(H):
                    ins = e.matmul(HB(ps[1][:, :])[:, h, :], B[:, n, h, :], U[:, h, :], start=True, stop=True)
                ins.then_inc(s["q"], 1)
                if n < NL - 1 or bg.n > 8:
                    bg.mm(e, n + 2)
                e.wait_ge(s["qs"], n)
                e.wait_ge(s["T"], n)
                e.wait_ge(s["L0"], H)
                for h in range(H):
                    ins = e.matmul(HB(ps[2][:, :])[:, h, :], Tm[:, h, :], Q[:, h, :], start=True, stop=True)
                if n < NL - 1:
                    e.wait_ge(s["at"], 1)
                    for h in range(H):
                        ins = e.matmul(HB(ps[3][:, :])[:, h, :], Q[:, h, :], Tm[:, h, :], start=True, stop=True)
                ins.then_inc(s["uq"], 1)
            e.wait_ge(s["U"], NL)
            e.wait_ge(s["vb"], H)
            e.wait_ge(s["kde"], 2 * H)
            for h in range(H):
                ins = e.matmul(HB(ps[4][:, :])[:, h, :], U[:, h, :], vb[:, h, :], start=True, stop=True)
            ins.then_inc(s["wu"], 1)
            for h in range(H):
                ins = e.matmul(HB(ps[5][:, :])[:, h, :], kbe[:, h, :], U[:, h, :], start=True, stop=True)
            ins.then_inc(s["wu"], 1)
            e.wait_ge(s["wt"], 1)
            e.wait_ge(s["at"], 1)
            e.wait_ge(s["qd"], 1)
            for c in range(2):
                rows = slice(c * GDN_C, (c + 1) * GDN_C)
                if c:
                    e.wait_ge(s["S"], H)
                for h in range(H):
                    ins = e.matmul(HB(ps[2][:, :])[:, h, :], wT[:, h, :], St[:, h, :], start=True, stop=True)
                ins.then_inc(s["vs"], 1)
                if c == 0:
                    bg.mm(e, bg.n - 1)
                e.wait_ge(s["vn"], c + 1)
                for h in range(H):
                    out = HB(ps[3][:, :])[:, h, rows]
                    e.matmul(out, St[:, h, :], qd[:, h, rows], start=True, stop=False)
                    ins = e.matmul(out, vn[rows, h, :], AT[rows, h, rows], start=False, stop=True)
                ins.then_inc(s["o"], 1)
                for h in range(H):
                    ins = e.matmul(HB(ps[0][:, :])[:, h, :], kd[rows, h, :], vn[rows, h, :], start=True, stop=True)
                ins.then_inc(s["st"], 1)
    retire(nc, s)


def gdn(nc, C, prm, l, wd, h_hi, h_lo, miscT, ba, o_hi, o_lo, nsa_rows, gla_gates):
    H = GDN_H
    with ExitStack() as ctx:
        sb = lambda n, shape: ctx.enter_context(sbuf(nc, n, shape, F32))
        z = sb("gdn_z", [P, H, S])
        qkv = sb("gdn_qkv", [P, 3 * H, S])
        beta = sb("gdn_beta", [P, NT, 4])
        g = sb("gdn_g", [P, NT, 4])
        o_raw = sb("gdn_o", [P, H, S])
        with ExitStack() as c2:
            pT = c2.enter_context(sbuf(nc, "gdn_pT", [P, 3 * H, 4 + S], F32))
            zero(nc, pT[:, :, 0:4])
            w_gdn = wd["w_gdn"]
            project(nc, C, h_hi, h_lo, [
                (6, (P, P), lambda it, u: w_gdn[l, 2 * it + u], lambda it, u: pT[:, 2 * it + u, 4:4 + S]),
                (2, (P, P), lambda it, u: w_gdn[l, 2 * it + (12 + u)], lambda it, u: z[:, 2 * it + u, :]),
                (1, (80,), lambda it, u: wd["w_misc"][l], lambda it, u: miscT[:, :])])
            jobs, sums = [], []
            for n in range(NSA_FIRST):
                jobs += column_jobs(NDK, h_hi, h_lo)
                sums.append(("store", nsa_rows[n]))
            for c in range(3):
                jobs += column_jobs(P, h_hi, h_lo)
                sums.append(("tanh", gla_gates[c]))
            gdn_prepare(nc, C, prm, pT, miscT, qkv, ba, beta, g, (wd["w_stream"], l, FIRST_JOB["gdn_prepare"]), jobs, sums)
        with ExitStack() as c2:
            W = {"qkv": qkv, "beta": beta, "g": g, "o_raw": o_raw}
            for k, n in enumerate(("qt", "kt", "vt", "gb", "DT", "DN", "EG", "L")):
                W[n] = C["merged"][:, k, :].rearrange("p (h c) -> p h c", h=H)
            for n in ("AT", "Tm", "U", "Q", "u", "wT", "kd", "vb", "kbe", "qd", "vn", "St"):
                W[n] = c2.enter_context(sbuf(nc, "gdn_" + n, [P, H, P], F32))
            W["B"] = c2.enter_context(sbuf(nc, "gdn_B", [P, 6, H, P], F32))
            W["sm"] = c2.enter_context(sbuf(nc, "gdn_sm", [P, 6, 4], F32))
            zero(nc, W["St"][:, :, :])
            with nc.Fori(0, NT) as t:
                jobs, sums = [], []
                per_tile = (NSA_CHUNKS - NSA_FIRST) // NT
                for c in range(per_tile):
                    n = per_tile * t + (NSA_FIRST + c)
                    jobs += column_jobs(NDK, h_hi, h_lo)
                    sums.append(("store", nsa_rows[bass.ds(n, 1)].rearrange("a p n -> (a p) n")))
                gdn_tile(nc, C, W, t, (wd["w_stream"], l, 2 * per_tile * t + FIRST_JOB["gdn"]), jobs, sums)
        gated_output(nc, C, o_raw, z[:, :, :], prm["gdn_norm"], o_hi, o_lo, (wd["w_stream"], l, FIRST_JOB["gdn_out"]),
                     column_jobs(P, h_hi, h_lo), [("tanh", gla_gates[3])])


def nsa_compress(nc, C, prm, l, wd, nsa_rows, early, miscT, gates, vnat, kcT, vc, stream, jobs, sums):
    kT, vT = early[:, 0:NSA_G, :], early[0:NDV, NSA_G:4 * NSA_G, :]
    s = phase(nc, Background.SEMS + ["early", "g0", "g1", "trg", "gate", "gate2", "tr0", "tr1", "v0", "v1", "xk", "xv", "wk0", "wk1", "wv0", "wv1", "usedk0",
                   "usedk1", "usedv0", "usedv1", "hk", "hv", "hid", "kc", "vc", "kcs"])
    ps = C["ps"]
    bg = Background(C, s, *stream, jobs, sums, [ps[6]])
    LB = 8
    NB = CMP_LEN // LB
    with ExitStack() as ctx:
        sb = lambda n, shape: ctx.enter_context(sbuf(nc, n, shape, F32))
        xk = sb("cmp_xk", [NDK, CMP_LEN, NSA_G, NCMP])
        xv = sb("cmp_xv", [NDV, CMP_LEN, NSA_G, NCMP])
        wk = sb("cmp_wk", [NDK, 2, LB, CMP_HID])
        wv = sb("cmp_wv", [NDV, 2, LB, CMP_HID])
        hk = sb("cmp_hk", [P, 2, NSA_G * NCMP])
        hv = sb("cmp_hv", [P, 2, NSA_G * NCMP])
        with nc.Block() as block:
            @block.sync
            def _(e):
                e.dma_start(early[:, :, :], nsa_rows[NSA_LATE:NSA_CHUNKS].rearrange("c p n -> p c n")).then_inc(s["early"], 16)
                for b in range(NB):
                    if b >= 2:
                        for j in (range(2, 8) if b == 2 else range(8, 12)):
                            bg.load(e, j)
                        e.wait_ge(s[f"usedk{b % 2}"], b // 2)
                    e.dma_start(wk[:, b % 2, :, :], wd["w_ck"][l, :, b * LB:(b + 1) * LB, :]).then_inc(s[f"wk{b % 2}"], 16)
                    if b >= 2:
                        e.wait_ge(s[f"usedv{b % 2}"], b // 2)
                    e.dma_start(wv[:, b % 2, :, :], wd["w_cv"][l, :, b * LB:(b + 1) * LB, :]).then_inc(s[f"wv{b % 2}"], 16)
                bg.load(e, 12)
                bg.load(e, 13)
                bg.loads_done(e)

            @block.gpsimd
            def _(e):
                bg.lo(e, 1)
                bg.lo(e, 2)
                for j in range(3, bg.n + 1):
                    bg.lo(e, j)
                    if jobs[j - 1][5] and bg.sum_of[j - 1] in bg.branches:
                        bg.add(e, bg.sum_of[j - 1])

            @block.tensor
            def _(e):
                bg.mm(e, 0)
                for t in range(NT):
                    ins = e.transpose(ps[7][:, t * P:t * P + 80], miscT[:, t * P:(t + 1) * P], C["ident"][0:80, 0:80])
                ins.then_inc(s["trg"], 1)
                e.wait_ge(s["early"], 16)
                for b in range(2):
                    for g in range(NSA_G):
                        for t in range(NT):
                            n = g * NT + t
                            ins = e.transpose(ps[4 + b][:, n * NDV:(n + 1) * NDV], vT[:, 2 * (b + 1) + g, t * P:(t + 1) * P],
                                              C["ident"][0:NDV, 0:NDV])
                    ins.then_inc(s[f"tr{b}"], 1)
                e.wait_ge(s["xk"], NSA_G)
                e.wait_ge(s["xv"], NSA_G)
                for b in range(NB):
                    e.wait_ge(s[f"wk{b % 2}"], 16 * (b // 2 + 1))
                    for j in range(LB):
                        p = b * LB + j
                        for c in range(2):
                            ins = e.matmul(ps[c][:, 0:NSA_G * NCMP], wk[:, b % 2, j, c * P:(c + 1) * P],
                                           xk[:, p, :, :].rearrange("p g n -> p (g n)"), start=(p == 0), stop=(p == CMP_LEN - 1))
                    ins.then_inc(s[f"usedk{b % 2}"], 1)
                    bg.mm(e, 3 * b + 1)
                    e.wait_ge(s[f"wv{b % 2}"], 16 * (b // 2 + 1))
                    for j in range(LB):
                        p = b * LB + j
                        for c in range(2):
                            ins = e.matmul(ps[2 + c][:, 0:NSA_G * NCMP], wv[:, b % 2, j, c * P:(c + 1) * P],
                                           xv[:, p, :, :].rearrange("p g n -> p (g n)"), start=(p == 0), stop=(p == CMP_LEN - 1))
                    ins.then_inc(s[f"usedv{b % 2}"], 1)
                    bg.mm(e, 3 * b + 2)
                    if b + 1 < NB:
                        bg.mm(e, 3 * b + 3)
                e.wait_ge(s["hid"], 4)
                e.wait_ge(s["kcs"], 2)
                for c in range(2):
                    ins = e.matmul(ps[4][0:NDK, 0:NSA_G * NCMP], prm["w2k"][:, c * NDK:(c + 1) * NDK], hk[:, c, :],
                                   start=(c == 0), stop=(c == 1))
                ins.then_inc(s["kc"], 1)
                for g in range(NSA_G):
                    for c in range(2):
                        ins = e.matmul(ps[5][0:NCMP, g * NDV:(g + 1) * NDV], hv[:, c, g * NCMP:(g + 1) * NCMP],
                                       prm["w2v"][:, c * NDV:(c + 1) * NDV], start=(c == 0), stop=(c == 1))
                ins.then_inc(s["vc"], 1)

            @block.scalar
            def _(e):
                e.wait_ge(s["trg"], 1)
                e.activation(gates[:, :, :], ps[7][:, :].rearrange("p (t c) -> p t c", t=NT)[:, :, 32:56], ACT.Tanh,
                             scale=0.5).then_inc(s["gate"], 1)
                bg.hi(e, 1)
                bg.hi(e, 2)
                for b in range(2):
                    e.wait_ge(s[f"tr{b}"], 1)
                    e.copy(vnat[:, b, :, :, :], ps[4 + b][:, :].rearrange("p (g t d) -> p g t d", g=NSA_G, t=NT)).then_inc(s["kcs"], 1)
                for j in range(3, bg.n + 1):
                    if jobs[j - 2][5]:
                        bg.out(e, bg.sum_of[j - 2])
                    bg.hi(e, j)
                e.wait_ge(s["usedk1"], NB // 2)
                for c in range(2):
                    e.activation(hk[:, c, :], ps[c][:, 0:NSA_G * NCMP], ACT.Gelu_apprx_tanh).then_inc(s["hid"], 1)
                e.wait_ge(s["usedv1"], NB // 2)
                for c in range(2):
                    e.activation(hv[:, c, :], ps[2 + c][:, 0:NSA_G * NCMP], ACT.Gelu_apprx_tanh).then_inc(s["hid"], 1)
                e.wait_ge(s["kc"], 1)
                e.copy(kcT[:, :, :], ps[4][0:NDK, 0:NSA_G * NCMP].rearrange("p (g n) -> p g n", g=NSA_G))
                e.wait_ge(s["vc"], 1)
                e.copy(vc[:, :, :], ps[5][0:NCMP, 0:NSA_G * NDV].rearrange("p (g d) -> p g d", g=NSA_G))

            @block.vector
            def _(e):
                def blocks(x, pe, out, sem):
                    for g in range(NSA_G):
                        for half in range(2):
                            pos = slice(half * CMP_STRIDE, (half + 1) * CMP_STRIDE)
                            src = x[:, g, half * CMP_STRIDE:half * CMP_STRIDE + NCMP * CMP_STRIDE]
                            ins = e.tensor_tensor(out[:, pos, g, :], src.rearrange("p (n j) -> p j n", j=CMP_STRIDE),
                                                  pe[:, pos].unsqueeze(2).to_broadcast([x.shape[0], CMP_STRIDE, NCMP]), ALU.add)
                        ins.then_inc(s[sem], 1)

                e.wait_ge(s["early"], 16)
                blocks(kT, prm["pe_k"][0:NDK, :], xk, "xk")
                blocks(vT, prm["pe_v"][0:NDV, :], xv, "xv")
                e.wait_ge(s["gate"], 1)
                e.tensor_scalar(gates[:, :, :], gates[:, :, :], 0.5, 0.5, ALU.mult, ALU.add).then_inc(s["gate2"], 1)
                e.wait_ge(s["gate2"], 1)
                cg = gates[:, 0, :].rearrange("p (h b) -> p h b", b=3)[:, :, 0]
                e.tensor_scalar(cg, cg, C["cmp_valid"], None, ALU.mult)
                for n in bg.branches:
                    bg.product(e, n)
    retire(nc, s)


def nsa_heads(nc, C, W, grp, stream, jobs, sums):
    s = phase(nc, Background.SEMS + ["q", "v", "vcs", "bias", "biasc", "gst", "sc", "scw", "scc", "lg", "lgw", "mx", "ex", "rc", "rg", "pn", "tr",
                   "pts", "ptc", "ptw", "o", "ohi", "olo"])
    ps = C["ps"]
    bg = Background(C, s, *stream, jobs, sums, [ps[2]])
    late, kcT, vnat, vc, gates = (W[n] for n in ("late", "kcT", "vnat", "vc", "gates"))
    qs, vs, vcs, bs, bcs, gs, lg, st, pt = (W[n] for n in ("qs", "vs", "vcs", "bs", "bcs", "gs", "lg", "st", "pt"))
    o_hi, o_lo = W["o_hi"], W["o_lo"]
    scale = NDK ** -0.5
    items = [(hh, t) for hh in range(HPG) for t in range(NT)]
    one = lambda ap, pat, **k: ap.rearrange(pat, **k)
    BR = 3
    with nc.Block() as block:
        @block.gpsimd
        def _(e):
            e.tensor_copy(vs[:, :, :, :], vnat[:, :, bass.ds(grp, 1), :, :].rearrange("p b a t d -> p b (a t) d")).then_inc(s["v"], 1)
            e.tensor_copy(vcs[:, :], vc[:, bass.ds(grp, 1), :].rearrange("p a d -> p (a d)")).then_inc(s["vcs"], 1)
            for j in range(1, bg.n + 1):
                bg.lo(e, j)
                if j >= 2 and jobs[j - 2][5] and bg.sum_of[j - 2] in bg.branches:
                    bg.add(e, bg.sum_of[j - 2])
            for n in bg.branches[-1:]:
                bg.add(e, n)

        @block.sync
        def _(e):
            e.dma_start(bs[:, :, :], W["bias"][bass.ds(grp, 1)].rearrange("a p h n -> (a p) h n")).then_inc(s["bias"], 16)
            e.dma_start(bcs[:, :, :], W["biasc"][bass.ds(grp, 1)].rearrange("a p h n -> (a p) h n")).then_inc(s["biasc"], 16)
            bg.loads(e)

        @block.tensor
        def _(e):
            def scores(i):
                hh, t = items[i]
                w = (t + 1) * P
                if i == 0:
                    e.wait_ge(s["q"], 1)
                lhs = qs[:, hh, t * P:(t + 1) * P]
                if i:
                    e.wait_ge(s["lg"], BR * (i - 1) + 1)
                if i >= 2:
                    e.wait_ge(s["ptc"], i - 1)
                e.matmul(ps[5][:, P:P + NCMP], lhs, kcT[:, bass.ds(grp, 1), :].rearrange("p a n -> p (a n)"),
                         start=True, stop=True).then_inc(s["sc"], 1)
                for b in range(2):
                    if i:
                        e.wait_ge(s["lg"], BR * (i - 1) + b + 2)
                    k = late[:, bass.ds(grp + (NSA_H + NSA_G * b), 1), 0:w].rearrange("p a n -> p (a n)")
                    e.matmul(ps[b][:, 0:w], lhs, k, start=True, stop=True).then_inc(s["sc"], 1)
            def values(i):
                hh, t = items[i]
                w = (t + 1) * P
                for b in (1, 2, 0):
                    e.wait_ge(s["pn"], BR * i + b + 1)
                    if i:
                        e.wait_ge(s[("ptc", "pts", "ptw")[b]], i)
                    if b:
                        for j in range(t + 1):
                            ins = e.transpose(ps[2 + b][:, j * P:(j + 1) * P], lg[:, i % 2, b, j * P:(j + 1) * P], C["ident"])
                    else:
                        if i + 1 < len(items):
                            e.wait_ge(s["lg"], BR * (i + 1) + 1)
                        ins = e.transpose(ps[5][0:NCMP, 0:P], lg[:, i % 2, b, 0:NCMP], C["ident"])
                    ins.then_inc(s["tr"], 1)
                if i == 0:
                    e.wait_ge(s["v"], 1)
                    e.wait_ge(s["vcs"], 1)
                if i >= 2:
                    e.wait_ge(s["olo"], i - 1)
                out = ps[6 + i % 2][(hh % 2) * NDV:(hh % 2 + 1) * NDV, 0:P]
                e.wait_ge(s["pts"], i + 1)
                for j in range(t + 1):
                    e.matmul(out, vs[:, 0, j, :], pt[:, 0, j * P:(j + 1) * P], start=(j == 0), stop=False)
                e.wait_ge(s["ptw"], i + 1)
                for j in range(t + 1):
                    e.matmul(out, vs[:, 1, j, :], pt[:, 1, j * P:(j + 1) * P], start=False, stop=False)
                e.wait_ge(s["ptc"], i + 1)
                e.matmul(out, vcs[:, :], pt[0:NCMP, 2, 0:P], start=False, stop=True).then_inc(s["o"], 1)

            bg.mm(e, 0)
            scores(0)
            for i in range(len(items)):
                if i + 1 < len(items):
                    scores(i + 1)
                bg.mm(e, i + 1)
                values(i)
            for j in range(len(items) + 1, len(jobs)):
                bg.mm(e, j)

        @block.vector
        def _(e):
            e.tensor_copy(gs[:, :, :], gates[:, :, bass.ds(3 * HPG * grp, 3 * HPG)]).then_inc(s["gst"], 1)
            e.wait_ge(s["bias"], 16)
            e.wait_ge(s["biasc"], 16)
            e.wait_ge(s["gst"], 1)

            def logits(i):
                hh, t = items[i]
                w = (t + 1) * P
                if i >= 2:
                    e.wait_ge(s["tr"], BR * (i - 1))
                for b in range(BR):
                    e.wait_ge(s["sc"], BR * i + b + 1)
                    n = w if b else NCMP
                    bb = bs[:, hh, S - w:S] if b else bcs[:, hh, (NT - 1 - t) * NCMP:(NT - t) * NCMP]
                    sc = ps[b - 1][:, 0:n] if b else ps[5][:, P:P + n]
                    e.scalar_tensor_tensor(out=lg[:, i % 2, b, 0:n], in0=sc, scalar=scale, in1=bb,
                                           op0=ALU.mult, op1=ALU.add).then_inc(s["lg"], 1)
                for b in range(BR):
                    n = w if b else NCMP
                    e.wait_ge(s["lg"], BR * i + b + 1)
                    e.tensor_reduce(st[:, i % 2, b:b + 1], lg[:, i % 2, b, 0:n], AX, ALU.max, negate=True).then_inc(s["mx"], 1)

            def normalise(i):
                hh, t = items[i]
                w = (t + 1) * P
                e.wait_ge(s["ex"], BR * (i + 1))
                e.reciprocal(st[:, i % 2, 8:11], st[:, i % 2, 4:7]).then_inc(s["rc"], 1)
                e.wait_ge(s["rc"], i + 1)
                e.tensor_tensor(st[:, i % 2, 12:15], st[:, i % 2, 8:11], gs[:, t, 3 * hh:3 * hh + 3], ALU.mult).then_inc(s["rg"], 1)
                e.wait_ge(s["rg"], i + 1)
                for b in range(BR):
                    n = w if b else NCMP
                    e.tensor_scalar(lg[:, i % 2, b, 0:n], lg[:, i % 2, b, 0:n], st[:, i % 2, 12 + b:13 + b], None, ALU.mult).then_inc(s["pn"], 1)

            def window_probs(i):
                hh, t = items[i]
                w = (t + 1) * P
                e.wait_ge(s["tr"], BR * i + 2)
                if i:
                    e.wait_ge(s["o"], i)
                e.tensor_copy(pt[:, 1, 0:w], ps[4][:, 0:w]).then_inc(s["ptw"], 1)

            def out_lo(i):
                hh, t = items[i]
                rows = slice((hh % 2) * NDV, (hh % 2 + 1) * NDV)
                e.wait_ge(s["ohi"], i + 1)
                dst = bass.ds(2 * grp + hh // 2, 1)
                e.tensor_tensor(o_lo[rows, dst, t * P:(t + 1) * P].rearrange("p a n -> p (a n)"), ps[6 + i % 2][rows, 0:P],
                                o_hi[rows, dst, t * P:(t + 1) * P].rearrange("p a n -> p (a n)").bitcast(F32), ALU.subtract).then_inc(s["olo"], 1)

            logits(0)
            for i in range(len(items)):
                normalise(i)
                if i + 1 < len(items):
                    logits(i + 1)
                window_probs(i)
                if i:
                    out_lo(i - 1)
                if jobs[i + 1][5] and bg.sum_of[i + 1] in bg.branches:
                    bg.product(e, bg.sum_of[i + 1])
            out_lo(len(items) - 1)
            bg.product(e, bg.branches[-1])

        @block.scalar
        def _(e):
            e.copy(qs[:, :, :], late[:, bass.ds(HPG * grp, HPG), :]).then_inc(s["q"], 1)
            bg.hi(e, 1)
            bg.hi(e, 2)

            def exps(i):
                hh, t = items[i]
                w = (t + 1) * P
                for b in range(BR):
                    n = w if b else NCMP
                    e.wait_ge(s["mx"], BR * i + b + 1)
                    e.activation(lg[:, i % 2, b, 0:n], lg[:, i % 2, b, 0:n], ACT.Exp, bias=st[:, i % 2, b:b + 1],
                                 accum_out=st[:, i % 2, 4 + b:5 + b]).then_inc(s["ex"], 1)

            def probs(i):
                hh, t = items[i]
                w = (t + 1) * P
                e.wait_ge(s["tr"], BR * i + 1)
                if i:
                    e.wait_ge(s["o"], i)
                e.copy(pt[:, 0, 0:w], ps[3][:, 0:w]).then_inc(s["pts"], 1)
                e.wait_ge(s["tr"], BR * i + 3)
                e.copy(pt[0:NCMP, 2, 0:P], ps[5][0:NCMP, 0:P]).then_inc(s["ptc"], 1)

            def out_hi(i):
                hh, t = items[i]
                rows = slice((hh % 2) * NDV, (hh % 2 + 1) * NDV)
                e.wait_ge(s["o"], i + 1)
                dst = bass.ds(2 * grp + hh // 2, 1)
                e.copy(o_hi[rows, dst, t * P:(t + 1) * P].rearrange("p a n -> p (a n)"), ps[6 + i % 2][rows, 0:P]).then_inc(s["ohi"], 1)

            exps(0)
            for i in range(len(items)):
                if i + 1 < len(items):
                    exps(i + 1)
                bg.hi(e, i + 3)
                if jobs[i + 1][5]:
                    bg.out(e, bg.sum_of[i + 1])
                probs(i)
                out_hi(i)
            bg.stored(e)
    retire(nc, s)


def nsa(nc, C, prm, l, wd, h_hi, h_lo, miscT, nsa_rows, gla_rows, bias, biasc, d_hi, d_lo, o_hi, o_lo):

    def merge(chunk):
        return merge_jobs(h_hi, h_lo, d_hi, d_lo, chunk, True)

    with ExitStack() as ctx:
        sb = lambda n, shape: ctx.enter_context(sbuf(nc, n, shape, F32))
        W = {"o_hi": o_hi, "o_lo": o_lo, "bias": bias, "biasc": biasc}
        vnat = W["vnat"] = sb("nsa_vnat", [P, 2, NSA_G, NT, NDV])
        kcT = W["kcT"] = sb("nsa_kcT", [NDK, NSA_G, NCMP])
        vc = W["vc"] = sb("nsa_vc", [NCMP, NSA_G, NDV])
        gates = W["gates"] = sb("nsa_gates", [P, NT, 3 * NSA_H])
        with ExitStack() as c2:
            early = c2.enter_context(sbuf(nc, "nsa_early", [NDK, NSA_CHUNKS - NSA_LATE, S], F32))
            jobs, sums = [], []
            for c in range(4):
                j, m = merge(4 + c)
                jobs, sums = jobs + j, sums + m
            nsa_compress(nc, C, prm, l, wd, nsa_rows, early, miscT, gates, vnat, kcT, vc,
                         (wd["w_stream"], l, FIRST_JOB["compress"]), jobs, sums)
        with ExitStack() as c2:
            late = W["late"] = c2.enter_context(sbuf(nc, "nsa_late", [NDK, NSA_LATE, S], F32))
            load(nc, late[:, :, :], nsa_rows[0:NSA_LATE].rearrange("c p n -> p c n"))
            for n, shape in (("qs", [NDK, HPG, S]), ("vs", [P, 2, NT, NDV]), ("vcs", [NCMP, NDV]), ("bs", [P, HPG, S]),
                             ("bcs", [P, HPG, NT * NCMP]), ("gs", [P, NT, 3 * HPG]), ("lg", [P, 2, 3, S]), ("st", [P, 2, 16]),
                             ("pt", [P, 3, S])):
                W[n] = c2.enter_context(sbuf(nc, "nsa_" + n, shape, F32))
            with nc.Fori(0, NSA_G) as grp:
                jobs, sums = [], []
                for pr in range(2):
                    for c in range(3):
                        jobs += column_jobs(P, h_hi, h_lo)
                        sums.append(("store", gla_rows[bass.ds(6 * grp + (3 * pr + c), 1)].rearrange("a p n -> (a p) n")))
                    j, m = merge(2 * grp + pr)
                    jobs, sums = jobs + j, sums + m
                nsa_heads(nc, C, W, grp, (wd["w_stream"], l, len(jobs) * grp + FIRST_JOB["heads"]), jobs, sums)


def gla_prepare(nc, C, prm, miscT, pT, q1, k1, qd, kd, ebc, stream, jobs, sums):
    s = phase(nc, Background.SEMS + ["lg", "x", "nx", "m", "ex", "ln", "ls", "cs", "d", "e", "q"])
    ps = C["ps"]
    bg = Background(C, s, *stream, jobs, sums, ps[2:6])
    NC_ = S // GLA_C
    with ExitStack() as ctx:
        sb = lambda n: ctx.enter_context(sbuf(nc, n, [P, 2, S], F32))
        x, y = sb("gla_x"), sb("gla_y")
        V = lambda ap: ap.rearrange("p a (n c) -> p (a n) c", c=GLA_C)
        at = lambda ap, i: V(ap)[:, :, i:i + 1].to_broadcast([P, 2 * NC_, GLA_C])
        with nc.Block() as block:
            @block.tensor
            def _(e):
                for c in range(2):
                    ins = e.matmul(ps[c][:, :], prm["gla_w"][64:80, c * P:(c + 1) * P], miscT[64:80, :], start=True, stop=True)
                ins.then_inc(s["lg"], 1)
                for j in range(bg.n):
                    bg.mm(e, j)

            @block.sync
            def _(e):
                bg.loads(e)

            @block.gpsimd
            def _(e):
                for j in range(1, bg.n + 1):
                    bg.lo(e, j)

            @block.vector
            def _(e):
                e.wait_ge(s["lg"], 1)
                for c in range(2):
                    e.tensor_scalar(x[:, c, :], ps[c][:, :], prm["gla_b"][:, c:c + 1], None, ALU.add).then_inc(s["x"], 1)
                e.wait_ge(s["x"], 2)
                e.tensor_scalar(y[:, :, :], x[:, :, :], -1.0, None, ALU.mult).then_inc(s["nx"], 1)
                e.wait_ge(s["nx"], 1)
                e.tensor_tensor(y[:, :, :], y[:, :, :], x[:, :, :], ALU.min).then_inc(s["m"], 1)
                e.wait_ge(s["ln"], 1)
                e.scalar_tensor_tensor(out=x[:, :, :], in0=x[:, :, :], scalar=0.0, in1=y[:, :, :], op0=ALU.min, op1=ALU.subtract).then_inc(s["ls"], 1)
                e.wait_ge(s["ls"], 1)
                e.tensor_scalar(x[:, :, :], x[:, :, :], 1.0 / GLA_TAU, None, ALU.mult).then_inc(s["cs"], 1)
                a, b, n = x, y, 1
                for sh in (1, 2, 4, 8):
                    e.wait_ge(s["cs"], n)
                    e.tensor_tensor(V(b[:, :, :])[:, :, sh:], V(a[:, :, :])[:, :, sh:], V(a[:, :, :])[:, :, :GLA_C - sh], ALU.add).then_inc(s["cs"], 1)
                    e.tensor_copy(V(b[:, :, :])[:, :, :sh], V(a[:, :, :])[:, :, :sh]).then_inc(s["cs"], 1)
                    a, b, n = b, a, n + 2
                e.wait_ge(s["cs"], n)
                bc = x
                e.tensor_tensor(V(q1[:, :, :]), V(bc[:, :, :]), at(bc[:, :, :], 7), ALU.subtract).then_inc(s["d"], 1)
                e.tensor_tensor(V(k1[:, :, :]), at(bc[:, :, :], 7), V(bc[:, :, :]), ALU.subtract).then_inc(s["d"], 1)
                e.tensor_tensor(V(kd[:, :, :]), at(bc[:, :, :], 15), V(bc[:, :, :]), ALU.subtract).then_inc(s["d"], 1)
                e.wait_ge(s["d"], 2)
                e.tensor_scalar(q1[:, :, :], q1[:, :, :], GLA_GUARD, None, ALU.min).then_inc(s["d"], 1)
                e.tensor_scalar(k1[:, :, :], k1[:, :, :], GLA_GUARD, None, ALU.min).then_inc(s["d"], 1)
                sc = (P // 2) ** -0.5
                e.wait_ge(s["e"], 4)
                e.scalar_tensor_tensor(out=q1[:, :, :], in0=pT[:, 0:2, :], scalar=sc, in1=q1[:, :, :], op0=ALU.mult, op1=ALU.mult)
                e.tensor_tensor(k1[:, :, :], pT[:, 2:4, :], k1[:, :, :], ALU.mult)
                e.tensor_tensor(kd[:, :, :], pT[:, 2:4, :], kd[:, :, :], ALU.mult)
                e.scalar_tensor_tensor(out=qd[:, :, :], in0=pT[:, 0:2, :], scalar=sc, in1=ebc[:, :, :], op0=ALU.mult, op1=ALU.mult)

            @block.scalar
            def _(e):
                bg.hi(e, 1)
                bg.hi(e, 2)
                e.wait_ge(s["m"], 1)
                e.activation(y[:, :, :], y[:, :, :], ACT.Exp).then_inc(s["ex"], 1)
                e.wait_ge(s["ex"], 1)
                e.activation(y[:, :, :], y[:, :, :], ACT.Ln, bias=C["one"]).then_inc(s["ln"], 1)
                bg.hi(e, 3)
                bg.hi(e, 4)
                bg.out(e, 0)
                bg.hi(e, 5)
                e.wait_ge(s["cs"], 9)
                e.activation(ebc[:, :, :], x[:, :, :], ACT.Exp).then_inc(s["e"], 1)
                bg.hi(e, 6)
                bg.out(e, 1)
                e.wait_ge(s["d"], 5)
                e.activation(kd[:, :, :], kd[:, :, :], ACT.Exp).then_inc(s["e"], 1)
                e.activation(q1[:, :, :], q1[:, :, :], ACT.Exp).then_inc(s["e"], 1)
                e.activation(k1[:, :, :], k1[:, :, :], ACT.Exp).then_inc(s["e"], 1)
                bg.hi(e, 7)
                bg.hi(e, 8)
                bg.out(e, 2)
                bg.out(e, 3)
                bg.stored(e)
    retire(nc, s)


def gla_tile(nc, C, W, t, stream, jobs, sums):
    s = phase(nc, Background.SEMS + ["k1", "kd", "vt", "qd", "eb", "trk", "trv", "kn", "vn", "at", "ats", "kv", "S", "o", "carry", "os", "q1"])
    ps = C["ps"]
    H = GLA_H
    cols = bass.ts(t, P)
    HB = lambda ap: ap.rearrange("p (h c) -> p h c", c=P)
    k1t, q1t, kdt, qdt, vt, ebt, kn, vn, at, SS = (W[n] for n in ("k1t", "q1t", "kdt", "qdt", "vt", "ebt", "kn", "vn", "at", "SS"))
    bg = Background(C, s, *stream, jobs, sums, [ps[7], ps[1]])
    kv_bank = [ps[4], ps[5], ps[6], ps[0]]
    NCH = P // GLA_C
    half = lambda h: slice((h % 2) * 64, (h % 2) * 64 + 64)
    with nc.Block() as block:
        @block.sync
        def _(e):
            bg.loads(e)

        @block.gpsimd
        def _(e):
            for j in range(1, 6):
                bg.lo(e, j)
            bg.add(e, bg.branches[0])
            bg.lo(e, 6)
            bg.add(e, bg.branches[1])

        @block.vector
        def _(e):
            e.tensor_copy(q1t[:, :, :], W["q1"][:, :, cols]).then_inc(s["q1"], 1)
            e.tensor_copy(qdt[:, :, :], W["qd"][:, :, cols]).then_inc(s["qd"], 1)
            e.tensor_copy(ebt[:, :, :], W["ebc"][:, :, cols]).then_inc(s["eb"], 1)
            e.wait_ge(s["trk"], 1)
            for par in range(2):
                e.tensor_scalar(kn[:, par, :], ps[0][:, 0:2 * P], C["parity"][:, par:par + 1], None, ALU.mult).then_inc(s["kn"], 1)
            e.wait_ge(s["at"], 1)
            for par in range(2):
                e.tensor_tensor(at[:, par, :, :], HB(ps[2 + par][:, 0:2 * P]), C["tri16"].unsqueeze(1).to_broadcast([P, 2, P]),
                                ALU.mult).then_inc(s["ats"], 1)
            e.wait_ge(s["eb"], 1)
            for c in range(NCH):
                e.wait_ge(s["kv"], 2 * (c // 2) + 2)
                if c:
                    e.wait_ge(s["S"], 2 * c)
                for p in range(2):
                    last = (c + 1) * GLA_C - 1
                    e.scalar_tensor_tensor(out=SS[:, c + 1, p, :], in0=SS[:, c, p, :], scalar=ebt[:, p, last:last + 1],
                                           in1=kv_bank[c // 2][:, (2 * (c % 2) + p) * P:(2 * (c % 2) + p + 1) * P],
                                           op0=ALU.mult, op1=ALU.add).then_inc(s["S"], 1)
            for n in bg.branches:
                bg.product(e, n)
            e.wait_ge(s["S"], 2 * NCH)
            e.wait_ge(s["o"], 1)
            e.tensor_copy(SS[:, 0, :, :], SS[:, NCH, :, :]).then_inc(s["carry"], 1)

        @block.scalar
        def _(e):
            e.copy(kdt[:, :, :], W["kd"][:, :, cols]).then_inc(s["kd"], 1)
            e.copy(vt[:, :, :], W["pT"][:, 4:8, cols]).then_inc(s["vt"], 1)
            e.copy(k1t[:, :, :], W["k1"][:, :, cols]).then_inc(s["k1"], 1)
            bg.hi(e, 1)
            e.wait_ge(s["trv"], 1)
            e.copy(vn[:, :, :], HB(ps[1][:, :])).then_inc(s["vn"], 1)
            bg.hi(e, 2)
            bg.hi(e, 3)
            bg.out(e, 0)
            for j in range(4, 7):
                bg.hi(e, j)
            bg.out(e, 2)
            e.wait_ge(s["o"], 1)
            for par in range(2):
                e.copy(W["o_raw"][:, :, cols].rearrange("p (a b) n -> p b a n", b=2)[:, par, :, :], HB(ps[2 + par][:, 0:2 * P])).then_inc(s["os"], 1)

        @block.tensor
        def _(e):
            bg.mm(e, 0)
            e.wait_ge(s["kd"], 1)
            for p in range(2):
                ins = e.transpose(ps[0][:, p * P:(p + 1) * P], kdt[:, p, :], C["ident"])
            ins.then_inc(s["trk"], 1)
            e.wait_ge(s["vt"], 1)
            for h in range(H):
                ins = e.transpose(HB(ps[1][:, :])[:, h, :], vt[:, h, :], C["ident"])
            ins.then_inc(s["trv"], 1)
            e.wait_ge(s["k1"], 1)
            e.wait_ge(s["q1"], 1)
            for h in range(H):
                ins = e.matmul(HB(ps[2 + h % 2][:, :])[:, h // 2, :], k1t[half(h), h // 2, :], q1t[half(h), h // 2, :], start=True, stop=True)
            ins.then_inc(s["at"], 1)
            bg.mm(e, 1)
            e.wait_ge(s["kn"], 2)
            e.wait_ge(s["vn"], 1)
            for c in range(NCH):
                rows = slice(32 * (c // 2), 32 * (c // 2) + 32)
                for h in range(H):
                    col = (2 * (c % 2) + h // 2) * P
                    ins = e.matmul(kv_bank[c // 2][half(h), col:col + P], kn[rows, c % 2, h * 64:(h + 1) * 64], vn[rows, h, :],
                                   start=True, stop=True)
                ins.then_inc(s["kv"], 1)
            for j in range(2, 6):
                bg.mm(e, j)
            e.wait_ge(s["ats"], 2)
            e.wait_ge(s["qd"], 1)
            e.wait_ge(s["S"], 2 * NCH - 2)
            for h in range(H):
                out = HB(ps[2 + h % 2][:, :])[:, h // 2, :]
                for c in range(NCH):
                    cc = slice(c * GLA_C, (c + 1) * GLA_C)
                    e.matmul(out[:, cc], SS[half(h), c, h // 2, :], qdt[half(h), h // 2, cc], start=(c == 0), stop=False,
                             skip_group_check=True)
                ins = e.matmul(out, vn[:, h, :], at[:, h % 2, h // 2, :], start=False, stop=True, skip_group_check=True)
            ins.then_inc(s["o"], 1)
    retire(nc, s)


def gla(nc, C, prm, l, wd, h_hi, h_lo, miscT, gla_rows, gla_gates, n_hi, n_lo, o_hi, o_lo):
    with ExitStack() as ctx:
        sb = lambda n, shape: ctx.enter_context(sbuf(nc, n, shape, F32))
        W = {}
        pT = W["pT"] = sb("gla_pT", [P, 12, S])
        o_raw = W["o_raw"] = sb("gla_o", [P, GLA_H, S])
        load(nc, pT[:, :, :], gla_rows.rearrange("c p n -> p c n"))
        with ExitStack() as c2:
            for n, shape in (("q1", [P, 2, S]), ("k1", [P, 2, S]), ("qd", [P, 2, S]), ("kd", [P, 2, S]), ("ebc", [P, 2, S])):
                W[n] = c2.enter_context(sbuf(nc, "gla_" + n, shape, F32))
            jobs, sums = [], []
            for c in range(4, KD):
                jobs += column_jobs(P, h_hi, h_lo)
                sums.append(("tanh", gla_gates[c]))
            gla_prepare(nc, C, prm, miscT, pT, W["q1"], W["k1"], W["qd"], W["kd"], W["ebc"],
                        (wd["w_stream"], l, FIRST_JOB["gla_prepare"]), jobs, sums)
            for n, shape in (("k1t", [P, 2, P]), ("q1t", [P, 2, P]), ("kdt", [P, 2, P]), ("qdt", [P, 2, P]), ("vt", [P, 4, P]),
                             ("ebt", [P, 2, P]), ("kn", [P, 2, 2 * P]), ("vn", [P, 4, P]), ("at", [P, 2, 2, P]), ("SS", [P, 9, 2, P])):
                W[n] = c2.enter_context(sbuf(nc, "gla_" + n, shape, F32))
            zero(nc, W["SS"][:, 0, :, :])
            with nc.Fori(0, NT) as t:
                jobs, sums = [], []
                for c in range(2):
                    chunk = 2 * t + c
                    j, m = merge_jobs(h_hi, h_lo, n_hi, n_lo, chunk, False)
                    jobs, sums = jobs + j, sums + m
                gla_tile(nc, C, W, t, (wd["w_stream"], l, len(jobs) * t + FIRST_JOB["gla"]), jobs, sums)
        gated_output(nc, C, o_raw, pT[:, 8:12, :], prm["gla_norm"], o_hi, o_lo, (wd["w_stream"], l, FIRST_JOB["last"]), [], [])


def position_bias(nc, C, rel_bias, one_hot, scratch, bias_dram, biasc_dram):
    s = phase(nc, ["tb", "mask", "oh", "row", "rows", "st", "ld", "flip", "out"])
    ps = C["ps"]
    with ExitStack() as ctx:
        sb = lambda n, shape: ctx.enter_context(sbuf(nc, n, shape, F32))
        tbl = sb("pb_tbl", [BUCKETS + 1, NSA_H])
        oh = sb("pb_oh", [BUCKETS + 1, RLEN])
        row = sb("pb_row", [NSA_H, RLEN])
        wt = sb("pb_wt", [P, NSA_H, WLEN])
        bias = sb("pb_bias", [P, NSA_H, S])
        biasc = sb("pb_biasc", [P, NSA_H, NT * NCMP])
        with nc.Block() as block:
            @block.sync
            def _(e):
                e.dma_start(tbl[0:BUCKETS, :], rel_bias).then_inc(s["tb"], 16)
                e.dma_start(oh[:, :], one_hot).then_inc(s["oh"], 16)
                e.wait_ge(s["rows"], 2)
                e.dma_start(scratch, row[:, :]).then_inc(s["st"], 16)
                e.wait_ge(s["st"], 16)
                src = bass.AP(scratch.tensor, 0, [[1, P], [RLEN, NSA_H], [1, WLEN]])
                e.dma_start(wt[:, :, :], src).then_inc(s["ld"], 16)
                e.wait_ge(s["out"], 2 * NSA_H)
                e.dma_start(bias_dram.rearrange("c p h n -> p c h n"), bias[:, :, :].rearrange("p (c h) n -> p c h n", h=HPG)).then_inc(s["st"], 16)
                e.dma_start(biasc_dram.rearrange("c p h n -> p c h n"), biasc[:, :, :].rearrange("p (c h) n -> p c h n", h=HPG)).then_inc(s["st"], 16)
                e.wait_ge(s["st"], 48)

            @block.vector
            def _(e):
                e.memset(tbl[BUCKETS:BUCKETS + 1, :], MASKED).then_inc(s["mask"], 1)
                e.wait_ge(s["row"], 2)
                for c in range(2):
                    e.tensor_copy(row[:, c * S:(c + 1) * S], ps[c][0:NSA_H, :]).then_inc(s["rows"], 1)
                for h in range(NSA_H):
                    e.wait_ge(s["flip"], h + 1)
                    e.tensor_copy(bias[:, h, :], ps[2 + 2 * (h % 2)][:, :]).then_inc(s["out"], 1)
                    e.tensor_copy(biasc[:, h, :], ps[3 + 2 * (h % 2)][:, 0:NT * NCMP]).then_inc(s["out"], 1)

            @block.tensor
            def _(e):
                e.wait_ge(s["tb"], 16)
                e.wait_ge(s["mask"], 1)
                e.wait_ge(s["oh"], 16)
                for c in range(2):
                    e.matmul(ps[c][0:NSA_H, :], tbl[:, :], oh[:, c * S:(c + 1) * S], start=True, stop=True).then_inc(s["row"], 1)
                e.wait_ge(s["ld"], 16)
                for h in range(NSA_H):
                    if h >= 2:
                        e.wait_ge(s["out"], 2 * (h - 1))
                    e.matmul(ps[2 + 2 * (h % 2)][:, :], C["anti"], wt[:, h, 0:S], start=True, stop=True)
                    src = wt[:, h, CMP_LEN - 1:CMP_LEN - 1 + NT * P]
                    for q in range(NT):
                        a = CMP_LEN - 1 + q * P
                        ins = e.matmul(ps[3 + 2 * (h % 2)][:, q * NCMP:(q + 1) * NCMP], C["anti"],
                                       wt[:, h, a:a + (NCMP - 1) * CMP_STRIDE + 1:CMP_STRIDE], start=True, stop=True)
                    ins.then_inc(s["flip"], 1)
    retire(nc, s)


def trunk(nc, x_in, rel_bias, consts, one_hot, params, wd, out, scratch):
    with ExitStack() as ctx:
        sb = lambda n, shape: ctx.enter_context(sbuf(nc, n, shape, F32))
        x = sb("x", [P, NT, D])
        cst = sb("consts", [P, CONST_N])
        prm_t = sb("params", [P, PARAM_N])
        bias = nc.dram_tensor("bias", (NSA_G, P, HPG, S), F32, kind="Internal").ap()
        biasc = nc.dram_tensor("biasc", (NSA_G, P, HPG, NT * NCMP), F32, kind="Internal").ap()
        nsa_rows = nc.dram_tensor("nsa_rows", (NSA_CHUNKS, NDK, S), F32, kind="Internal").ap()
        gla_rows = nc.dram_tensor("gla_rows", (GLA_CHUNKS, P, S), F32, kind="Internal").ap()
        gla_gates = nc.dram_tensor("gla_gates", (KD, P, S), F32, kind="Internal").ap()
        ps = [ctx.enter_context(nc.psum_tensor(f"ps{i}", [P, S], F32)) for i in range(8)]
        C = {n: cst[:, a:b] for n, (a, b) in CONST_COLS.items()}
        C["x"], C["ps"] = x, ps
        s = phase(nc, ["x", "c"])
        with nc.Block() as block:
            @block.sync
            def _(e):
                e.dma_start(x[:, :, :], x_in.rearrange("b (t p) d -> p (b t) d", p=P)).then_inc(s["x"], 16)
                e.dma_start(cst[:, :], consts).then_inc(s["c"], 16)
                e.wait_ge(s["x"], 16)
                e.wait_ge(s["c"], 16)
        retire(nc, s)
        position_bias(nc, C, rel_bias, one_hot, scratch, bias, biasc)

        with nc.Fori(0, DEPTH) as l:
            s = phase(nc, ["p"])
            with nc.Block() as block:
                @block.sync
                def _(e):
                    e.dma_start(prm_t[:, :], params[l]).then_inc(s["p"], 16)
                    e.wait_ge(s["p"], 16)
            retire(nc, s)
            prm = {n: prm_t[:, a:b] for n, (a, b) in PARAM_COLS.items()}
            ffn(nc, C, l, prm["ffn1_pre"], wd["w_gu1"], wd["w_down1"], wd["post1"], )
            with ExitStack() as cm:
                merged = cm.enter_context(sbuf(nc, "merged", [P, KD, S], F32))
                with ExitStack() as ch:
                    h_hi = ch.enter_context(sbuf(nc, "m_h_hi", [P, KD, S], F32R))
                    h_lo = ch.enter_context(sbuf(nc, "m_h_lo", [P, KD, S], F32R))
                    miscT = ch.enter_context(sbuf(nc, "miscT", [80, S], F32))
                    ba = ch.enter_context(sbuf(nc, "misc", [P, NT, 80], F32))
                    o_hi = ch.enter_context(sbuf(nc, "o_hi", [P, 4, S], F32R))
                    o_lo = ch.enter_context(sbuf(nc, "o_lo", [P, 4, S], F32R))
                    C["merged"] = merged
                    C["bg"] = tuple(ch.enter_context(sbuf(nc, n, [P, 2, S], dt)) for n, dt in
                                    (("bg_raw", F32), ("bg_hi", F32R), ("bg_lo", F32R), ("bg_stage", F32))) + tuple(
                        ch.enter_context(sbuf(nc, n, [P, S], F32)) for n in ("bg_sg", "bg_pr"))
                    norm_transpose(nc, C, prm["mix_pre"], h_hi, h_lo)
                    gdn(nc, C, prm, l, wd, h_hi, h_lo, miscT, ba, o_hi, o_lo, nsa_rows, gla_gates)
                    with ExitStack() as cb:
                        n_hi = cb.enter_context(sbuf(nc, "n_hi", [P, 4, S], F32R))
                        n_lo = cb.enter_context(sbuf(nc, "n_lo", [P, 4, S], F32R))
                        nsa(nc, C, prm, l, wd, h_hi, h_lo, miscT, nsa_rows, gla_rows, bias, biasc, o_hi, o_lo, n_hi, n_lo)
                        gla(nc, C, prm, l, wd, h_hi, h_lo, miscT, gla_rows, gla_gates, n_hi, n_lo, o_hi, o_lo)
                    merge_last(nc, C, l, wd["w_stream"], gla_gates, o_hi, o_lo, h_hi, h_lo)
                    yT = ch.enter_context(sbuf(nc, "m_yT", [P, KD, S], F32))
                    contract(nc, C, l, wd["w_out"], KD, h_hi, h_lo, yT)
                    residual(nc, C, l, yT, wd["mix_post"], 1.0)
            ffn(nc, C, l, prm["ffn2_pre"], wd["w_gu2"], wd["w_down2"], wd["post2"])

        s = phase(nc, ["out"])
        with nc.Block() as block:
            @block.sync
            def _(e):
                e.dma_start(out.rearrange("b (t p) d -> p (b t) d", p=P), x[:, :, :]).then_inc(s["out"], 16)
                e.wait_ge(s["out"], 16)


def constants():
    import numpy as np
    c = np.zeros((P, CONST_N), np.float32)
    i, j = np.arange(P)[:, None], np.arange(P)[None, :]

    def put(name, v):
        a, b = CONST_COLS[name]
        c[:, a:b] = v

    put("ident", i == j)
    put("ones", 1.0)
    put("anti", i + j == P - 1)
    same64 = i // GDN_C == j // GDN_C
    put("tri64", (i <= j) & same64)
    put("blk64", same64)
    lv = [((i // (2 * b) == j // (2 * b)) & (i % (2 * b) >= b) & (j % (2 * b) < b)) for b in (1, 2, 4, 8, 16, 32)]
    put("lvl", np.concatenate(lv, 1))
    put("tri16", (i <= j) & (i // GLA_C == j // GLA_C))
    put("parity", np.concatenate([(i // GLA_C) % 2 == 0, (i // GLA_C) % 2 == 1], 1))
    put("cmp_valid", i >= CMP_LEN - 1)
    put("eps", EPS)
    put("gdn_eps", EPS)
    put("one", 1.0)
    put("lnq", 0.0)
    dist = S - 1 - np.arange(RLEN)
    n = np.maximum(dist, 0)
    exact = BUCKETS // 2
    large = exact + (np.log(np.maximum(n, 1).astype(np.float64) / exact) / np.log(128 / exact) * (BUCKETS - exact) + 1e-9).astype(np.int64)
    bucket = np.where(n < exact, n, np.minimum(large, BUCKETS - 1))
    oh = np.zeros((BUCKETS + 1, RLEN), np.float32)
    oh[bucket, np.arange(RLEN)] = dist >= 0
    oh[BUCKETS] = dist < 0
    return c, oh


def kernel(**inputs):
    import numpy as np
    import concourse.bacc as bacc
    from concourse import mybir as mb
    from concourse.bass_utils import run_bass_kernel_spmd as run

    a = {k: np.asarray(v) for k, v in inputs.items()}
    L = DEPTH
    c, oh = constants()

    def tiles(w, width):
        k, n = w.shape[1] // P, w.shape[2] // width
        return w.reshape(L, k, P, n, width).transpose(0, 3, 2, 1, 4).reshape(L, n, P, k * width)

    arrays = {"x": a["x"], "rel_bias": a["rel_bias"], "consts": c, "one_hot": oh}
    for f in ("1", "2"):
        gu = a[f"ffn{f}_w_gate_up"]
        g, u = tiles(gu[:, :, :FF], P), tiles(gu[:, :, FF:], P)
        arrays["w_gu" + f] = np.stack([g, u], 2)
        arrays["w_down" + f] = a[f"ffn{f}_w_down"].reshape(L, KF // 2, 2, P, D)
        arrays["post" + f] = a[f"ffn{f}_norm_post"].reshape(L, 1, D)
    arrays["w_out"] = a["w_out"].reshape(L, KD // 2, 2, P, D)
    arrays["mix_post"] = a["mix_norm_post"].reshape(L, 1, D)
    wi = a["w_in"]
    at = 0

    def take(n):
        nonlocal at
        at += n
        return wi[:, :, at - n:at]

    arrays["w_gdn"] = tiles(take(2048), P)
    w_ba = take(8)
    nq = take(NSA_H * NDK).reshape(L, D, NSA_H, NDK)
    kv = take(3 * NSA_G * (NDK + NDV)).reshape(L, D, 3 * NSA_G, NDK + NDV)
    nk, nv = kv[..., :NDK], np.zeros((L, D, 3 * NSA_G, NDK), np.float32)
    nv[..., :NDV] = kv[..., NDK:]
    streamed = {}
    streamed["nsa"] = tiles(np.concatenate([nq, nk[:, :, NSA_G:], nk[:, :, :NSA_G], nv], 2).reshape(L, D, -1), NDK)
    w_ng = take(3 * NSA_H)
    streamed["gla"] = tiles(take(1536), P)
    w_ga = take(16)
    misc = np.zeros((L, D, 80), np.float32)
    misc[:, :, 0:8], misc[:, :, 32:56], misc[:, :, 64:80] = w_ba, w_ng, w_ga
    arrays["w_misc"] = tiles(misc, 80)[:, 0]
    for b, name in enumerate(("gdn", "nsa", "gla")):
        streamed["gate", b] = tiles(take(D), P)
        streamed["branch", b] = tiles(a[f"w_branch_{name}"], P)
    arrays["w_stream"] = np.zeros((L, STREAM_N, P, HALF * P), np.float32)
    for j, (kind, n, part) in enumerate(STREAM):
        w = streamed[kind][:, n] if kind in ("nsa", "gla") else streamed[kind, n[0]][:, n[1]]
        cols = HALF * (NDK if kind == "nsa" else P)
        arrays["w_stream"][:, j, :, 0:cols] = w[:, :, part * cols:(part + 1) * cols]
    arrays["w_ck"] = a["nsa_cmp_k_w1"].reshape(L, CMP_LEN, NDK, CMP_HID).transpose(0, 2, 1, 3)
    arrays["w_cv"] = a["nsa_cmp_v_w1"].reshape(L, CMP_LEN, NDV, CMP_HID).transpose(0, 2, 1, 3)

    prm = np.zeros((L, P, PARAM_N), np.float32)

    def put(name, v, rows=slice(0, P)):
        lo, hi = PARAM_COLS[name]
        prm[:, rows, lo:hi] = v

    for name, key in (("ffn1_pre", "ffn1_norm_pre"), ("mix_pre", "mix_norm_pre"), ("ffn2_pre", "ffn2_norm_pre")):
        put(name, a[key].reshape(L, KD, P).transpose(0, 2, 1))
    put("conv", a["gdn_conv_w"].reshape(L, 4, 12, P).transpose(0, 3, 1, 2).reshape(L, P, 48))
    put("gdn_norm", a["gdn_norm_w"].reshape(L, P, 1))
    put("gla_norm", a["gla_norm_w"].reshape(L, P, 1))
    put("gla_b", a["gla_gate_b"].reshape(L, 2, P).transpose(0, 2, 1))
    put("pe_k", a["nsa_pe_k"].transpose(0, 2, 1), slice(0, NDK))
    put("pe_v", a["nsa_pe_v"].transpose(0, 2, 1), slice(0, NDV))
    put("gla_w", a["gla_gate_w"], slice(64, 80))
    put("a_log", a["gdn_a_log"].reshape(L, 1, 4))
    put("dt_bias", a["gdn_dt_bias"].reshape(L, 1, 4))
    put("w2k", a["nsa_cmp_k_w2"].reshape(L, 2, P, NDK).transpose(0, 2, 1, 3).reshape(L, P, -1))
    put("w2v", a["nsa_cmp_v_w2"].reshape(L, 2, P, NDV).transpose(0, 2, 1, 3).reshape(L, P, -1))
    arrays["params"] = prm

    nc = bacc.Bacc("TRN2", target_bir_lowering=False, num_devices=1)
    arrays = {"in_" + k: np.ascontiguousarray(v) for k, v in arrays.items()}
    t = {k[3:]: nc.dram_tensor(k, v.shape, mb.dt.from_np(v.dtype), kind="ExternalInput").ap() for k, v in arrays.items()}
    out = nc.dram_tensor("out", (1, S, D), F32, kind="ExternalOutput").ap()
    scratch = nc.dram_tensor("bias_rows", (NSA_H, RLEN), F32, kind="Internal").ap()
    trunk(nc, t["x"], t["rel_bias"], t["consts"], t["one_hot"], t["params"], t, out, scratch)
    return run(nc, [arrays], core_ids=[0]).results[0]["out"]
```

```python
from contextlib import ExitStack

import concourse.bass as bass
from concourse import mybir

F32 = mybir.dt.float32
F32R = mybir.dt.float32r
ALU = mybir.AluOpType
ACT = mybir.ActivationFunctionType
AX = mybir.AxisListType.X

P = 128
D = 1024
S = 512
DEPTH = 2
FF = 2816
NT = S // P
KD = D // P
KF = FF // P
EPS = 1e-6
MASKED = -1e30

GDN_H = 4
GDN_C = 64
NSA_H = 8
NSA_G = 2
HPG = NSA_H // NSA_G
NDK = 96
NDV = 64
NCMP = 31
CMP_LEN = 32
CMP_STRIDE = 16
CMP_HID = 256
GLA_H = 4
GLA_C = 16
GLA_TAU = 16.0
GLA_GUARD = 40.0
BUCKETS = 32
NSA_LATE = NSA_H + 2 * NSA_G
NSA_CHUNKS = NSA_H + 6 * NSA_G
GLA_CHUNKS = 12
RLEN = 1024
WLEN = RLEN - P

PARAM_COLS = {}
_at = 0
for _name, _n in (("ffn1_pre", KD), ("mix_pre", KD), ("ffn2_pre", KD), ("conv", 48), ("gdn_norm", 1),
                  ("gla_norm", 1), ("gla_b", 2), ("pe_k", CMP_LEN), ("pe_v", CMP_LEN), ("gla_w", 256),
                  ("a_log", 4), ("dt_bias", 4), ("w2k", 2 * NDK), ("w2v", 2 * NDV)):
    PARAM_COLS[_name] = (_at, _at + _n)
    _at += _n
PARAM_N = _at

CONST_COLS = {}
_at = 0
for _name, _n in (("ident", P), ("ones", P), ("anti", P), ("tri64", P), ("blk64", P), ("lvl", 6 * P),
                  ("tri16", P), ("parity", 2), ("cmp_valid", 1), ("eps", 1), ("one", 1)):
    CONST_COLS[_name] = (_at, _at + _n)
    _at += _n
CONST_N = _at


def sbuf(nc, name, shape, dtype):
    return nc.sbuf_tensor(f"{name}_{nc.next_id()}", shape, dtype)


def phase(nc, names):
    return {n: nc.alloc_semaphore(name=f"{n}_{nc.next_id()}") for n in names}


def retire(nc, sems):
    nums = sorted(s.num for s in sems.values())
    first = nums[0]
    for a, b in zip(nums, nums[1:] + [None]):
        if b != a + 1:
            nc.sync.sem_clear(range(first, a + 1))
            first = b
    nc.all_engine_barrier()
    for s in sems.values():
        nc.release_semaphore(s)


def load(nc, out, in_):
    s = phase(nc, ["load"])
    with nc.Block() as block:
        @block.sync
        def _(e):
            e.dma_start(out, in_).then_inc(s["load"], 16)
            e.wait_ge(s["load"], 16)
    retire(nc, s)


def zero(nc, ap):
    with nc.Block() as block:
        @block.vector
        def _(e):
            e.memset(ap, 0.0)


def mm3(e, out, w_hi, w_lo, m_hi, m_lo, start, stop):
    e.matmul(out, w_hi, m_hi, start=start, stop=False, skip_group_check=True)
    e.matmul(out, w_lo, m_hi, start=False, stop=False, skip_group_check=True)
    return e.matmul(out, w_hi, m_lo, start=False, stop=stop, skip_group_check=True)


HALF = 4
STREAM = []
FIRST_JOB = {}


def _stream():
    column = lambda kind, n: [(kind, n, i) for i in range(2)]
    gate = lambda b, chunk: [("gate", (b, chunk), i) for i in range(2)]
    merge = lambda b, chunk: gate(b, chunk) + [("branch", (b, chunk), 0)]
    heads = [j for half in range(4) for j in
             [x for c in range(3) for x in column("gla", 3 * half + c)] + merge(0, half)]
    for name, jobs in (("gdn_prepare", [x for c in range(3) for x in gate(2, c)]),
                       ("gdn", [x for n in range(NSA_CHUNKS) for x in column("nsa", n)]),
                       ("gdn_out", gate(2, 3)),
                       ("compress", [x for c in range(4, KD) for x in merge(0, c)]),
                       ("heads", heads),
                       ("gla_prepare", [x for c in range(4, KD) for x in gate(2, c)]),
                       ("gla", [x for c in range(KD) for x in merge(1, c)]),
                       ("last", [("branch", (2, c), 0) for c in range(KD)])):
        FIRST_JOB[name] = len(STREAM)
        STREAM.extend(jobs)


_stream()
STREAM_N = len(STREAM) + 2


class Background:

    SEMS = ["b_raw0", "b_raw1", "b_hi", "b_lo", "b_acc", "b_out", "b_pr", "b_add", "b_st0", "b_st1", "b_st2", "b_st3"]

    def __init__(self, C, s, w_stream, l, first_job, jobs, sums, banks, started=(2, 1)):
        self.C, self.s, self.jobs, self.sums, self.banks = C, s, jobs, sums, banks
        self.src = lambda j: w_stream[l, first_job + j]
        self.n = len(jobs)
        assert self.n % 2 == 0
        self.loaded, self.split = started
        self.raw, self.hi_, self.lo_, self.stage, self.sg, self.pr = C["bg"]
        self.merged = C["merged"]
        self.sum_of, n = [], 0
        for job in jobs:
            self.sum_of.append(n)
            n += job[5]
        self.branches = [n for n, x in enumerate(sums) if x[0] == "branch"]
        self.stores = [n for n, x in enumerate(sums) if x[0] in ("store", "tanh")]
        self.stages = [self.stage[:, 0, :], self.stage[:, 1, :]]
        if not self.branches:
            self.stages += [self.sg[:, :], self.pr[:, :]]

    def width(self, j):
        return HALF * (self.jobs[j][0] if j < self.n else P)

    def load(self, e, j):
        w = self.width(j)
        if j - 1 - self.split > 0:
            e.wait_ge(self.s["b_lo"], j - 1 - self.split)
        e.dma_start(self.raw[:, j % 2, 0:w], self.src(j)[:, 0:w]).then_inc(self.s[f"b_raw{j % 2}"], 16)

    def loads(self, e):
        for j in range(self.loaded, self.n + 2):
            self.load(e, j)
        self.loads_done(e)

    def loads_done(self, e):
        slot = (self.n + 1) % 2
        if n := (self.n + 1) // 2 + 1 - self.loaded // 2:
            e.wait_ge(self.s[f"b_raw{slot}"], 16 * n)

    def hi(self, e, j):
        n = self.width(j)
        if j >= self.loaded:
            e.wait_ge(self.s[f"b_raw{j % 2}"], 16 * (j // 2 + 1 - self.loaded // 2))
        if j >= 2:
            e.wait_ge(self.s["b_acc"], j - 1)
        e.copy(self.hi_[:, j % 2, 0:n], self.raw[:, j % 2, 0:n]).then_inc(self.s["b_hi"], 1)

    def lo(self, e, j):
        n = self.width(j)
        e.wait_ge(self.s["b_hi"], j + 1 - self.split)
        e.tensor_tensor(self.lo_[:, j % 2, 0:n], self.raw[:, j % 2, 0:n], self.hi_[:, j % 2, 0:n].bitcast(F32),
                        ALU.subtract).then_inc(self.s["b_lo"], 1)

    def bank(self, n):
        return self.banks[n % len(self.banks)]

    def mm(self, e, j, part=None):
        w, m_hi, m_lo, k0, first, last = self.jobs[j]
        if j >= self.split and part != 1:
            e.wait_ge(self.s["b_lo"], j + 1 - self.split)
        m = self.sum_of[j]
        if first and m >= len(self.banks) and part != 1:
            self._read(e, m - len(self.banks))
        for k in range(HALF // 2 if part == 1 else 0, HALF // 2 if part == 0 else HALF):
            ins = mm3(e, self.bank(m)[0:w, :], self.hi_[:, j % 2, k * w:(k + 1) * w], self.lo_[:, j % 2, k * w:(k + 1) * w],
                      m_hi[:, k0 + k, :], m_lo[:, k0 + k, :], first and k == 0, last and k == HALF - 1)
        if part != 0:
            ins.then_inc(self.s["b_acc"], 1)

    def _read(self, e, n):
        if n in self.branches:
            e.wait_ge(self.s["b_pr"], self.branches.index(n) + 1)
        else:
            e.wait_ge(self.s["b_out"], 1 + len([m for m in range(n) if m not in self.branches]))

    def _sum_ready(self, e, n):
        e.wait_ge(self.s["b_acc"], max(j for j, m in enumerate(self.sum_of) if m == n) + 1)

    def out(self, e, n):
        kind, dst = self.sums[n]
        if kind == "branch":
            return
        self._sum_ready(e, n)
        if kind == "gate":
            done = [b for b in self.branches if b < n]
            if done:
                e.wait_ge(self.s["b_pr"], len(done))
            e.activation(self.sg[:, :], self.bank(n)[:, :], ACT.Tanh, scale=0.5).then_inc(self.s["b_out"], 1)
        else:
            i = self.stores.index(n)
            slot, used = i % len(self.stages), i // len(self.stages)
            if used:
                e.wait_ge(self.s[f"b_st{slot}"], 16 * used)
            w = dst.shape[0]
            stage = self.stages[slot][0:w, :]
            if kind == "tanh":
                e.activation(stage, self.bank(n)[0:w, :], ACT.Tanh, scale=0.5).then_inc(self.s["b_out"], 1)
            else:
                e.copy(stage, self.bank(n)[0:w, :]).then_inc(self.s["b_out"], 1)
            self._read(e, n)
            e.dma_start(dst, stage).then_inc(self.s[f"b_st{slot}"], 16)

    def product(self, e, n):
        i = self.branches.index(n)
        first, chunk = self.sums[n][1]
        self._sum_ready(e, n)
        self._read(e, n - 1)
        out = self.pr[:, :]
        if first:
            out = self.merged[:, bass.ds(chunk, 1), :].rearrange("p a n -> p (a n)")
        elif i:
            e.wait_ge(self.s["b_add"], i)
        e.scalar_tensor_tensor(out=out, in0=self.sg[:, :], scalar=1.0, in1=self.bank(n)[:, :],
                               op0=ALU.add, op1=ALU.mult).then_inc(self.s["b_pr"], 1)

    def add(self, e, n):
        i = self.branches.index(n)
        first, chunk = self.sums[n][1]
        if first:
            return
        e.wait_ge(self.s["b_pr"], i + 1)
        m = self.merged[:, bass.ds(chunk, 1), :].rearrange("p a n -> p (a n)")
        e.tensor_tensor(m, m, self.pr[:, :], ALU.add).then_inc(self.s["b_add"], 1)

    def stored(self, e):
        for slot in range(len(self.stages)):
            if n := len(self.stores[slot::len(self.stages)]):
                e.wait_ge(self.s[f"b_st{slot}"], 16 * n)


def column_jobs(w, h_hi, h_lo):
    return [(w, h_hi, h_lo, i * HALF, i == 0, i == 1) for i in range(2)]


def merge_jobs(h_hi, h_lo, o_hi, o_lo, chunk, first):
    jobs = column_jobs(P, h_hi, h_lo) + [(P, o_hi, o_lo, 0, True, True)]
    return jobs, [("gate", None), ("branch", (first, chunk))]


def norm_transpose(nc, C, w_pre, h_hi, h_lo, raw, first):
    s = phase(nc, ["xn0", "xn1", "tr", "hi", "first0", "first1"])
    x, ps, rstd = C["x"], C["ps"], C["rstd"]
    with ExitStack() as ctx:
        xn = ctx.enter_context(sbuf(nc, "nt_xn", [P, NT, D], F32))
        with nc.Block() as block:
            @block.sync
            def _(e):
                load_first(e, s, raw, first)

            @block.scalar
            def _(e):
                for t in range(NT):
                    for half in range(2):
                        e.wait_ge(s["tr"], 2 * t + half + 1)
                        for b in range(4):
                            k = 4 * half + b
                            ins = e.mul(h_hi[:, k, t * P:(t + 1) * P], ps[2 * t + half][:, b * P:(b + 1) * P], w_pre[:, k:k + 1])
                        ins.then_inc(s["hi"], 1)

            @block.gpsimd
            def _(e):
                for t in range(1, NT, 2):
                    e.tensor_scalar(xn[:, t, :], x[:, t, :], rstd[:, t:t + 1], None, ALU.mult).then_inc(s["xn1"], 1)

            @block.vector
            def _(e):
                for t in range(0, NT, 2):
                    e.tensor_scalar(xn[:, t, :], x[:, t, :], rstd[:, t:t + 1], None, ALU.mult).then_inc(s["xn0"], 1)
                for t in range(NT):
                    for half in range(2):
                        e.wait_ge(s["hi"], 2 * t + half + 1)
                        for b in range(4):
                            k = 4 * half + b
                            e.scalar_tensor_tensor(out=h_lo[:, k, t * P:(t + 1) * P], in0=ps[2 * t + half][:, b * P:(b + 1) * P],
                                                   scalar=w_pre[:, k:k + 1], in1=h_hi[:, k, t * P:(t + 1) * P].bitcast(F32),
                                                   op0=ALU.mult, op1=ALU.subtract)

            @block.tensor
            def _(e):
                for t in range(NT):
                    e.wait_ge(s[f"xn{t % 2}"], t // 2 + 1)
                    for half in range(2):
                        for b in range(4):
                            k = 4 * half + b
                            ins = e.transpose(ps[2 * t + half][:, b * P:(b + 1) * P], xn[:, t, k * P:(k + 1) * P], C["ident"])
                        ins.then_inc(s["tr"], 1)
    retire(nc, s)


def raw_buffer(nc, ctx):
    return ctx.enter_context(sbuf(nc, "w_raw", [P, 2, D], F32))


def load_first(e, s, raw, first):
    for u in range(2):
        n = first[u].shape[-1]
        e.dma_start(raw[:, u, 0:n], first[u]).then_inc(s[f"first{u}"], 16)
    for u in range(2):
        e.wait_ge(s[f"first{u}"], 16)


def weight_buffers(nc, ctx):
    hi = ctx.enter_context(sbuf(nc, "w_hi", [P, 2, D], F32R))
    lo = ctx.enter_context(sbuf(nc, "w_lo", [P, 2, D], F32R))
    return hi, lo


def ffn_gate_up(nc, C, l, raw, w_gu, h_hi, h_lo, a_hi, a_lo, first):
    s = phase(nc, ["raw0", "raw1", "hi0", "hi1", "lo0", "lo1", "acc0", "acc1", "silu", "act", "ahi", "alo", "first0", "first1"])
    ps = C["ps"]
    with ExitStack() as ctx:
        hi, lo = weight_buffers(nc, ctx)
        sg = ctx.enter_context(sbuf(nc, "sg", [P, S], F32))
        a32 = ctx.enter_context(sbuf(nc, "a32", [P, S], F32))
        RAW, HI, LO, ACC = ([s[n + "0"], s[n + "1"]] for n in ("raw", "hi", "lo", "acc"))
        FREE = [s["silu"], s["act"]]
        with nc.Block() as block:
            @block.sync
            def _(e):
                for u in range(2):
                    e.sem_inc(RAW[u], 16)
                with e.Fori(1, KF) as it:
                    for u in range(2):
                        e.wait_ge(LO[u], it + 1)
                        e.dma_start(raw[:, u, :], w_gu[l, it, u]).then_inc(RAW[u], 16)
                for u in range(2):
                    e.wait_ge(LO[u], KF + 1)
                load_first(e, s, raw, first)

            @block.tensor
            def _(e):
                for u in range(2):
                    e.sem_inc(ACC[u], 1)
                with e.Fori(0, KF) as it:
                    for u in range(2):
                        e.wait_ge(HI[u], it + 1)
                        e.wait_ge(LO[u], it + 2)
                        e.wait_ge(FREE[u], it + 1)
                        for k in range(KD):
                            ins = mm3(e, ps[u][:, :], hi[:, u, k * P:(k + 1) * P], lo[:, u, k * P:(k + 1) * P],
                                      h_hi[:, k, :], h_lo[:, k, :], k == 0, k == KD - 1)
                        ins.then_inc(ACC[u], 1)

            @block.scalar
            def _(e):
                def split_hi(it, u):
                    e.wait_ge(RAW[u], 16 * (it + 1))
                    e.wait_ge(ACC[u], it + 1)
                    e.copy(hi[:, u, :], raw[:, u, :]).then_inc(HI[u], 1)

                e.sem_inc(s["silu"], 1)

                def silu(it):
                    e.wait_ge(ACC[0], it + 2)
                    e.wait_ge(s["act"], it + 1)
                    e.activation(sg[:, :], ps[0][:, :], ACT.Silu).then_inc(s["silu"], 1)

                def a_hi_copy(it):
                    e.wait_ge(s["act"], it + 2)
                    e.copy(a_hi[:, it, :], a32[:, :]).then_inc(s["ahi"], 1)

                split_hi(0, 0)
                split_hi(0, 1)
                with e.Fori(0, KF - 1) as it:
                    split_hi(it + 1, 0)
                    silu(it)
                    split_hi(it + 1, 1)
                    a_hi_copy(it)
                silu(KF - 1)
                a_hi_copy(KF - 1)

            @block.vector
            def _(e):
                for n in ("lo0", "lo1", "act", "alo"):
                    e.sem_inc(s[n], 1)

                def split_lo(it, u):
                    e.wait_ge(HI[u], it + 1)
                    e.tensor_tensor(lo[:, u, :], raw[:, u, :], hi[:, u, :].bitcast(F32), ALU.subtract).then_inc(LO[u], 1)

                def act(it):
                    e.wait_ge(ACC[1], it + 2)
                    e.wait_ge(s["silu"], it + 2)
                    e.wait_ge(s["alo"], it + 1)
                    e.tensor_tensor(a32[:, :], sg[:, :], ps[1][:, :], ALU.mult).then_inc(s["act"], 1)

                def a_lo_sub(it):
                    e.wait_ge(s["ahi"], it + 1)
                    e.tensor_tensor(a_lo[:, it, :], a32[:, :], a_hi[:, it, :].bitcast(F32), ALU.subtract).then_inc(s["alo"], 1)

                split_lo(0, 0)
                split_lo(0, 1)
                with e.Fori(0, KF - 1) as it:
                    split_lo(it + 1, 0)
                    act(it)
                    split_lo(it + 1, 1)
                    a_lo_sub(it)
                act(KF - 1)
                a_lo_sub(KF - 1)
    retire(nc, s)


def contract(nc, C, l, raw, w_rows, kc, m_hi, m_lo, w_post, res):
    s = phase(nc, ["raw0", "raw1", "hi0", "hi1", "lo0", "lo1", "used0", "used1", "wp", "wpr", "y0", "y1", "tr", "sq", "ss",
                   "sqrt", "rstd", "t", "x0", "x1", "ssx", "rsx"])
    ps, x, rstd_x = C["ps"], C["x"], C["rstd"]
    pairs = kc // 2
    with ExitStack() as ctx:
        hi, lo = weight_buffers(nc, ctx)
        yT = ctx.enter_context(sbuf(nc, "yT", [P, KD, S], F32))
        wp = ctx.enter_context(sbuf(nc, "y_wp", [P, 2, S], F32))
        junk = ctx.enter_context(sbuf(nc, "y_junk", [P, 4, S], F32))
        tmp = ctx.enter_context(sbuf(nc, "y_tmp", [P, 4, S], F32))
        ssq = ctx.enter_context(sbuf(nc, "y_ssq", [P, NT, 2], F32))
        rstd = ctx.enter_context(sbuf(nc, "y_rstd", [P, NT], F32))
        ssx = ctx.enter_context(sbuf(nc, "x_ssq", [P, NT], F32))
        RAW, HI, LO, USED = ([s[n + "0"], s[n + "1"]] for n in ("raw", "hi", "lo", "used"))
        with nc.Block() as block:
            @block.sync
            def _(e):
                for u in range(2):
                    e.sem_inc(RAW[u], 16)
                with e.Fori(1, pairs) as it:
                    for u in range(2):
                        e.wait_ge(LO[u], it + 1)
                        e.dma_start(raw[:, u, :], w_rows[l, it, u]).then_inc(RAW[u], 16)
                e.dma_start(wp[:, :, :].rearrange("p a n -> p (a n)"), w_post[l].partition_broadcast(P)).then_inc(s["wp"], 16)

            @block.gpsimd
            def _(e):
                for t in range(NT):
                    e.wait_ge(s["t"], 2 * t + 2)
                    e.tensor_tensor(x[:, t, S:D], x[:, t, S:D], tmp[:, (2 * t + 1) % 4, :], ALU.add).then_inc(s["x1"], 1)

            @block.scalar
            def _(e):
                with e.Fori(0, pairs) as it:
                    for u in range(2):
                        e.wait_ge(RAW[u], 16 * (it + 1))
                        e.wait_ge(USED[u], it + 1)
                        e.copy(hi[:, u, :], raw[:, u, :]).then_inc(HI[u], 1)
                e.wait_ge(USED[0], pairs + 1)
                e.wait_ge(USED[1], pairs + 1)
                for c in range(0, KD, 2):
                    e.copy(yT[:, c, :], ps[c][:, :]).then_inc(s["y0"], 1)

                def squares(t):
                    e.wait_ge(s["tr"], t + 1)
                    for half in range(2):
                        n = 2 * t + half
                        if n >= 2:
                            e.wait_ge(s["sq"], n - 1)
                        e.activation(junk[:, half, :], ps[n][:, :], ACT.Square, accum_out=ssq[:, t, half:half + 1]).then_inc(s["sq"], 1)

                def squares_x(t):
                    e.wait_ge(s["x0"], t + 1)
                    e.wait_ge(s["x1"], t + 1)
                    if t:
                        e.wait_ge(s["ssx"], t)
                    e.activation(junk[:, 2:4, :], x[:, t, :].rearrange("p (a n) -> p a n", a=2), ACT.Square,
                                 accum_out=ssx[:, t:t + 1]).then_inc(s["ssx"], 1)

                squares(0)
                for t in range(NT):
                    if t + 1 < NT:
                        squares(t + 1)
                    e.wait_ge(s["ss"], t + 1)
                    e.activation(rstd[:, t:t + 1], rstd[:, t:t + 1], ACT.Sqrt, bias=C["eps"], scale=1.0 / D).then_inc(s["sqrt"], 1)
                    if t >= 2:
                        squares_x(t - 2)
                squares_x(NT - 2)
                squares_x(NT - 1)
                e.wait_ge(s["ssx"], NT)
                e.activation(ssx[:, :], ssx[:, :], ACT.Sqrt, bias=C["eps"], scale=1.0 / D).then_inc(s["rsx"], 1)

            @block.vector
            def _(e):
                e.sem_inc(LO[0], 1)
                e.sem_inc(LO[1], 1)
                with e.Fori(0, pairs) as it:
                    for u in range(2):
                        e.wait_ge(HI[u], it + 1)
                        e.tensor_tensor(lo[:, u, :], raw[:, u, :], hi[:, u, :].bitcast(F32), ALU.subtract).then_inc(LO[u], 1)
                e.wait_ge(USED[0], pairs + 1)
                e.wait_ge(USED[1], pairs + 1)
                for c in range(1, KD, 2):
                    e.tensor_copy(yT[:, c, :], ps[c][:, :]).then_inc(s["y1"], 1)
                e.wait_ge(s["wp"], 16)
                e.tensor_scalar(wp[:, :, :], wp[:, :, :], res, None, ALU.mult).then_inc(s["wpr"], 1)

                def total(t):
                    e.wait_ge(s["sq"], 2 * t + 2)
                    e.tensor_tensor(rstd[:, t:t + 1], ssq[:, t, 0:1], ssq[:, t, 1:2], ALU.add).then_inc(s["ss"], 1)

                total(0)
                e.wait_ge(s["wpr"], 1)
                for t in range(NT):
                    if t + 1 < NT:
                        total(t + 1)
                    e.wait_ge(s["sqrt"], t + 1)
                    e.reciprocal(rstd[:, t:t + 1], rstd[:, t:t + 1]).then_inc(s["rstd"], 1)
                    e.wait_ge(s["rstd"], t + 1)
                    if t >= 2:
                        e.wait_ge(s["x0"], t - 1)
                        e.wait_ge(s["x1"], t - 1)
                    for half in range(2):
                        n = 2 * t + half
                        e.scalar_tensor_tensor(out=tmp[:, n % 4, :], in0=ps[n][:, :], scalar=rstd[:, t:t + 1], in1=wp[:, half, :],
                                               op0=ALU.mult, op1=ALU.mult).then_inc(s["t"], 1)
                    e.wait_ge(s["t"], 2 * t + 1)
                    e.tensor_tensor(x[:, t, 0:S], x[:, t, 0:S], tmp[:, 2 * t % 4, :], ALU.add).then_inc(s["x0"], 1)
                e.wait_ge(s["rsx"], 1)
                e.reciprocal(rstd_x[:, :], ssx[:, :])

            @block.tensor
            def _(e):
                e.sem_inc(USED[0], 1)
                e.sem_inc(USED[1], 1)

                def pair(it, first, last):
                    for u in range(2):
                        e.wait_ge(HI[u], it + 1)
                        e.wait_ge(LO[u], it + 2)
                        for c in range(KD):
                            ins = mm3(e, ps[c][:, :], hi[:, u, c * P:(c + 1) * P], lo[:, u, c * P:(c + 1) * P],
                                      m_hi[:, 2 * it + u, :], m_lo[:, 2 * it + u, :], first and u == 0, last and u == 1)
                        ins.then_inc(USED[u], 1)

                pair(0, True, False)
                with e.Fori(1, pairs - 1) as it:
                    pair(it, False, False)
                pair(pairs - 1, False, True)

                e.wait_ge(s["y0"], KD // 2)
                e.wait_ge(s["y1"], KD // 2)
                for t in range(NT):
                    for c in range(KD):
                        ins = e.transpose(ps[2 * t + c // 4][:, (c % 4) * P:(c % 4 + 1) * P], yT[:, c, t * P:(t + 1) * P], C["ident"])
                    ins.then_inc(s["tr"], 1)
    retire(nc, s)


def ffn(nc, C, l, w_pre, w_gu, w_down, w_post):
    with ExitStack() as outer:
        a_hi = outer.enter_context(sbuf(nc, "a_hi", [P, KF, S], F32R))
        a_lo = outer.enter_context(sbuf(nc, "a_lo", [P, KF, S], F32R))
        raw = raw_buffer(nc, outer)
        with ExitStack() as ctx:
            h_hi = ctx.enter_context(sbuf(nc, "h_hi", [P, KD, S], F32R))
            h_lo = ctx.enter_context(sbuf(nc, "h_lo", [P, KD, S], F32R))
            norm_transpose(nc, C, w_pre, h_hi, h_lo, raw, [w_gu[l, 0, u] for u in range(2)])
            ffn_gate_up(nc, C, l, raw, w_gu, h_hi, h_lo, a_hi, a_lo, [w_down[l, 0, u] for u in range(2)])
        contract(nc, C, l, raw, w_down, KF, a_hi, a_lo, w_post, 0.5)


def project(nc, C, raw, h_hi, h_lo, runs, first):
    s = phase(nc, ["raw0", "raw1", "hi0", "hi1", "lo0", "lo1", "acc0", "acc1", "free0", "free1", "first0", "first1"])
    ps = C["ps"]
    with ExitStack() as ctx:
        hi, lo = weight_buffers(nc, ctx)
        RAW, HI, LO, ACC, FREE = ([s[n + "0"], s[n + "1"]] for n in ("raw", "hi", "lo", "acc", "free"))

        def over(e, n, body, first=0):
            if n - first == 1:
                body(first)
            elif n > first:
                with e.Fori(first, n) as it:
                    body(it)

        def starts():
            seen, out = [0, 0], []
            for iters, widths, _, _ in runs:
                out.append(tuple(seen))
                for u in range(len(widths)):
                    seen[u] += iters
            return out

        BASE = starts()
        with nc.Block() as block:
            @block.sync
            def _(e):
                for u in range(2):
                    e.sem_inc(RAW[u], 16)
                for run, ((iters, widths, src, _), base) in enumerate(zip(runs, BASE)):
                    def body(it):
                        for u, w in enumerate(widths):
                            e.wait_ge(LO[u], it + (base[u] + 1))
                            e.dma_start(raw[:, u, 0:KD * w], src(it, u)).then_inc(RAW[u], 16)
                    over(e, iters, body, first=1 if run == 0 else 0)
                load_first(e, s, C["bg"][0], first)

            @block.tensor
            def _(e):
                for u in range(2):
                    e.sem_inc(ACC[u], 1)
                for (iters, widths, _, _), base in zip(runs, BASE):
                    def body(it):
                        for u, w in enumerate(widths):
                            e.wait_ge(HI[u], it + (base[u] + 1))
                            e.wait_ge(LO[u], it + (base[u] + 2))
                            e.wait_ge(FREE[u], it + (base[u] + 1))
                            for k in range(KD):
                                ins = mm3(e, ps[u][0:w, :], hi[:, u, k * w:(k + 1) * w], lo[:, u, k * w:(k + 1) * w],
                                          h_hi[:, k, :], h_lo[:, k, :], k == 0, k == KD - 1)
                            ins.then_inc(ACC[u], 1)
                    over(e, iters, body)

            @block.scalar
            def _(e):
                e.sem_inc(FREE[0], 1)
                for (iters, widths, _, dst), base in zip(runs, BASE):
                    def split_hi(it, u):
                        n = KD * widths[u]
                        e.wait_ge(RAW[u], 16 * it + 16 * (base[u] + 1))
                        e.wait_ge(ACC[u], it + (base[u] + 1))
                        e.copy(hi[:, u, 0:n], raw[:, u, 0:n]).then_inc(HI[u], 1)

                    def out0(it):
                        e.wait_ge(ACC[0], it + (base[0] + 2))
                        e.copy(dst(it, 0), ps[0][0:widths[0], :]).then_inc(FREE[0], 1)

                    for u in range(len(widths)):
                        split_hi(0, u)

                    def body(it):
                        split_hi(it + 1, 0)
                        out0(it)
                        if len(widths) > 1:
                            split_hi(it + 1, 1)
                    over(e, iters - 1, body)
                    out0(iters - 1)

            @block.vector
            def _(e):
                e.sem_inc(LO[0], 1)
                e.sem_inc(LO[1], 1)
                e.sem_inc(FREE[1], 1)
                for (iters, widths, _, dst), base in zip(runs, BASE):
                    def split_lo(it, u):
                        n = KD * widths[u]
                        e.wait_ge(HI[u], it + (base[u] + 1))
                        e.tensor_tensor(lo[:, u, 0:n], raw[:, u, 0:n], hi[:, u, 0:n].bitcast(F32), ALU.subtract).then_inc(LO[u], 1)

                    def out1(it):
                        e.wait_ge(ACC[1], it + (base[1] + 2))
                        e.tensor_copy(dst(it, 1), ps[1][0:widths[1], :]).then_inc(FREE[1], 1)

                    for u in range(len(widths)):
                        split_lo(0, u)

                    def body(it):
                        split_lo(it + 1, 0)
                        if len(widths) > 1:
                            out1(it)
                            split_lo(it + 1, 1)
                    over(e, iters - 1, body)
                    if len(widths) > 1:
                        out1(iters - 1)
    retire(nc, s)


def merge_last(nc, C, l, w_stream, gla_gates, o_hi, o_lo, g_hi, g_lo, raw, first):
    s = phase(nc, Background.SEMS + ["tg0", "tg1", "ghi", "first0", "first1"])
    ps, merged = C["ps"], C["merged"]
    sums = [("branch", (False, c)) for c in range(KD)]
    bg = Background(C, s, w_stream, l, FIRST_JOB["last"], [(P, o_hi, o_lo, 0, True, True)] * KD, sums, [ps[0], ps[1]])
    with ExitStack() as ctx:
        tg = ctx.enter_context(sbuf(nc, "tanh_gate", [P, 2, KD // 2, S], F32))
        with nc.Block() as block:
            @block.sync
            def _(e):
                for half in range(2):
                    e.dma_start(tg[:, half, :, :], gla_gates[half * (KD // 2):(half + 1) * (KD // 2)].rearrange("c p n -> p c n")
                                ).then_inc(s[f"tg{half}"], 16)
                bg.loads(e)
                load_first(e, s, raw, first)

            @block.gpsimd
            def _(e):
                bg.lo(e, 1)
                for c in range(KD):
                    if c + 2 <= bg.n:
                        bg.lo(e, c + 2)
                    bg.add(e, c)

            @block.tensor
            def _(e):
                for c in range(KD):
                    bg.mm(e, c)

            @block.vector
            def _(e):
                def split_lo(c):
                    e.wait_ge(s["ghi"], c + 1)
                    e.scalar_tensor_tensor(out=g_lo[:, c, :], in0=merged[:, c, :], scalar=0.5, in1=g_hi[:, c, :].bitcast(F32),
                                           op0=ALU.mult, op1=ALU.subtract)

                for c in range(KD):
                    if c % (KD // 2) == 0:
                        e.wait_ge(s[f"tg{c // (KD // 2)}"], 16)
                    e.wait_ge(s["b_acc"], c + 1)
                    if c:
                        e.wait_ge(s["b_add"], c)
                    e.scalar_tensor_tensor(out=bg.pr[:, :], in0=tg[:, c // (KD // 2), c % (KD // 2), :], scalar=1.0,
                                           in1=bg.bank(c)[:, :], op0=ALU.add, op1=ALU.mult).then_inc(s["b_pr"], 1)
                    if c >= 2:
                        split_lo(c - 2)
                split_lo(KD - 2)
                split_lo(KD - 1)

            @block.scalar
            def _(e):
                bg.hi(e, 1)
                for c in range(KD):
                    if c + 2 <= bg.n:
                        bg.hi(e, c + 2)
                    if c:
                        e.wait_ge(s["b_add"], c)
                        e.mul(g_hi[:, c - 1, :], merged[:, c - 1, :], 0.5).then_inc(s["ghi"], 1)
                e.wait_ge(s["b_add"], KD)
                e.mul(g_hi[:, KD - 1, :], merged[:, KD - 1, :], 0.5).then_inc(s["ghi"], 1)
    retire(nc, s)


def gated_output(nc, C, o_raw, z, norm_w, o_hi, o_lo, stream, jobs, sums):
    s = phase(nc, Background.SEMS + ["sq", "ss", "ln", "rs", "silu", "a", "b", "hi"])
    ps = C["ps"]
    H = 4
    bg = Background(C, s, *stream, jobs, sums, [ps[4]])
    with ExitStack() as ctx:
        sq = ctx.enter_context(sbuf(nc, "go_sq", [P, H, S], F32))
        rs = ctx.enter_context(sbuf(nc, "go_rs", [P, H, S], F32))
        sz = ctx.enter_context(sbuf(nc, "go_sz", [P, H, S], F32))
        with nc.Block() as block:
            @block.sync
            def _(e):
                bg.loads(e)

            @block.gpsimd
            def _(e):
                for j in range(1, bg.n + 1):
                    bg.lo(e, j)

            @block.scalar
            def _(e):
                if jobs:
                    bg.hi(e, 1)
                e.activation(sz[:, :, :], z, ACT.Silu).then_inc(s["silu"], 1)
                for h in range(H):
                    e.wait_ge(s["ss"], h + 1)
                    e.activation(rs[:, h, :], ps[h][:, :], ACT.Ln, bias=C["eps"], scale=1.0 / P).then_inc(s["ln"], 1)
                for half in range(2):
                    e.wait_ge(s["ln"], 2 * half + 2)
                    r = rs[:, 2 * half:2 * half + 2, :]
                    e.activation(r, r, ACT.Exp, scale=-0.5).then_inc(s["rs"], 1)
                if jobs:
                    bg.out(e, 0)
                for h in range(H):
                    e.wait_ge(s["b"], h + 1)
                    e.copy(o_hi[:, h, :], sz[:, h, :]).then_inc(s["hi"], 1)
                    if jobs and h == 1:
                        bg.hi(e, 2)
                bg.stored(e)

            @block.tensor
            def _(e):
                if jobs:
                    bg.mm(e, 0)
                for h in range(H):
                    e.wait_ge(s["sq"], h + 1)
                    e.matmul(ps[h][:, :], C["ones"], sq[:, h, :], start=True, stop=True).then_inc(s["ss"], 1)
                if jobs:
                    bg.mm(e, 1)

            @block.vector
            def _(e):
                for h in range(H):
                    e.tensor_tensor(sq[:, h, :], o_raw[:, h, :], o_raw[:, h, :], ALU.mult).then_inc(s["sq"], 1)
                e.wait_ge(s["silu"], 1)
                for h in range(H):
                    e.scalar_tensor_tensor(out=sz[:, h, :], in0=o_raw[:, h, :], scalar=norm_w, in1=sz[:, h, :],
                                           op0=ALU.mult, op1=ALU.mult).then_inc(s["a"], 1)
                for h in range(H):
                    e.wait_ge(s["a"], h + 1)
                    e.wait_ge(s["rs"], h // 2 + 1)
                    e.tensor_tensor(sz[:, h, :], sz[:, h, :], rs[:, h, :], ALU.mult).then_inc(s["b"], 1)
                    if h:
                        e.wait_ge(s["hi"], h)
                        e.tensor_tensor(o_lo[:, h - 1, :], sz[:, h - 1, :], o_hi[:, h - 1, :].bitcast(F32), ALU.subtract)
                e.wait_ge(s["hi"], H)
                e.tensor_tensor(o_lo[:, H - 1, :], sz[:, H - 1, :], o_hi[:, H - 1, :].bitcast(F32), ALU.subtract)
    retire(nc, s)


def gdn_prepare(nc, C, prm, pT, miscT, qkv, ba, beta, g, stream, jobs, sums):
    s = phase(nc, Background.SEMS + ["n2", "conv", "silu", "sq", "ss", "ln", "rs", "tr", "ba", "y", "ny", "my", "ex", "lg", "eb", "ea", "b1", "sp"])
    ps = C["ps"]
    QKV = 3 * GDN_H
    SPLITS = {0: 2, 1: 3, 2: 4, 4: 5, 6: 6}
    bg = Background(C, s, *stream, jobs, sums, [ps[4], ps[5], ps[6]], started=(2, 0))
    with ExitStack() as ctx:
        cv = ctx.enter_context(sbuf(nc, "cv", [P, 3, S], F32))
        sq = ctx.enter_context(sbuf(nc, "l2_sq", [P, 4, S], F32))
        rs = ctx.enter_context(sbuf(nc, "l2_rs", [P, 2 * GDN_H, S], F32))
        y = ctx.enter_context(sbuf(nc, "sp_y", [P, NT, 4], F32))
        ny = ctx.enter_context(sbuf(nc, "sp_ny", [P, NT, 4], F32))
        ea = ctx.enter_context(sbuf(nc, "exp_a_log", [P, 4], F32))
        eb = ctx.enter_context(sbuf(nc, "exp_b", [P, NT, 4], F32))
        w = prm["conv"]
        with nc.Block() as block:
            @block.sync
            def _(e):
                bg.loads(e)

            @block.vector
            def _(e):
                def conv(c):
                    if c >= 3:
                        e.wait_ge(s["silu"], c - 2)
                    for n, j in enumerate(range(3, -1, -1)):
                        src = pT[:, c, 1 + j:1 + j + S]
                        wj = w[:, j * QKV + c:j * QKV + c + 1]
                        if n == 0:
                            e.tensor_scalar(cv[:, c % 3, :], src, wj, None, ALU.mult).then_inc(s["conv"], 1)
                        else:
                            e.wait_ge(s["conv"], 4 * c + n)
                            e.scalar_tensor_tensor(out=cv[:, c % 3, :], in0=src, scalar=wj, in1=cv[:, c % 3, :],
                                                   op0=ALU.mult, op1=ALU.add).then_inc(s["conv"], 1)

                e.wait_ge(s["tr"], 1)
                e.tensor_copy(ba[:, :, :], ps[7][:, :].rearrange("p (t c) -> p t c", t=NT)[:, :, 0:80]).then_inc(s["ba"], 1)
                e.wait_ge(s["ba"], 1)
                e.tensor_tensor(y[:, :, :], ba[:, :, 4:8], prm["dt_bias"].unsqueeze(1).to_broadcast([P, NT, 4]), ALU.add).then_inc(s["y"], 1)
                e.wait_ge(s["y"], 1)
                e.tensor_scalar(ny[:, :, :], y[:, :, :], -1.0, None, ALU.mult).then_inc(s["ny"], 1)
                e.wait_ge(s["ny"], 1)
                e.tensor_tensor(ny[:, :, :], ny[:, :, :], y[:, :, :], ALU.min).then_inc(s["my"], 1)
                conv(0)
                conv(1)
                e.wait_ge(s["eb"], 1)
                e.tensor_scalar(eb[:, :, :], eb[:, :, :], 1.0, None, ALU.add).then_inc(s["b1"], 1)
                e.wait_ge(s["b1"], 1)
                e.reciprocal(beta[:, :, :], eb[:, :, :])
                for c in range(2, 11):
                    conv(c)
                e.wait_ge(s["lg"], 1)
                e.scalar_tensor_tensor(out=y[:, :, :], in0=y[:, :, :], scalar=0.0, in1=ny[:, :, :], op0=ALU.max, op1=ALU.add).then_inc(s["sp"], 1)
                e.wait_ge(s["sp"], 1)
                e.wait_ge(s["ea"], 1)
                e.scalar_tensor_tensor(out=g[:, :, :], in0=y[:, :, :], scalar=-1.0, in1=ea[:, :].unsqueeze(1).to_broadcast([P, NT, 4]),
                                       op0=ALU.mult, op1=ALU.mult)

                def scale(c):
                    e.wait_ge(s["rs"], c // 4 + 1)
                    e.scalar_tensor_tensor(out=qkv[:, c, :], in0=qkv[:, c, :], scalar=(P ** -0.5 if c < GDN_H else 1.0),
                                           in1=rs[:, c, :], op0=ALU.mult, op1=ALU.mult).then_inc(s["sp"], 1)

                for c in range(6):
                    scale(c)
                conv(11)
                for c in range(6, 2 * GDN_H):
                    scale(c)

            @block.scalar
            def _(e):
                def silu(c):
                    e.wait_ge(s["conv"], 4 * (c + 1))
                    e.activation(qkv[:, c, :], cv[:, c % 3, :], ACT.Silu).then_inc(s["silu"], 1)

                def keep_norm(c):
                    e.wait_ge(s["ss"], c + 1)
                    e.copy(rs[:, c, :], ps[c % 4][:, :]).then_inc(s["n2"], 1)

                e.activation(ea[:, :], prm["a_log"], ACT.Exp).then_inc(s["ea"], 1)
                e.wait_ge(s["ba"], 1)
                e.activation(eb[:, :, :], ba[:, :, 0:4], ACT.Exp, scale=-1.0).then_inc(s["eb"], 1)
                e.wait_ge(s["my"], 1)
                e.activation(ny[:, :, :], ny[:, :, :], ACT.Exp).then_inc(s["ex"], 1)
                bg.hi(e, 0)
                bg.hi(e, 1)
                for c in range(2 * GDN_H):
                    silu(c)
                    if c in SPLITS:
                        bg.hi(e, SPLITS[c])
                    if c:
                        keep_norm(c - 1)
                e.wait_ge(s["ex"], 1)
                e.activation(ny[:, :, :], ny[:, :, :], ACT.Ln, bias=C["one"]).then_inc(s["lg"], 1)
                for half in range(2):
                    if half:
                        keep_norm(2 * GDN_H - 1)
                    e.wait_ge(s["n2"], 4 * (half + 1))
                    r = rs[:, 4 * half:4 * half + 4, :]
                    e.activation(r, r, ACT.Ln, bias=C["eps"]).then_inc(s["ln"], 1)
                for half in range(2):
                    e.wait_ge(s["ln"], half + 1)
                    r = rs[:, 4 * half:4 * half + 4, :]
                    e.activation(r, r, ACT.Exp, scale=-0.5).then_inc(s["rs"], 1)
                for n in range(3):
                    bg.out(e, n)
                for c in range(2 * GDN_H, QKV):
                    silu(c)
                bg.stored(e)

            @block.gpsimd
            def _(e):
                bg.lo(e, 0)
                bg.lo(e, 1)
                for c in range(2 * GDN_H):
                    e.wait_ge(s["silu"], c + 1)
                    if c >= 4:
                        e.wait_ge(s["ss"], c - 3)
                    e.tensor_tensor(sq[:, c % 4, :], qkv[:, c, :], qkv[:, c, :], ALU.mult).then_inc(s["sq"], 1)
                    if c in SPLITS:
                        bg.lo(e, SPLITS[c])

            @block.tensor
            def _(e):
                for t in range(NT):
                    ins = e.transpose(ps[7][:, t * P:t * P + 80], miscT[:, t * P:(t + 1) * P], C["ident"][0:80, 0:80])
                ins.then_inc(s["tr"], 1)

                def squares(c):
                    e.wait_ge(s["sq"], c + 1)
                    if c >= 4:
                        e.wait_ge(s["n2"], c - 3)
                    e.matmul(ps[c % 4][:, :], C["ones"], sq[:, c % 4, :], start=True, stop=True).then_inc(s["ss"], 1)

                bg.mm(e, 0)
                bg.mm(e, 1)
                for c in range(2 * GDN_H):
                    squares(c)
                    bg.mm(e, c // 2 + 2, c % 2)
    retire(nc, s)


def gdn_tile(nc, C, W, t, stream, jobs, sums):
    s = phase(nc, ["qt", "kt", "vt", "gb", "gcb", "gc", "gcs", "dt0", "dt1", "dn0", "dn1", "eg", "egc", "ekd", "kd0", "qd",
                   "kk", "kq", "dtm", "at", "L0", "bbeta", "trk", "trv", "kde", "ken", "vb", "lv", "b1t", "T", "U", "q", "qs",
                   "uq", "wu", "u", "wt", "vs", "vn", "o", "st", "S", "os"] + Background.SEMS)
    ps = C["ps"]
    bg = Background(C, s, *stream, jobs, sums, [ps[6], ps[7]])
    H = GDN_H
    HB = lambda ap: ap.rearrange("p (h c) -> p h c", h=H)
    cols = bass.ts(t, P)
    (qt, kt, vt, gb, DT, DN, EG, L, AT, B, Tm, U, Q, u, wT, kd, vb, kbe, qd, vn, St, sm) = (
        W[n] for n in ("qt", "kt", "vt", "gb", "DT", "DN", "EG", "L", "AT", "B", "Tm", "U", "Q", "u", "wT", "kd", "vb",
                       "kbe", "qd", "vn", "St", "sm"))
    qkv, beta, g, o_raw = W["qkv"], W["beta"], W["g"], W["o_raw"]
    gc, ekd, egc, beg, bt, gt = (sm[:, i, :] for i in range(6))
    lvl = lambda n: C["lvl"][:, n * P:(n + 1) * P].unsqueeze(1).to_broadcast([P, H, P])
    bc = lambda ap: ap.unsqueeze(1).to_broadcast([P, H, P])
    NL = 6
    with nc.Block() as block:
        @block.sync
        def _(e):
            bg.loads(e)

        @block.gpsimd
        def _(e):
            bg.lo(e, 1)
            e.wait_ge(s["L0"], H)
            for n in range(NL):
                e.tensor_tensor(B[:, n, :, :], L[:, :, :], lvl(n), ALU.mult).then_inc(s["lv"], 1)
                bg.lo(e, n + 2)
            for j in range(NL + 2, bg.n + 1):
                bg.lo(e, j)

        @block.vector
        def _(e):
            e.tensor_copy(gt, g[:, bass.ds(t, 1), :].rearrange("p a h -> p (a h)")).then_inc(s["gc"], 1)
            e.tensor_copy(bt, beta[:, bass.ds(t, 1), :].rearrange("p a h -> p (a h)")).then_inc(s["bbeta"], 1)
            e.wait_ge(s["gc"], 1)
            e.tensor_tensor(gb[:, :, :], bc(C["ones"]), gt.unsqueeze(2).to_broadcast([P, H, P]), ALU.mult).then_inc(s["gb"], 1)
            e.wait_ge(s["gcb"], 1)
            e.tensor_copy(gc, ps[0][:, 0:H]).then_inc(s["gcs"], 1)
            e.wait_ge(s["gcs"], 1)
            e.tensor_tensor(ekd, ps[0][:, H:2 * H], gc, ALU.subtract).then_inc(s["ekd"], 1)
            gcB = HB(ps[1][:, :])
            e.wait_ge(s["eg"], 1)
            for h in range(H):
                e.tensor_scalar(DT[:, h, :], gcB[:, h, :], gc[:, h:h + 1], 0.0, ALU.subtract, ALU.min).then_inc(s["dt0"], 1)
                e.tensor_scalar(DN[:, h, :], gcB[:, h, :], gc[:, h:h + 1], 0.0, ALU.subtract, ALU.max).then_inc(s["dn0"], 1)
            e.wait_ge(s["dt1"], 1)
            e.tensor_tensor(DT[:, :, :], DT[:, :, :], bc(C["tri64"]), ALU.mult).then_inc(s["dtm"], 1)
            e.wait_ge(s["kk"], 1)
            e.wait_ge(s["dn1"], 1)
            e.wait_ge(s["bbeta"], 1)
            for h in range(H):
                e.scalar_tensor_tensor(out=L[:, h, :], in0=HB(ps[2][:, :])[:, h, :], scalar=bt[:, h:h + 1], in1=DN[:, h, :],
                                       op0=ALU.mult, op1=ALU.mult).then_inc(s["L0"], 1)
            e.wait_ge(s["kq"], 1)
            e.wait_ge(s["dtm"], 1)
            e.tensor_tensor(AT[:, :, :], HB(ps[3][:, :]), DT[:, :, :], ALU.mult).then_inc(s["at"], 1)
            e.wait_ge(s["eg"], 1)
            e.wait_ge(s["qt"], 1)
            e.tensor_tensor(qd[:, :, :], qt[:, :, :], EG[:, :, :], ALU.mult).then_inc(s["qd"], 1)
            e.wait_ge(s["egc"], 2)
            e.tensor_tensor(beg, egc, bt, ALU.mult).then_inc(s["ken"], 1)
            e.wait_ge(s["ken"], 1)
            e.wait_ge(s["trk"], 1)
            for h in range(H):
                kn = HB(ps[4][:, :])[:, h, :]
                e.tensor_scalar(kd[:, h, :], kn, ekd[:, h:h + 1], None, ALU.mult).then_inc(s["kde"], 1)
                e.tensor_scalar(kbe[:, h, :], kn, beg[:, h:h + 1], None, ALU.mult).then_inc(s["kde"], 1)
            e.wait_ge(s["trv"], 1)
            for h in range(H):
                e.tensor_scalar(vb[:, h, :], HB(ps[5][:, :])[:, h, :], bt[:, h:h + 1], None, ALU.mult).then_inc(s["vb"], 1)
            e.wait_ge(s["lv"], 1)
            e.tensor_tensor(Tm[:, :, :], bc(C["ident"]), B[:, 0, :, :], ALU.subtract).then_inc(s["T"], 1)
            e.wait_ge(s["b1t"], 1)
            e.tensor_tensor(U[:, :, :], bc(C["ident"]), HB(ps[0][:, :]), ALU.subtract).then_inc(s["U"], 1)
            for n in range(1, NL):
                e.wait_ge(s["q"], n)
                e.tensor_copy(Q[:, :, :], HB(ps[1][:, :])).then_inc(s["qs"], 1)
                e.wait_ge(s["uq"], n)
                e.tensor_tensor(U[:, :, :], U[:, :, :], HB(ps[2][:, :]), ALU.subtract).then_inc(s["U"], 1)
                if n < NL - 1:
                    e.tensor_tensor(Tm[:, :, :], Tm[:, :, :], HB(ps[3][:, :]), ALU.subtract).then_inc(s["T"], 1)
            e.wait_ge(s["wu"], 1)
            e.tensor_copy(u[:, :, :], HB(ps[4][:, :])).then_inc(s["u"], 1)
            e.wait_ge(s["u"], 1)
            for c in range(2):
                rows = slice(c * GDN_C, (c + 1) * GDN_C)
                e.wait_ge(s["vs"], c + 1)
                e.tensor_tensor(vn[rows, :, :], u[rows, :, :], HB(ps[2][rows, :]), ALU.subtract).then_inc(s["vn"], 1)
                e.wait_ge(s["st"], c + 1)
                for h in range(H):
                    last = (c + 1) * GDN_C - 1
                    e.scalar_tensor_tensor(out=St[:, h, :], in0=St[:, h, :], scalar=EG[:, h, last:last + 1],
                                           in1=HB(ps[0][:, :])[:, h, :], op0=ALU.mult, op1=ALU.add).then_inc(s["S"], 1)

        @block.scalar
        def _(e):
            e.copy(kt[:, :, :], qkv[:, H:2 * H, cols]).then_inc(s["kt"], 1)
            bg.hi(e, 1)
            e.copy(qt[:, :, :], qkv[:, 0:H, cols]).then_inc(s["qt"], 1)
            e.wait_ge(s["gcb"], 1)
            e.activation(EG[:, :, :], HB(ps[1][:, :]), ACT.Exp).then_inc(s["eg"], 1)
            e.copy(vt[:, :, :], qkv[:, 2 * H:3 * H, cols]).then_inc(s["vt"], 1)
            e.wait_ge(s["ekd"], 1)
            e.activation(ekd, ekd, ACT.Exp).then_inc(s["egc"], 1)
            e.activation(egc, gc, ACT.Exp).then_inc(s["egc"], 1)
            e.wait_ge(s["dt0"], H)
            e.activation(DT[:, :, :], DT[:, :, :], ACT.Exp).then_inc(s["dt1"], 1)
            e.wait_ge(s["dn0"], H)
            e.activation(DN[:, :, :], DN[:, :, :], ACT.Exp, scale=-1.0).then_inc(s["dn1"], 1)
            bg.hi(e, 2)
            for n in range(len(sums) - 2):
                bg.hi(e, 2 * n + 3)
                bg.out(e, n)
                bg.hi(e, 2 * n + 4)
            bg.hi(e, bg.n - 1)
            bg.out(e, len(sums) - 2)
            e.wait_ge(s["wu"], 2)
            e.copy(wT[:, :, :], HB(ps[5][:, :])).then_inc(s["wt"], 1)
            bg.hi(e, bg.n)
            bg.out(e, len(sums) - 1)
            e.wait_ge(s["o"], 2)
            e.copy(o_raw[:, :, cols], HB(ps[3][:, :])).then_inc(s["os"], 1)
            bg.stored(e)

        @block.tensor
        def _(e):
            bg.mm(e, 0, 0)
            e.wait_ge(s["gc"], 1)
            e.matmul(ps[0][:, 0:H], C["tri64"], gt, start=True, stop=True)
            e.matmul(ps[0][:, H:2 * H], C["blk64"], gt, start=True, stop=True)
            e.wait_ge(s["gb"], 1)
            for h in range(H):
                ins = e.matmul(HB(ps[1][:, :])[:, h, :], gb[:, h, :], C["tri64"], start=True, stop=True)
            ins.then_inc(s["gcb"], 1)
            bg.mm(e, 0, 1)
            e.wait_ge(s["kt"], 1)
            for h in range(H):
                ins = e.matmul(HB(ps[2][:, :])[:, h, :], kt[:, h, :], kt[:, h, :], start=True, stop=True)
            ins.then_inc(s["kk"], 1)
            e.wait_ge(s["qt"], 1)
            for h in range(H):
                ins = e.matmul(HB(ps[3][:, :])[:, h, :], kt[:, h, :], qt[:, h, :], start=True, stop=True)
            ins.then_inc(s["kq"], 1)
            for h in range(H):
                ins = e.transpose(HB(ps[4][:, :])[:, h, :], kt[:, h, :], C["ident"])
            ins.then_inc(s["trk"], 1)
            e.wait_ge(s["vt"], 1)
            for h in range(H):
                ins = e.transpose(HB(ps[5][:, :])[:, h, :], vt[:, h, :], C["ident"])
            ins.then_inc(s["trv"], 1)
            bg.mm(e, 1)
            e.wait_ge(s["lv"], 1)
            e.wait_ge(s["ekd"], 1)
            for h in range(H):
                ins = e.transpose(HB(ps[0][:, :])[:, h, :], B[:, 0, h, :], C["ident"])
            ins.then_inc(s["b1t"], 1)
            bg.mm(e, 2)
            for n in range(1, NL):
                e.wait_ge(s["lv"], n + 1)
                e.wait_ge(s["U"], n)
                e.wait_ge(s["dn0"], H)
                for h in range(H):
                    ins = e.matmul(HB(ps[1][:, :])[:, h, :], B[:, n, h, :], U[:, h, :], start=True, stop=True)
                ins.then_inc(s["q"], 1)
                bg.mm(e, n + 2, 0)
                e.wait_ge(s["qs"], n)
                e.wait_ge(s["T"], n)
                e.wait_ge(s["L0"], H)
                for h in range(H):
                    ins = e.matmul(HB(ps[2][:, :])[:, h, :], Tm[:, h, :], Q[:, h, :], start=True, stop=True)
                if n < NL - 1:
                    e.wait_ge(s["at"], 1)
                    for h in range(H):
                        ins = e.matmul(HB(ps[3][:, :])[:, h, :], Q[:, h, :], Tm[:, h, :], start=True, stop=True)
                ins.then_inc(s["uq"], 1)
                bg.mm(e, n + 2, 1)
            e.wait_ge(s["U"], NL)
            e.wait_ge(s["vb"], H)
            e.wait_ge(s["kde"], 2 * H)
            for h in range(H):
                ins = e.matmul(HB(ps[4][:, :])[:, h, :], U[:, h, :], vb[:, h, :], start=True, stop=True)
            ins.then_inc(s["wu"], 1)
            for h in range(H):
                ins = e.matmul(HB(ps[5][:, :])[:, h, :], kbe[:, h, :], U[:, h, :], start=True, stop=True)
            ins.then_inc(s["wu"], 1)
            bg.mm(e, NL + 2, 0)
            e.wait_ge(s["wt"], 1)
            e.wait_ge(s["at"], 1)
            e.wait_ge(s["qd"], 1)
            for c in range(2):
                rows = slice(c * GDN_C, (c + 1) * GDN_C)
                if c:
                    bg.mm(e, NL + 3, 0)
                    e.wait_ge(s["S"], H)
                for h in range(H):
                    ins = e.matmul(HB(ps[2][:, :])[:, h, :], wT[:, h, :], St[:, h, :], start=True, stop=True)
                ins.then_inc(s["vs"], 1)
                bg.mm(e, NL + 2 + c, 1)
                e.wait_ge(s["vn"], c + 1)
                for h in range(H):
                    out = HB(ps[3][:, :])[:, h, rows]
                    e.matmul(out, St[:, h, :], qd[:, h, rows], start=True, stop=False)
                    ins = e.matmul(out, vn[rows, h, :], AT[rows, h, rows], start=False, stop=True)
                ins.then_inc(s["o"], 1)
                for h in range(H):
                    ins = e.matmul(HB(ps[0][:, :])[:, h, :], kd[rows, h, :], vn[rows, h, :], start=True, stop=True)
                ins.then_inc(s["st"], 1)
    retire(nc, s)


def gdn(nc, C, prm, l, wd, h_hi, h_lo, miscT, ba, o_hi, o_lo, nsa_rows, gla_gates):
    H = GDN_H
    with ExitStack() as ctx:
        sb = lambda n, shape: ctx.enter_context(sbuf(nc, n, shape, F32))
        z = sb("gdn_z", [P, H, S])
        qkv = sb("gdn_qkv", [P, 3 * H, S])
        beta = sb("gdn_beta", [P, NT, 4])
        g = sb("gdn_g", [P, NT, 4])
        o_raw = sb("gdn_o", [P, H, S])
        with ExitStack() as c2:
            pT = c2.enter_context(sbuf(nc, "gdn_pT", [P, 3 * H, 4 + S], F32))
            w_gdn = wd["w_gdn"]
            with ExitStack() as c3:
                raw = raw_buffer(nc, c3)
                norm_transpose(nc, C, prm["mix_pre"], h_hi, h_lo, raw, [w_gdn[l, u] for u in range(2)])
                zero(nc, pT[:, :, 0:4])
                project(nc, C, raw, h_hi, h_lo, [
                    (6, (P, P), lambda it, u: w_gdn[l, 2 * it + u], lambda it, u: pT[:, 2 * it + u, 4:4 + S]),
                    (2, (P, P), lambda it, u: w_gdn[l, 2 * it + (12 + u)], lambda it, u: z[:, 2 * it + u, :]),
                    (1, (80,), lambda it, u: wd["w_misc"][l], lambda it, u: miscT[:, :])],
                    [wd["w_stream"][l, FIRST_JOB["gdn_prepare"] + u] for u in range(2)])
            jobs, sums = [], []
            for c in range(3):
                jobs += column_jobs(P, h_hi, h_lo)
                sums.append(("tanh", gla_gates[c]))
            gdn_prepare(nc, C, prm, pT, miscT, qkv, ba, beta, g, (wd["w_stream"], l, FIRST_JOB["gdn_prepare"]), jobs, sums)
        with ExitStack() as c2:
            W = {"qkv": qkv, "beta": beta, "g": g, "o_raw": o_raw}
            for k, n in enumerate(("qt", "kt", "vt", "gb", "DT", "DN", "EG", "L")):
                W[n] = C["merged"][:, k, :].rearrange("p (h c) -> p h c", h=H)
            for n in ("AT", "Tm", "U", "Q", "u", "wT", "kd", "vb", "kbe", "qd", "vn", "St"):
                W[n] = c2.enter_context(sbuf(nc, "gdn_" + n, [P, H, P], F32))
            W["B"] = c2.enter_context(sbuf(nc, "gdn_B", [P, 6, H, P], F32))
            W["sm"] = c2.enter_context(sbuf(nc, "gdn_sm", [P, 6, 4], F32))
            zero(nc, W["St"][:, :, :])
            with nc.Fori(0, NT) as t:
                jobs, sums = [], []
                per_tile = NSA_CHUNKS // NT
                for c in range(per_tile):
                    n = per_tile * t + c
                    jobs += column_jobs(NDK, h_hi, h_lo)
                    sums.append(("store", nsa_rows[bass.ds(n, 1)].rearrange("a p n -> (a p) n")))
                gdn_tile(nc, C, W, t, (wd["w_stream"], l, 2 * per_tile * t + FIRST_JOB["gdn"]), jobs, sums)
        gated_output(nc, C, o_raw, z[:, :, :], prm["gdn_norm"], o_hi, o_lo, (wd["w_stream"], l, FIRST_JOB["gdn_out"]),
                     column_jobs(P, h_hi, h_lo), [("tanh", gla_gates[3])])


def nsa_compress(nc, C, prm, l, wd, nsa_rows, early, miscT, gates, vnat, kcT, vc, stream, jobs, sums):
    kT, vT = early[:, 0:NSA_G, :], early[0:NDV, NSA_G:4 * NSA_G, :]
    s = phase(nc, Background.SEMS + ["early", "g0", "g1", "trg", "gate", "gate2", "tr0", "tr1", "v0", "v1", "xk", "xv", "wk0", "wk1", "wv0", "wv1", "usedk0",
                   "usedk1", "usedv0", "usedv1", "hk", "hv", "hid", "kc", "vc", "kcs"])
    ps = C["ps"]
    bg = Background(C, s, *stream, jobs, sums, [ps[6], ps[7]])
    LB = 8
    NB = CMP_LEN // LB
    with ExitStack() as ctx:
        sb = lambda n, shape: ctx.enter_context(sbuf(nc, n, shape, F32))
        xk = sb("cmp_xk", [NDK, CMP_LEN, NSA_G, NCMP])
        xv = sb("cmp_xv", [NDV, CMP_LEN, NSA_G, NCMP])
        wk = sb("cmp_wk", [NDK, 2, LB, CMP_HID])
        wv = sb("cmp_wv", [NDV, 2, LB, CMP_HID])
        hk = sb("cmp_hk", [P, 2, NSA_G * NCMP])
        hv = sb("cmp_hv", [P, 2, NSA_G * NCMP])
        with nc.Block() as block:
            @block.sync
            def _(e):
                bg.load(e, 2)
                e.dma_start(early[:, :, :], nsa_rows[NSA_LATE:NSA_CHUNKS].rearrange("c p n -> p c n")).then_inc(s["early"], 16)
                bg.load(e, 3)
                j = 4
                for b in range(NB):
                    for w, wx, key in ((wk, "w_ck", "k"), (wv, "w_cv", "v")):
                        if b >= 2:
                            bg.load(e, j)
                            j += 1
                            e.wait_ge(s[f"used{key}{b % 2}"], b // 2)
                        e.dma_start(w[:, b % 2, :, :], wd[wx][l, :, b * LB:(b + 1) * LB, :]).then_inc(s[f"w{key}{b % 2}"], 16)
                    if b < 2:
                        bg.load(e, j)
                        bg.load(e, j + 1)
                        j += 2
                for j in range(j, bg.n + 2):
                    bg.load(e, j)
                bg.loads_done(e)

            @block.gpsimd
            def _(e):
                bg.lo(e, 1)
                bg.lo(e, 2)
                for j in range(3, bg.n + 1):
                    bg.lo(e, j)
                    if jobs[j - 1][5] and bg.sum_of[j - 1] in bg.branches:
                        bg.add(e, bg.sum_of[j - 1])

            @block.tensor
            def _(e):
                bg.mm(e, 0)
                for t in range(NT):
                    ins = e.transpose(ps[7][:, t * P:t * P + 80], miscT[:, t * P:(t + 1) * P], C["ident"][0:80, 0:80])
                ins.then_inc(s["trg"], 1)
                bg.mm(e, 1)
                e.wait_ge(s["early"], 16)
                for b in range(2):
                    for g in range(NSA_G):
                        for t in range(NT):
                            n = g * NT + t
                            ins = e.transpose(ps[4 + b][:, n * NDV:(n + 1) * NDV], vT[:, 2 * (b + 1) + g, t * P:(t + 1) * P],
                                              C["ident"][0:NDV, 0:NDV])
                    ins.then_inc(s[f"tr{b}"], 1)
                e.wait_ge(s["gate"], 1)
                bg.mm(e, 2)
                e.wait_ge(s["xk"], NSA_G)
                e.wait_ge(s["xv"], NSA_G)
                for b in range(NB):
                    e.wait_ge(s[f"wk{b % 2}"], 16 * (b // 2 + 1))
                    for j in range(LB):
                        p = b * LB + j
                        for c in range(2):
                            ins = e.matmul(ps[c][:, 0:NSA_G * NCMP], wk[:, b % 2, j, c * P:(c + 1) * P],
                                           xk[:, p, :, :].rearrange("p g n -> p (g n)"), start=(p == 0), stop=(p == CMP_LEN - 1))
                    ins.then_inc(s[f"usedk{b % 2}"], 1)
                    bg.mm(e, 2 * b + 3)
                    e.wait_ge(s[f"wv{b % 2}"], 16 * (b // 2 + 1))
                    for j in range(LB):
                        p = b * LB + j
                        for c in range(2):
                            ins = e.matmul(ps[2 + c][:, 0:NSA_G * NCMP], wv[:, b % 2, j, c * P:(c + 1) * P],
                                           xv[:, p, :, :].rearrange("p g n -> p (g n)"), start=(p == 0), stop=(p == CMP_LEN - 1))
                    ins.then_inc(s[f"usedv{b % 2}"], 1)
                    bg.mm(e, 2 * b + 4)
                bg.mm(e, 2 * NB + 3)
                e.wait_ge(s["hid"], 4)
                e.wait_ge(s["kcs"], 2)
                for c in range(2):
                    ins = e.matmul(ps[4][0:NDK, 0:NSA_G * NCMP], prm["w2k"][:, c * NDK:(c + 1) * NDK], hk[:, c, :],
                                   start=(c == 0), stop=(c == 1))
                ins.then_inc(s["kc"], 1)
                for g in range(NSA_G):
                    for c in range(2):
                        ins = e.matmul(ps[5][0:NCMP, g * NDV:(g + 1) * NDV], hv[:, c, g * NCMP:(g + 1) * NCMP],
                                       prm["w2v"][:, c * NDV:(c + 1) * NDV], start=(c == 0), stop=(c == 1))
                ins.then_inc(s["vc"], 1)

            @block.scalar
            def _(e):
                bg.hi(e, 1)
                e.wait_ge(s["trg"], 1)
                e.activation(gates[:, :, :], ps[7][:, :].rearrange("p (t c) -> p t c", t=NT)[:, :, 32:56], ACT.Tanh,
                             scale=0.5).then_inc(s["gate"], 1)
                bg.hi(e, 2)
                for b in range(2):
                    e.wait_ge(s[f"tr{b}"], 1)
                    e.copy(vnat[:, b, :, :, :], ps[4 + b][:, :].rearrange("p (g t d) -> p g t d", g=NSA_G, t=NT)).then_inc(s["kcs"], 1)
                for j in range(3, bg.n + 1):
                    if jobs[j - 2][5]:
                        bg.out(e, bg.sum_of[j - 2])
                    bg.hi(e, j)
                e.wait_ge(s["usedk1"], NB // 2)
                for c in range(2):
                    e.activation(hk[:, c, :], ps[c][:, 0:NSA_G * NCMP], ACT.Gelu_apprx_tanh).then_inc(s["hid"], 1)
                e.wait_ge(s["usedv1"], NB // 2)
                for c in range(2):
                    e.activation(hv[:, c, :], ps[2 + c][:, 0:NSA_G * NCMP], ACT.Gelu_apprx_tanh).then_inc(s["hid"], 1)
                e.wait_ge(s["kc"], 1)
                e.copy(kcT[:, :, :], ps[4][0:NDK, 0:NSA_G * NCMP].rearrange("p (g n) -> p g n", g=NSA_G))
                e.wait_ge(s["vc"], 1)
                e.copy(vc[:, :, :], ps[5][0:NCMP, 0:NSA_G * NDV].rearrange("p (g d) -> p g d", g=NSA_G))

            @block.vector
            def _(e):
                def blocks(x, pe, out, sem):
                    for g in range(NSA_G):
                        for half in range(2):
                            pos = slice(half * CMP_STRIDE, (half + 1) * CMP_STRIDE)
                            src = x[:, g, half * CMP_STRIDE:half * CMP_STRIDE + NCMP * CMP_STRIDE]
                            ins = e.tensor_tensor(out[:, pos, g, :], src.rearrange("p (n j) -> p j n", j=CMP_STRIDE),
                                                  pe[:, pos].unsqueeze(2).to_broadcast([x.shape[0], CMP_STRIDE, NCMP]), ALU.add)
                        ins.then_inc(s[sem], 1)

                e.wait_ge(s["early"], 16)
                blocks(kT, prm["pe_k"][0:NDK, :], xk, "xk")
                blocks(vT, prm["pe_v"][0:NDV, :], xv, "xv")
                e.wait_ge(s["gate"], 1)
                e.tensor_scalar(gates[:, :, :], gates[:, :, :], 0.5, 0.5, ALU.mult, ALU.add).then_inc(s["gate2"], 1)
                e.wait_ge(s["gate2"], 1)
                cg = gates[:, 0, :].rearrange("p (h b) -> p h b", b=3)[:, :, 0]
                e.tensor_scalar(cg, cg, C["cmp_valid"], None, ALU.mult)
                for n in bg.branches:
                    bg.product(e, n)
    retire(nc, s)


def nsa_heads(nc, C, W, grp, stream, jobs, sums):
    s = phase(nc, Background.SEMS + ["q0", "q1", "k0", "k1", "v", "vcs", "bias0", "bias1", "biasc", "gst", "sc", "lg", "mx", "ex", "rc", "rg", "pn", "tr",
                   "pts", "ptc", "ptw", "o", "ohi", "olo"])
    ps = C["ps"]
    bg = Background(C, s, *stream, jobs, sums, [ps[2]])
    rows, kcT, vnat, vc, gates = (W[n] for n in ("nsa_rows", "kcT", "vnat", "vc", "gates"))
    ks = W["ks"]
    qs, vs, vcs, bs, bcs, gs, lg, st, pt = (W[n] for n in ("qs", "vs", "vcs", "bs", "bcs", "gs", "lg", "st", "pt"))
    o_hi, o_lo = W["o_hi"], W["o_lo"]
    scale = NDK ** -0.5
    items = [(hh, t) for hh in range(HPG) for t in range(NT)]
    one = lambda ap, pat, **k: ap.rearrange(pat, **k)
    BR = 3
    with nc.Block() as block:
        @block.gpsimd
        def _(e):
            bg.lo(e, 1)
            e.tensor_copy(vs[:, :, :, :], vnat[:, :, bass.ds(grp, 1), :, :].rearrange("p b a t d -> p b (a t) d")).then_inc(s["v"], 1)
            e.tensor_copy(vcs[:, :], vc[:, bass.ds(grp, 1), :].rearrange("p a d -> p (a d)")).then_inc(s["vcs"], 1)
            for j in range(2, bg.n + 1):
                bg.lo(e, j)
                if jobs[j - 2][5] and bg.sum_of[j - 2] in bg.branches:
                    bg.add(e, bg.sum_of[j - 2])
            for n in bg.branches[-1:]:
                bg.add(e, n)

        @block.sync
        def _(e):
            e.dma_start(qs[:, 0, :], rows[bass.ds(HPG * grp, 1)].rearrange("a p n -> (a p) n")).then_inc(s["q0"], 16)
            for b in range(2):
                e.dma_start(ks[:, b, :], rows[bass.ds(grp + (NSA_H + NSA_G * b), 1)].rearrange("a p n -> (a p) n")).then_inc(s[f"k{b}"], 16)
            bias = W["bias"][bass.ds(grp, 1)].rearrange("a p h n -> (a p) h n")
            e.dma_start(bcs[:, :, :], W["biasc"][bass.ds(grp, 1)].rearrange("a p h n -> (a p) h n")).then_inc(s["biasc"], 16)
            e.dma_start(bs[:, 0, :], bias[:, 0, :]).then_inc(s["bias0"], 16)
            bg.load(e, 2)
            e.dma_start(qs[:, 1:HPG, :], rows[bass.ds(HPG * grp + 1, HPG - 1)].rearrange("c p n -> p c n")).then_inc(s["q1"], 16)
            e.dma_start(bs[:, 1:HPG, :], bias[:, 1:HPG, :]).then_inc(s["bias1"], 16)
            for j in range(3, bg.n + 2):
                bg.load(e, j)
            bg.loads_done(e)

        @block.tensor
        def _(e):
            def scores(i):
                hh, t = items[i]
                w = (t + 1) * P
                if t == 0 and hh < 2:
                    e.wait_ge(s[f"q{hh}"], 16)
                lhs = qs[:, hh, t * P:(t + 1) * P]
                if i:
                    e.wait_ge(s["lg"], BR * (i - 1) + 1)
                if i >= 2:
                    e.wait_ge(s["ptc"], i - 1)
                e.matmul(ps[5][:, P:P + NCMP], lhs, kcT[:, bass.ds(grp, 1), :].rearrange("p a n -> p (a n)"),
                         start=True, stop=True).then_inc(s["sc"], 1)
                for b in range(2):
                    if i:
                        e.wait_ge(s["lg"], BR * (i - 1) + b + 2)
                    if i == 0:
                        e.wait_ge(s[f"k{b}"], 16)
                    e.matmul(ps[b][:, 0:w], lhs, ks[:, b, 0:w], start=True, stop=True).then_inc(s["sc"], 1)
            def values(i):
                hh, t = items[i]
                w = (t + 1) * P
                for b in (1, 2, 0):
                    e.wait_ge(s["pn"], BR * i + b + 1)
                    if i:
                        e.wait_ge(s[("ptc", "pts", "ptw")[b]], i)
                    if b:
                        for j in range(t + 1):
                            ins = e.transpose(ps[2 + b][:, j * P:(j + 1) * P], lg[:, i % 2, b, j * P:(j + 1) * P], C["ident"])
                    else:
                        if i + 1 < len(items):
                            e.wait_ge(s["lg"], BR * (i + 1) + 1)
                        ins = e.transpose(ps[5][0:NCMP, 0:P], lg[:, i % 2, b, 0:NCMP], C["ident"])
                    ins.then_inc(s["tr"], 1)
                bg.mm(e, i + 1, 1)
                if i == 0:
                    e.wait_ge(s["v"], 1)
                    e.wait_ge(s["vcs"], 1)
                if i >= 2:
                    e.wait_ge(s["olo"], i - 1)
                out = ps[6 + i % 2][(hh % 2) * NDV:(hh % 2 + 1) * NDV, 0:P]
                e.wait_ge(s["pts"], i + 1)
                for j in range(t + 1):
                    e.matmul(out, vs[:, 0, j, :], pt[:, 0, j * P:(j + 1) * P], start=(j == 0), stop=False)
                e.wait_ge(s["ptw"], i + 1)
                for j in range(t + 1):
                    e.matmul(out, vs[:, 1, j, :], pt[:, 1, j * P:(j + 1) * P], start=False, stop=False)
                e.wait_ge(s["ptc"], i + 1)
                e.matmul(out, vcs[:, :], pt[0:NCMP, 2, 0:P], start=False, stop=True).then_inc(s["o"], 1)

            bg.mm(e, 0)
            scores(0)
            for i in range(len(items)):
                if i + 1 < len(items):
                    scores(i + 1)
                bg.mm(e, i + 1, 0)
                values(i)
            for j in range(len(items) + 1, len(jobs)):
                bg.mm(e, j)

        @block.vector
        def _(e):
            e.tensor_copy(gs[:, :, :], gates[:, :, bass.ds(3 * HPG * grp, 3 * HPG)]).then_inc(s["gst"], 1)
            e.wait_ge(s["biasc"], 16)
            e.wait_ge(s["gst"], 1)

            def logits(i):
                hh, t = items[i]
                w = (t + 1) * P
                if t == 0 and hh < 2:
                    e.wait_ge(s[f"bias{hh}"], 16)
                if i >= 2:
                    e.wait_ge(s["tr"], BR * (i - 1))
                for b in range(BR):
                    e.wait_ge(s["sc"], BR * i + b + 1)
                    n = w if b else NCMP
                    bb = bs[:, hh, S - w:S] if b else bcs[:, hh, (NT - 1 - t) * NCMP:(NT - t) * NCMP]
                    sc = ps[b - 1][:, 0:n] if b else ps[5][:, P:P + n]
                    e.scalar_tensor_tensor(out=lg[:, i % 2, b, 0:n], in0=sc, scalar=scale, in1=bb,
                                           op0=ALU.mult, op1=ALU.add).then_inc(s["lg"], 1)
                for b in range(BR):
                    n = w if b else NCMP
                    e.wait_ge(s["lg"], BR * i + b + 1)
                    e.tensor_reduce(st[:, i % 2, b:b + 1], lg[:, i % 2, b, 0:n], AX, ALU.max, negate=True).then_inc(s["mx"], 1)

            def normalise(i):
                hh, t = items[i]
                w = (t + 1) * P
                e.wait_ge(s["ex"], BR * (i + 1))
                e.reciprocal(st[:, i % 2, 8:11], st[:, i % 2, 4:7]).then_inc(s["rc"], 1)
                e.wait_ge(s["rc"], i + 1)
                e.tensor_tensor(st[:, i % 2, 12:15], st[:, i % 2, 8:11], gs[:, t, 3 * hh:3 * hh + 3], ALU.mult).then_inc(s["rg"], 1)
                e.wait_ge(s["rg"], i + 1)
                for b in range(BR):
                    n = w if b else NCMP
                    e.tensor_scalar(lg[:, i % 2, b, 0:n], lg[:, i % 2, b, 0:n], st[:, i % 2, 12 + b:13 + b], None, ALU.mult).then_inc(s["pn"], 1)

            def window_probs(i):
                hh, t = items[i]
                w = (t + 1) * P
                e.wait_ge(s["tr"], BR * i + 2)
                if i:
                    e.wait_ge(s["o"], i)
                e.tensor_copy(pt[:, 1, 0:w], ps[4][:, 0:w]).then_inc(s["ptw"], 1)

            def out_lo(i):
                hh, t = items[i]
                rows = slice((hh % 2) * NDV, (hh % 2 + 1) * NDV)
                e.wait_ge(s["ohi"], i + 1)
                dst = bass.ds(2 * grp + hh // 2, 1)
                e.tensor_tensor(o_lo[rows, dst, t * P:(t + 1) * P].rearrange("p a n -> p (a n)"), ps[6 + i % 2][rows, 0:P],
                                o_hi[rows, dst, t * P:(t + 1) * P].rearrange("p a n -> p (a n)").bitcast(F32), ALU.subtract).then_inc(s["olo"], 1)

            logits(0)
            for i in range(len(items)):
                normalise(i)
                if i + 1 < len(items):
                    logits(i + 1)
                window_probs(i)
                if i:
                    out_lo(i - 1)
                if jobs[i + 1][5] and bg.sum_of[i + 1] in bg.branches:
                    bg.product(e, bg.sum_of[i + 1])
            out_lo(len(items) - 1)
            bg.product(e, bg.branches[-1])

        @block.scalar
        def _(e):
            bg.hi(e, 1)
            bg.hi(e, 2)

            def exps(i):
                hh, t = items[i]
                w = (t + 1) * P
                for b in range(BR):
                    n = w if b else NCMP
                    e.wait_ge(s["mx"], BR * i + b + 1)
                    e.activation(lg[:, i % 2, b, 0:n], lg[:, i % 2, b, 0:n], ACT.Exp, bias=st[:, i % 2, b:b + 1],
                                 accum_out=st[:, i % 2, 4 + b:5 + b]).then_inc(s["ex"], 1)

            def probs(i):
                hh, t = items[i]
                w = (t + 1) * P
                e.wait_ge(s["tr"], BR * i + 1)
                if i:
                    e.wait_ge(s["o"], i)
                e.copy(pt[:, 0, 0:w], ps[3][:, 0:w]).then_inc(s["pts"], 1)
                e.wait_ge(s["tr"], BR * i + 3)
                e.copy(pt[0:NCMP, 2, 0:P], ps[5][0:NCMP, 0:P]).then_inc(s["ptc"], 1)

            def out_hi(i):
                hh, t = items[i]
                rows = slice((hh % 2) * NDV, (hh % 2 + 1) * NDV)
                e.wait_ge(s["o"], i + 1)
                dst = bass.ds(2 * grp + hh // 2, 1)
                e.copy(o_hi[rows, dst, t * P:(t + 1) * P].rearrange("p a n -> p (a n)"), ps[6 + i % 2][rows, 0:P]).then_inc(s["ohi"], 1)

            exps(0)
            for i in range(len(items)):
                if i + 1 < len(items):
                    exps(i + 1)
                probs(i)
                bg.hi(e, i + 3)
                if jobs[i + 1][5]:
                    bg.out(e, bg.sum_of[i + 1])
                out_hi(i)
            bg.stored(e)
    retire(nc, s)


def nsa(nc, C, prm, l, wd, h_hi, h_lo, miscT, nsa_rows, gla_rows, bias, biasc, d_hi, d_lo, o_hi, o_lo):

    def merge(chunk):
        return merge_jobs(h_hi, h_lo, d_hi, d_lo, chunk, True)

    with ExitStack() as ctx:
        sb = lambda n, shape: ctx.enter_context(sbuf(nc, n, shape, F32))
        W = {"o_hi": o_hi, "o_lo": o_lo, "bias": bias, "biasc": biasc}
        vnat = W["vnat"] = sb("nsa_vnat", [P, 2, NSA_G, NT, NDV])
        kcT = W["kcT"] = sb("nsa_kcT", [NDK, NSA_G, NCMP])
        vc = W["vc"] = sb("nsa_vc", [NCMP, NSA_G, NDV])
        gates = W["gates"] = sb("nsa_gates", [P, NT, 3 * NSA_H])
        with ExitStack() as c2:
            early = c2.enter_context(sbuf(nc, "nsa_early", [NDK, NSA_CHUNKS - NSA_LATE, S], F32))
            jobs, sums = [], []
            for c in range(4):
                j, m = merge(4 + c)
                jobs, sums = jobs + j, sums + m
            nsa_compress(nc, C, prm, l, wd, nsa_rows, early, miscT, gates, vnat, kcT, vc,
                         (wd["w_stream"], l, FIRST_JOB["compress"]), jobs, sums)
        with ExitStack() as c2:
            W["nsa_rows"] = nsa_rows
            for n, shape in (("qs", [NDK, HPG, S]), ("ks", [NDK, 2, S]), ("vs", [P, 2, NT, NDV]), ("vcs", [NCMP, NDV]), ("bs", [P, HPG, S]),
                             ("bcs", [P, HPG, NT * NCMP]), ("gs", [P, NT, 3 * HPG]), ("lg", [P, 2, 3, S]), ("st", [P, 2, 16]),
                             ("pt", [P, 3, S])):
                W[n] = c2.enter_context(sbuf(nc, "nsa_" + n, shape, F32))
            with nc.Fori(0, NSA_G) as grp:
                jobs, sums = [], []
                for pr in range(2):
                    for c in range(3):
                        jobs += column_jobs(P, h_hi, h_lo)
                        sums.append(("store", gla_rows[bass.ds(6 * grp + (3 * pr + c), 1)].rearrange("a p n -> (a p) n")))
                    j, m = merge(2 * grp + pr)
                    jobs, sums = jobs + j, sums + m
                nsa_heads(nc, C, W, grp, (wd["w_stream"], l, len(jobs) * grp + FIRST_JOB["heads"]), jobs, sums)


def gla_prepare(nc, C, prm, miscT, pT, q1, k1, qd, kd, ebc, gla_rows, stream, jobs, sums):
    s = phase(nc, Background.SEMS + ["lg", "x", "nx", "m", "ex", "ln", "ls", "cs", "d", "e", "pT"])
    ps = C["ps"]
    bg = Background(C, s, *stream, jobs, sums, ps[2:6])
    NC_ = S // GLA_C
    with ExitStack() as ctx:
        sb = lambda n: ctx.enter_context(sbuf(nc, n, [P, 2, S], F32))
        x, y = sb("gla_x"), sb("gla_y")
        V = lambda ap: ap.rearrange("p a (n c) -> p (a n) c", c=GLA_C)
        at = lambda ap, i: V(ap)[:, :, i:i + 1].to_broadcast([P, 2 * NC_, GLA_C])
        with nc.Block() as block:
            @block.tensor
            def _(e):
                for c in range(2):
                    ins = e.matmul(ps[c][:, :], prm["gla_w"][64:80, c * P:(c + 1) * P], miscT[64:80, :], start=True, stop=True)
                ins.then_inc(s["lg"], 1)
                for j in range(bg.n):
                    bg.mm(e, j)

            @block.sync
            def _(e):
                bg.load(e, 2)
                bg.load(e, 3)
                e.dma_start(pT[:, :, :], gla_rows.rearrange("c p n -> p c n")).then_inc(s["pT"], 16)
                for j in range(4, bg.n + 2):
                    bg.load(e, j)
                bg.loads_done(e)

            @block.gpsimd
            def _(e):
                for j in range(1, bg.n + 1):
                    bg.lo(e, j)

            @block.vector
            def _(e):
                e.wait_ge(s["lg"], 1)
                for c in range(2):
                    e.tensor_scalar(x[:, c, :], ps[c][:, :], prm["gla_b"][:, c:c + 1], None, ALU.add).then_inc(s["x"], 1)
                e.wait_ge(s["x"], 2)
                e.tensor_scalar(y[:, :, :], x[:, :, :], -1.0, None, ALU.mult).then_inc(s["nx"], 1)
                e.wait_ge(s["nx"], 1)
                e.tensor_tensor(y[:, :, :], y[:, :, :], x[:, :, :], ALU.min).then_inc(s["m"], 1)
                e.wait_ge(s["ln"], 1)
                e.scalar_tensor_tensor(out=x[:, :, :], in0=x[:, :, :], scalar=0.0, in1=y[:, :, :], op0=ALU.min, op1=ALU.subtract).then_inc(s["ls"], 1)
                e.wait_ge(s["ls"], 1)
                e.tensor_scalar(x[:, :, :], x[:, :, :], 1.0 / GLA_TAU, None, ALU.mult).then_inc(s["cs"], 1)
                a, b, n = x, y, 1
                for sh in (1, 2, 4, 8):
                    e.wait_ge(s["cs"], n)
                    e.tensor_tensor(V(b[:, :, :])[:, :, sh:], V(a[:, :, :])[:, :, sh:], V(a[:, :, :])[:, :, :GLA_C - sh], ALU.add).then_inc(s["cs"], 1)
                    e.tensor_copy(V(b[:, :, :])[:, :, :sh], V(a[:, :, :])[:, :, :sh]).then_inc(s["cs"], 1)
                    a, b, n = b, a, n + 2
                e.wait_ge(s["cs"], n)
                bc = x
                e.tensor_tensor(V(q1[:, :, :]), V(bc[:, :, :]), at(bc[:, :, :], 7), ALU.subtract).then_inc(s["d"], 1)
                e.tensor_tensor(V(k1[:, :, :]), at(bc[:, :, :], 7), V(bc[:, :, :]), ALU.subtract).then_inc(s["d"], 1)
                e.tensor_tensor(V(kd[:, :, :]), at(bc[:, :, :], 15), V(bc[:, :, :]), ALU.subtract).then_inc(s["d"], 1)
                e.wait_ge(s["d"], 2)
                e.tensor_scalar(q1[:, :, :], q1[:, :, :], GLA_GUARD, None, ALU.min).then_inc(s["d"], 1)
                e.tensor_scalar(k1[:, :, :], k1[:, :, :], GLA_GUARD, None, ALU.min).then_inc(s["d"], 1)
                sc = (P // 2) ** -0.5
                e.wait_ge(s["pT"], 16)
                e.wait_ge(s["e"], 4)
                e.scalar_tensor_tensor(out=q1[:, :, :], in0=pT[:, 0:2, :], scalar=sc, in1=q1[:, :, :], op0=ALU.mult, op1=ALU.mult)
                e.tensor_tensor(k1[:, :, :], pT[:, 2:4, :], k1[:, :, :], ALU.mult)
                e.tensor_tensor(kd[:, :, :], pT[:, 2:4, :], kd[:, :, :], ALU.mult)
                e.scalar_tensor_tensor(out=qd[:, :, :], in0=pT[:, 0:2, :], scalar=sc, in1=ebc[:, :, :], op0=ALU.mult, op1=ALU.mult)

            @block.scalar
            def _(e):
                bg.hi(e, 1)
                bg.hi(e, 2)
                e.wait_ge(s["m"], 1)
                e.activation(y[:, :, :], y[:, :, :], ACT.Exp).then_inc(s["ex"], 1)
                e.wait_ge(s["ex"], 1)
                e.activation(y[:, :, :], y[:, :, :], ACT.Ln, bias=C["one"]).then_inc(s["ln"], 1)
                bg.hi(e, 3)
                bg.hi(e, 4)
                bg.out(e, 0)
                bg.hi(e, 5)
                e.wait_ge(s["cs"], 9)
                e.activation(ebc[:, :, :], x[:, :, :], ACT.Exp).then_inc(s["e"], 1)
                bg.hi(e, 6)
                bg.out(e, 1)
                bg.hi(e, 7)
                e.wait_ge(s["d"], 5)
                e.activation(kd[:, :, :], kd[:, :, :], ACT.Exp).then_inc(s["e"], 1)
                e.activation(q1[:, :, :], q1[:, :, :], ACT.Exp).then_inc(s["e"], 1)
                e.activation(k1[:, :, :], k1[:, :, :], ACT.Exp).then_inc(s["e"], 1)
                bg.hi(e, 8)
                bg.out(e, 2)
                bg.out(e, 3)
                bg.stored(e)
    retire(nc, s)


def gla_tile(nc, C, W, t, stream, jobs, sums):
    s = phase(nc, Background.SEMS + ["k1", "kd", "vt", "qd", "eb", "trk", "trv", "kn", "vn", "at", "ats", "kv", "S", "o", "carry", "os", "q1"])
    ps = C["ps"]
    H = GLA_H
    cols = bass.ts(t, P)
    HB = lambda ap: ap.rearrange("p (h c) -> p h c", c=P)
    k1t, q1t, kdt, qdt, vt, ebt, kn, vn, at, SS = (W[n] for n in ("k1t", "q1t", "kdt", "qdt", "vt", "ebt", "kn", "vn", "at", "SS"))
    bg = Background(C, s, *stream, jobs, sums, [ps[7], ps[1]])
    kv_bank = [ps[4], ps[5], ps[6], ps[0]]
    NCH = P // GLA_C
    half = lambda h: slice((h % 2) * 64, (h % 2) * 64 + 64)
    with nc.Block() as block:
        @block.sync
        def _(e):
            bg.loads(e)

        @block.gpsimd
        def _(e):
            for j in range(1, 6):
                bg.lo(e, j)
            bg.add(e, bg.branches[0])
            bg.lo(e, 6)
            bg.add(e, bg.branches[1])

        @block.vector
        def _(e):
            e.tensor_copy(q1t[:, :, :], W["q1"][:, :, cols]).then_inc(s["q1"], 1)
            e.tensor_copy(qdt[:, :, :], W["qd"][:, :, cols]).then_inc(s["qd"], 1)
            e.tensor_copy(ebt[:, :, :], W["ebc"][:, :, cols]).then_inc(s["eb"], 1)
            e.wait_ge(s["trk"], 1)
            for par in range(2):
                e.tensor_scalar(kn[:, par, :], ps[0][:, 0:2 * P], C["parity"][:, par:par + 1], None, ALU.mult).then_inc(s["kn"], 1)
            e.wait_ge(s["at"], 1)
            for par in range(2):
                e.tensor_tensor(at[:, par, :, :], HB(ps[2 + par][:, 0:2 * P]), C["tri16"].unsqueeze(1).to_broadcast([P, 2, P]),
                                ALU.mult).then_inc(s["ats"], 1)
            e.wait_ge(s["eb"], 1)
            for c in range(NCH):
                e.wait_ge(s["kv"], 2 * (c // 2) + 2)
                if c:
                    e.wait_ge(s["S"], 2 * c)
                for p in range(2):
                    last = (c + 1) * GLA_C - 1
                    e.scalar_tensor_tensor(out=SS[:, c + 1, p, :], in0=SS[:, c, p, :], scalar=ebt[:, p, last:last + 1],
                                           in1=kv_bank[c // 2][:, (2 * (c % 2) + p) * P:(2 * (c % 2) + p + 1) * P],
                                           op0=ALU.mult, op1=ALU.add).then_inc(s["S"], 1)
            for n in bg.branches:
                bg.product(e, n)
            e.wait_ge(s["S"], 2 * NCH)
            e.wait_ge(s["o"], 1)
            e.tensor_copy(SS[:, 0, :, :], SS[:, NCH, :, :]).then_inc(s["carry"], 1)

        @block.scalar
        def _(e):
            e.copy(kdt[:, :, :], W["kd"][:, :, cols]).then_inc(s["kd"], 1)
            e.copy(vt[:, :, :], W["pT"][:, 4:8, cols]).then_inc(s["vt"], 1)
            e.copy(k1t[:, :, :], W["k1"][:, :, cols]).then_inc(s["k1"], 1)
            bg.hi(e, 1)
            e.wait_ge(s["trv"], 1)
            e.copy(vn[:, :, :], HB(ps[1][:, :])).then_inc(s["vn"], 1)
            bg.hi(e, 2)
            bg.hi(e, 3)
            bg.out(e, 0)
            for j in range(4, 7):
                bg.hi(e, j)
            bg.out(e, 2)
            e.wait_ge(s["o"], 1)
            for par in range(2):
                e.copy(W["o_raw"][:, :, cols].rearrange("p (a b) n -> p b a n", b=2)[:, par, :, :], HB(ps[2 + par][:, 0:2 * P])).then_inc(s["os"], 1)

        @block.tensor
        def _(e):
            bg.mm(e, 0)
            e.wait_ge(s["kd"], 1)
            for p in range(2):
                ins = e.transpose(ps[0][:, p * P:(p + 1) * P], kdt[:, p, :], C["ident"])
            ins.then_inc(s["trk"], 1)
            e.wait_ge(s["vt"], 1)
            for h in range(H):
                ins = e.transpose(HB(ps[1][:, :])[:, h, :], vt[:, h, :], C["ident"])
            ins.then_inc(s["trv"], 1)
            e.wait_ge(s["k1"], 1)
            e.wait_ge(s["q1"], 1)
            for h in range(H):
                ins = e.matmul(HB(ps[2 + h % 2][:, :])[:, h // 2, :], k1t[half(h), h // 2, :], q1t[half(h), h // 2, :], start=True, stop=True)
            ins.then_inc(s["at"], 1)
            bg.mm(e, 1)
            e.wait_ge(s["kn"], 2)
            e.wait_ge(s["vn"], 1)
            for c in range(NCH):
                rows = slice(32 * (c // 2), 32 * (c // 2) + 32)
                for h in range(H):
                    col = (2 * (c % 2) + h // 2) * P
                    ins = e.matmul(kv_bank[c // 2][half(h), col:col + P], kn[rows, c % 2, h * 64:(h + 1) * 64], vn[rows, h, :],
                                   start=True, stop=True)
                ins.then_inc(s["kv"], 1)
            for j in range(2, 5):
                bg.mm(e, j)
            e.wait_ge(s["ats"], 2)
            e.wait_ge(s["qd"], 1)
            e.wait_ge(s["S"], 2 * NCH - 2)
            for h in range(H):
                out = HB(ps[2 + h % 2][:, :])[:, h // 2, :]
                for c in range(NCH):
                    cc = slice(c * GLA_C, (c + 1) * GLA_C)
                    e.matmul(out[:, cc], SS[half(h), c, h // 2, :], qdt[half(h), h // 2, cc], start=(c == 0), stop=False,
                             skip_group_check=True)
                ins = e.matmul(out, vn[:, h, :], at[:, h % 2, h // 2, :], start=False, stop=True, skip_group_check=True)
                if h == 1:
                    bg.mm(e, 5)
            ins.then_inc(s["o"], 1)
    retire(nc, s)


def gla(nc, C, prm, l, wd, h_hi, h_lo, miscT, gla_rows, gla_gates, n_hi, n_lo, o_hi, o_lo):
    with ExitStack() as ctx:
        sb = lambda n, shape: ctx.enter_context(sbuf(nc, n, shape, F32))
        W = {}
        pT = W["pT"] = sb("gla_pT", [P, 12, S])
        o_raw = W["o_raw"] = sb("gla_o", [P, GLA_H, S])
        with ExitStack() as c2:
            for n, shape in (("q1", [P, 2, S]), ("k1", [P, 2, S]), ("qd", [P, 2, S]), ("kd", [P, 2, S]), ("ebc", [P, 2, S])):
                W[n] = c2.enter_context(sbuf(nc, "gla_" + n, shape, F32))
            jobs, sums = [], []
            for c in range(4, KD):
                jobs += column_jobs(P, h_hi, h_lo)
                sums.append(("tanh", gla_gates[c]))
            gla_prepare(nc, C, prm, miscT, pT, W["q1"], W["k1"], W["qd"], W["kd"], W["ebc"], gla_rows,
                        (wd["w_stream"], l, FIRST_JOB["gla_prepare"]), jobs, sums)
            for n, shape in (("k1t", [P, 2, P]), ("q1t", [P, 2, P]), ("kdt", [P, 2, P]), ("qdt", [P, 2, P]), ("vt", [P, 4, P]),
                             ("ebt", [P, 2, P]), ("kn", [P, 2, 2 * P]), ("vn", [P, 4, P]), ("at", [P, 2, 2, P]), ("SS", [P, 9, 2, P])):
                W[n] = c2.enter_context(sbuf(nc, "gla_" + n, shape, F32))
            zero(nc, W["SS"][:, 0, :, :])
            with nc.Fori(0, NT) as t:
                jobs, sums = [], []
                for c in range(2):
                    chunk = 2 * t + c
                    j, m = merge_jobs(h_hi, h_lo, n_hi, n_lo, chunk, False)
                    jobs, sums = jobs + j, sums + m
                gla_tile(nc, C, W, t, (wd["w_stream"], l, len(jobs) * t + FIRST_JOB["gla"]), jobs, sums)
        gated_output(nc, C, o_raw, pT[:, 8:12, :], prm["gla_norm"], o_hi, o_lo, (wd["w_stream"], l, FIRST_JOB["last"]), [], [])


def start(nc, C, cst, consts, x_in, rel_bias, one_hot, scratch, bias_dram, biasc_dram):
    s = phase(nc, ["tb", "mask", "oh", "row", "rows", "st", "ld", "flip", "out", "x", "c", "ssq", "sqrt", "st_bias", "st_biasc"])
    ps, x, rstd = C["ps"], C["x"], C["rstd"]
    with ExitStack() as ctx:
        sb = lambda n, shape: ctx.enter_context(sbuf(nc, n, shape, F32))
        tbl = sb("pb_tbl", [BUCKETS + 1, NSA_H])
        oh = sb("pb_oh", [BUCKETS + 1, RLEN])
        row = sb("pb_row", [NSA_H, RLEN])
        wt = sb("pb_wt", [P, NSA_H, WLEN])
        bias = sb("pb_bias", [P, NSA_H, S])
        biasc = sb("pb_biasc", [P, NSA_H, NT * NCMP])
        junk = sb("fr_junk", [P, NT, D])
        ssq = sb("fr_ssq", [P, NT])
        with nc.Block() as block:
            @block.sync
            def _(e):
                e.dma_start(tbl[0:BUCKETS, :], rel_bias).then_inc(s["tb"], 16)
                e.dma_start(oh[:, :], one_hot).then_inc(s["oh"], 16)
                e.dma_start(cst[:, :], consts).then_inc(s["c"], 16)
                e.wait_ge(s["rows"], 2)
                e.dma_start(scratch, row[:, :]).then_inc(s["st"], 16)
                e.wait_ge(s["st"], 16)
                src = bass.AP(scratch.tensor, 0, [[1, P], [RLEN, NSA_H], [1, WLEN]])
                e.dma_start(wt[:, :, :], src).then_inc(s["ld"], 16)
                e.wait_ge(s["out"], 2 * NSA_H)
                e.dma_start(bias_dram.rearrange("c p h n -> p c h n"), bias[:, :, :].rearrange("p (c h) n -> p c h n", h=HPG)
                            ).then_inc(s["st_bias"], 16)
                e.dma_start(biasc_dram.rearrange("c p h n -> p c h n"), biasc[:, :, :].rearrange("p (c h) n -> p c h n", h=HPG)
                            ).then_inc(s["st_biasc"], 16)
                e.wait_ge(s["st_bias"], 16)
                e.wait_ge(s["st_biasc"], 16)

            @block.scalar
            def _(e):
                e.wait_ge(s["row"], 2)
                e.dma_start(x[:, :, :], x_in.rearrange("b (t p) d -> p (b t) d", p=P)).then_inc(s["x"], 16)
                e.wait_ge(s["x"], 16)
                for t in range(NT):
                    e.activation(junk[:, t, :], x[:, t, :], ACT.Square, accum_out=ssq[:, t:t + 1]).then_inc(s["ssq"], 1)
                e.wait_ge(s["ssq"], NT)
                e.wait_ge(s["c"], 16)
                e.activation(ssq[:, :], ssq[:, :], ACT.Sqrt, bias=C["eps"], scale=1.0 / D).then_inc(s["sqrt"], 1)

            @block.vector
            def _(e):
                e.memset(tbl[BUCKETS:BUCKETS + 1, :], MASKED).then_inc(s["mask"], 1)
                e.wait_ge(s["row"], 2)
                for c in range(2):
                    e.tensor_copy(row[:, c * S:(c + 1) * S], ps[c][0:NSA_H, :]).then_inc(s["rows"], 1)
                for h in range(NSA_H):
                    e.wait_ge(s["flip"], h + 1)
                    e.tensor_copy(bias[:, h, :], ps[2 + 2 * (h % 2)][:, :]).then_inc(s["out"], 1)
                    e.tensor_copy(biasc[:, h, :], ps[3 + 2 * (h % 2)][:, 0:NT * NCMP]).then_inc(s["out"], 1)
                e.wait_ge(s["sqrt"], 1)
                e.reciprocal(rstd[:, :], ssq[:, :])

            @block.tensor
            def _(e):
                e.wait_ge(s["tb"], 16)
                e.wait_ge(s["mask"], 1)
                e.wait_ge(s["oh"], 16)
                for c in range(2):
                    e.matmul(ps[c][0:NSA_H, :], tbl[:, :], oh[:, c * S:(c + 1) * S], start=True, stop=True).then_inc(s["row"], 1)
                e.wait_ge(s["c"], 16)
                e.wait_ge(s["ld"], 16)
                for h in range(NSA_H):
                    if h >= 2:
                        e.wait_ge(s["out"], 2 * (h - 1))
                    e.matmul(ps[2 + 2 * (h % 2)][:, :], C["anti"], wt[:, h, 0:S], start=True, stop=True)
                    src = wt[:, h, CMP_LEN - 1:CMP_LEN - 1 + NT * P]
                    for q in range(NT):
                        a = CMP_LEN - 1 + q * P
                        ins = e.matmul(ps[3 + 2 * (h % 2)][:, q * NCMP:(q + 1) * NCMP], C["anti"],
                                       wt[:, h, a:a + (NCMP - 1) * CMP_STRIDE + 1:CMP_STRIDE], start=True, stop=True)
                    ins.then_inc(s["flip"], 1)
    retire(nc, s)


def trunk(nc, x_in, rel_bias, consts, one_hot, params, wd, out, scratch):
    with ExitStack() as ctx:
        sb = lambda n, shape: ctx.enter_context(sbuf(nc, n, shape, F32))
        x = sb("x", [P, NT, D])
        cst = sb("consts", [P, CONST_N])
        prm_t = sb("params", [P, PARAM_N])
        rstd_x = sb("rstd_x", [P, NT])
        bias = nc.dram_tensor("bias", (NSA_G, P, HPG, S), F32, kind="Internal").ap()
        biasc = nc.dram_tensor("biasc", (NSA_G, P, HPG, NT * NCMP), F32, kind="Internal").ap()
        nsa_rows = nc.dram_tensor("nsa_rows", (NSA_CHUNKS, NDK, S), F32, kind="Internal").ap()
        gla_rows = nc.dram_tensor("gla_rows", (GLA_CHUNKS, P, S), F32, kind="Internal").ap()
        gla_gates = nc.dram_tensor("gla_gates", (KD, P, S), F32, kind="Internal").ap()
        ps = [ctx.enter_context(nc.psum_tensor(f"ps{i}", [P, S], F32)) for i in range(8)]
        C = {n: cst[:, a:b] for n, (a, b) in CONST_COLS.items()}
        C["x"], C["ps"], C["rstd"] = x, ps, rstd_x
        start(nc, C, cst, consts, x_in, rel_bias, one_hot, scratch, bias, biasc)

        with nc.Fori(0, DEPTH) as l:
            s = phase(nc, ["p"])
            with nc.Block() as block:
                @block.sync
                def _(e):
                    e.dma_start(prm_t[:, :], params[l]).then_inc(s["p"], 16)
                    e.wait_ge(s["p"], 16)
            retire(nc, s)
            prm = {n: prm_t[:, a:b] for n, (a, b) in PARAM_COLS.items()}
            ffn(nc, C, l, prm["ffn1_pre"], wd["w_gu1"], wd["w_down1"], wd["post1"])
            with ExitStack() as cm:
                merged = cm.enter_context(sbuf(nc, "merged", [P, KD, S], F32))
                with ExitStack() as ch:
                    h_hi = ch.enter_context(sbuf(nc, "m_h_hi", [P, KD, S], F32R))
                    h_lo = ch.enter_context(sbuf(nc, "m_h_lo", [P, KD, S], F32R))
                    miscT = ch.enter_context(sbuf(nc, "miscT", [80, S], F32))
                    ba = ch.enter_context(sbuf(nc, "misc", [P, NT, 80], F32))
                    o_hi = ch.enter_context(sbuf(nc, "o_hi", [P, 4, S], F32R))
                    o_lo = ch.enter_context(sbuf(nc, "o_lo", [P, 4, S], F32R))
                    C["merged"] = merged
                    C["bg"] = tuple(ch.enter_context(sbuf(nc, n, [P, 2, S], dt)) for n, dt in
                                    (("bg_raw", F32), ("bg_hi", F32R), ("bg_lo", F32R), ("bg_stage", F32))) + tuple(
                        ch.enter_context(sbuf(nc, n, [P, S], F32)) for n in ("bg_sg", "bg_pr"))
                    gdn(nc, C, prm, l, wd, h_hi, h_lo, miscT, ba, o_hi, o_lo, nsa_rows, gla_gates)
                    with ExitStack() as cb:
                        n_hi = cb.enter_context(sbuf(nc, "n_hi", [P, 4, S], F32R))
                        n_lo = cb.enter_context(sbuf(nc, "n_lo", [P, 4, S], F32R))
                        nsa(nc, C, prm, l, wd, h_hi, h_lo, miscT, nsa_rows, gla_rows, bias, biasc, o_hi, o_lo, n_hi, n_lo)
                        gla(nc, C, prm, l, wd, h_hi, h_lo, miscT, gla_rows, gla_gates, n_hi, n_lo, o_hi, o_lo)
                    raw = raw_buffer(nc, ch)
                    merge_last(nc, C, l, wd["w_stream"], gla_gates, o_hi, o_lo, h_hi, h_lo, raw, [wd["w_out"][l, 0, u] for u in range(2)])
                    contract(nc, C, l, raw, wd["w_out"], KD, h_hi, h_lo, wd["mix_post"], 1.0)
            ffn(nc, C, l, prm["ffn2_pre"], wd["w_gu2"], wd["w_down2"], wd["post2"])

        s = phase(nc, ["out"])
        with nc.Block() as block:
            @block.sync
            def _(e):
                e.dma_start(out.rearrange("b (t p) d -> p (b t) d", p=P), x[:, :, :]).then_inc(s["out"], 16)
                e.wait_ge(s["out"], 16)


def constants():
    import numpy as np
    c = np.zeros((P, CONST_N), np.float32)
    i, j = np.arange(P)[:, None], np.arange(P)[None, :]

    def put(name, v):
        a, b = CONST_COLS[name]
        c[:, a:b] = v

    put("ident", i == j)
    put("ones", 1.0)
    put("anti", i + j == P - 1)
    same64 = i // GDN_C == j // GDN_C
    put("tri64", (i <= j) & same64)
    put("blk64", same64)
    lv = [((i // (2 * b) == j // (2 * b)) & (i % (2 * b) >= b) & (j % (2 * b) < b)) for b in (1, 2, 4, 8, 16, 32)]
    put("lvl", np.concatenate(lv, 1))
    put("tri16", (i <= j) & (i // GLA_C == j // GLA_C))
    put("parity", np.concatenate([(i // GLA_C) % 2 == 0, (i // GLA_C) % 2 == 1], 1))
    put("cmp_valid", i >= CMP_LEN - 1)
    put("eps", EPS)
    put("one", 1.0)
    dist = S - 1 - np.arange(RLEN)
    n = np.maximum(dist, 0)
    exact = BUCKETS // 2
    large = exact + (np.log(np.maximum(n, 1).astype(np.float64) / exact) / np.log(128 / exact) * (BUCKETS - exact) + 1e-9).astype(np.int64)
    bucket = np.where(n < exact, n, np.minimum(large, BUCKETS - 1))
    oh = np.zeros((BUCKETS + 1, RLEN), np.float32)
    oh[bucket, np.arange(RLEN)] = dist >= 0
    oh[BUCKETS] = dist < 0
    return c, oh


def kernel(**inputs):
    import numpy as np
    import concourse.bacc as bacc
    from concourse import mybir as mb
    from concourse.bass_utils import run_bass_kernel_spmd as run

    a = {k: np.asarray(v) for k, v in inputs.items()}
    L = DEPTH
    c, oh = constants()

    def tiles(w, width):
        k, n = w.shape[1] // P, w.shape[2] // width
        return w.reshape(L, k, P, n, width).transpose(0, 3, 2, 1, 4).reshape(L, n, P, k * width)

    arrays = {"x": a["x"], "rel_bias": a["rel_bias"], "consts": c, "one_hot": oh}
    for f in ("1", "2"):
        gu = a[f"ffn{f}_w_gate_up"]
        g, u = tiles(gu[:, :, :FF], P), tiles(gu[:, :, FF:], P)
        arrays["w_gu" + f] = np.stack([g, u], 2)
        arrays["w_down" + f] = a[f"ffn{f}_w_down"].reshape(L, KF // 2, 2, P, D)
        arrays["post" + f] = a[f"ffn{f}_norm_post"].reshape(L, 1, D)
    arrays["mix_post"] = a["mix_norm_post"].reshape(L, 1, D)
    arrays["w_out"] = a["w_out"].reshape(L, KD // 2, 2, P, D)
    wi = a["w_in"]
    at = 0

    def take(n):
        nonlocal at
        at += n
        return wi[:, :, at - n:at]

    arrays["w_gdn"] = tiles(take(2048), P)
    w_ba = take(8)
    nq = take(NSA_H * NDK).reshape(L, D, NSA_H, NDK)
    kv = take(3 * NSA_G * (NDK + NDV)).reshape(L, D, 3 * NSA_G, NDK + NDV)
    nk, nv = kv[..., :NDK], np.zeros((L, D, 3 * NSA_G, NDK), np.float32)
    nv[..., :NDV] = kv[..., NDK:]
    streamed = {}
    streamed["nsa"] = tiles(np.concatenate([nq, nk[:, :, NSA_G:], nk[:, :, :NSA_G], nv], 2).reshape(L, D, -1), NDK)
    w_ng = take(3 * NSA_H)
    streamed["gla"] = tiles(take(1536), P)
    w_ga = take(16)
    misc = np.zeros((L, D, 80), np.float32)
    misc[:, :, 0:8], misc[:, :, 32:56], misc[:, :, 64:80] = w_ba, w_ng, w_ga
    arrays["w_misc"] = tiles(misc, 80)[:, 0]
    for b, name in enumerate(("gdn", "nsa", "gla")):
        streamed["gate", b] = tiles(take(D), P)
        streamed["branch", b] = tiles(a[f"w_branch_{name}"], P)
    arrays["w_stream"] = np.zeros((L, STREAM_N, P, HALF * P), np.float32)
    for j, (kind, n, part) in enumerate(STREAM):
        w = streamed[kind][:, n] if kind in ("nsa", "gla") else streamed[kind, n[0]][:, n[1]]
        cols = HALF * (NDK if kind == "nsa" else P)
        arrays["w_stream"][:, j, :, 0:cols] = w[:, :, part * cols:(part + 1) * cols]
    arrays["w_ck"] = a["nsa_cmp_k_w1"].reshape(L, CMP_LEN, NDK, CMP_HID).transpose(0, 2, 1, 3)
    arrays["w_cv"] = a["nsa_cmp_v_w1"].reshape(L, CMP_LEN, NDV, CMP_HID).transpose(0, 2, 1, 3)

    prm = np.zeros((L, P, PARAM_N), np.float32)

    def put(name, v, rows=slice(0, P)):
        lo, hi = PARAM_COLS[name]
        prm[:, rows, lo:hi] = v

    for name, key in (("ffn1_pre", "ffn1_norm_pre"), ("mix_pre", "mix_norm_pre"), ("ffn2_pre", "ffn2_norm_pre")):
        put(name, a[key].reshape(L, KD, P).transpose(0, 2, 1))
    put("conv", a["gdn_conv_w"].reshape(L, 4, 12, P).transpose(0, 3, 1, 2).reshape(L, P, 48))
    put("gdn_norm", a["gdn_norm_w"].reshape(L, P, 1))
    put("gla_norm", a["gla_norm_w"].reshape(L, P, 1))
    put("gla_b", a["gla_gate_b"].reshape(L, 2, P).transpose(0, 2, 1))
    put("pe_k", a["nsa_pe_k"].transpose(0, 2, 1), slice(0, NDK))
    put("pe_v", a["nsa_pe_v"].transpose(0, 2, 1), slice(0, NDV))
    put("gla_w", a["gla_gate_w"], slice(64, 80))
    put("a_log", a["gdn_a_log"].reshape(L, 1, 4))
    put("dt_bias", a["gdn_dt_bias"].reshape(L, 1, 4))
    put("w2k", a["nsa_cmp_k_w2"].reshape(L, 2, P, NDK).transpose(0, 2, 1, 3).reshape(L, P, -1))
    put("w2v", a["nsa_cmp_v_w2"].reshape(L, 2, P, NDV).transpose(0, 2, 1, 3).reshape(L, P, -1))
    arrays["params"] = prm

    nc = bacc.Bacc("TRN2", target_bir_lowering=False, num_devices=1)
    arrays = {"in_" + k: np.ascontiguousarray(v) for k, v in arrays.items()}
    t = {k[3:]: nc.dram_tensor(k, v.shape, mb.dt.from_np(v.dtype), kind="ExternalInput").ap() for k, v in arrays.items()}
    out = nc.dram_tensor("out", (1, S, D), F32, kind="ExternalOutput").ap()
    scratch = nc.dram_tensor("bias_rows", (NSA_H, RLEN), F32, kind="Internal").ap()
    trunk(nc, t["x"], t["rel_bias"], t["consts"], t["one_hot"], t["params"], t, out, scratch)
    return run(nc, [arrays], core_ids=[0]).results[0]["out"]
```
